# Optimizing a Trainium2 kernel written in Bass

```python
import math
import jax, jax.numpy as jnp
from jax import lax
import numpy as np

D_MODEL = 1024
BATCH = 1
SEQ = 128
DEPTH = 2
DEC_BATCH = 1
DEC_SEQ = 512
PAST_LEN = 128

GRID_W = 64
BLOCK = 128
A_HEADS = 8
A_KV_HEADS = 2
A_HEAD_DIM = 64
WINDOW = 128
B_HEADS = 4
B_DK = 128
B_DV = 128
CHUNK = 64
SHORT_CONV = 3
C_HEADS = 8
C_Q_LORA = 384
C_KV_LORA = 256
C_NOPE = 128
C_ROPE = 64
C_V = 128
D_FF = 2816
FFN_CONV = 3
ROPE_BASE = 10000.0
EPS = 1e-6
N_MOD = 6

A_Q = A_HEADS * A_HEAD_DIM
A_KV = A_KV_HEADS * A_HEAD_DIM
B_QK = B_HEADS * B_DK
B_VW = B_HEADS * B_DV
B_CONV_CH = 2 * B_QK + B_VW
EVEN_IN = A_Q + 2 * A_KV + B_CONV_CH + B_VW + 4 * B_HEADS
EVEN_OUT = A_Q + B_VW
ODD_IN = C_Q_LORA + C_KV_LORA + C_ROPE

kernel_name = "hybrid_diffusion_prefix_trunk_step"

def rmsnorm(x, g):
    xf = x.astype(jnp.float32)
    y = xf * lax.rsqrt(jnp.mean(xf * xf, axis=-1, keepdims=True) + EPS)
    return (y * g.astype(jnp.float32)).astype(x.dtype)

def l2norm(x):
    xf = x.astype(jnp.float32)
    return (xf * lax.rsqrt(jnp.sum(xf * xf, axis=-1, keepdims=True) + EPS)).astype(x.dtype)

def dwconv_centred(x, w):
    k = w.shape[0]
    return lax.conv_general_dilated(
        x, w[:, None, :].astype(x.dtype), window_strides=(1,), padding=[(k // 2, k // 2)],
        dimension_numbers=("NWC", "WIO", "NWC"), feature_group_count=x.shape[-1])

def axial_rope_tables(seq_len, rot_dim):
    rows = seq_len // GRID_W
    t = jnp.arange(rows * GRID_W)
    row = (t // GRID_W).astype(jnp.float32)
    col = (t % GRID_W).astype(jnp.float32)
    n_freq = rot_dim // 4
    inv_freq = ROPE_BASE ** (-jnp.arange(n_freq, dtype=jnp.float32) / n_freq)
    ang = jnp.concatenate([row[:, None] * inv_freq, col[:, None] * inv_freq], axis=-1)
    return jnp.cos(ang), jnp.sin(ang)

def apply_rope(x, cos, sin):
    half = x.shape[-1] // 2
    shape = (1, x.shape[1]) + (1,) * (x.ndim - 3) + (half,)
    c = cos.reshape(shape).astype(x.dtype)
    s = sin.reshape(shape).astype(x.dtype)
    x1, x2 = x[..., :half], x[..., half:]
    return jnp.concatenate([x1 * c - x2 * s, x2 * c + x1 * s], axis=-1)

def softmax_sink(s, sink, groups, rep):
    if sink is None:
        return jax.nn.softmax(s, axis=-1)
    sk = sink.astype(jnp.float32).reshape(groups, rep, 1, 1)
    m = jnp.maximum(jnp.max(s, axis=-1, keepdims=True), sk)
    e = jnp.exp(s - m)
    return e / (jnp.sum(e, axis=-1, keepdims=True) + jnp.exp(sk - m))

def dense_attention(q, k, v, sink, scale):
    bsz, lq, n_heads, hd = q.shape
    groups = k.shape[2]
    rep = n_heads // groups
    n_blk = lq // BLOCK
    qb = jnp.moveaxis(q.reshape(bsz, n_blk, BLOCK, groups, rep, hd), 1, 0)

    def block(q_i):
        s = jnp.einsum("bqgrd,bkgd->bgrqk", q_i, k, preferred_element_type=jnp.float32) * scale
        p = softmax_sink(s, sink, groups, rep).astype(v.dtype)
        return jnp.einsum("bgrqk,bkgv->bqgrv", p, v)

    o = lax.map(block, qb)
    return jnp.moveaxis(o, 0, 1).reshape(bsz, lq, n_heads, v.shape[-1])

def window_ctx_attention(q, k, v, k_ctx, v_ctx, sink, scale):
    bsz, seq, n_heads, hd = q.shape
    groups = k.shape[2]
    rep = n_heads // groups
    n_blk = seq // BLOCK
    band = BLOCK + 2 * WINDOW
    n_ctx = k_ctx.shape[1]
    pad = ((0, 0), (WINDOW, WINDOW), (0, 0), (0, 0))
    kp, vp = jnp.pad(k, pad), jnp.pad(v, pad)
    qb = jnp.moveaxis(q.reshape(bsz, n_blk, BLOCK, groups, rep, hd), 1, 0)
    offs_q = jnp.arange(BLOCK)
    offs_k = jnp.arange(band)

    def block(args):
        i, q_i = args
        start = i * BLOCK
        k_i = lax.dynamic_slice_in_dim(kp, start, band, axis=1)
        v_i = lax.dynamic_slice_in_dim(vp, start, band, axis=1)
        qpos = start + offs_q
        kpos = start - WINDOW + offs_k
        valid = ((jnp.abs(qpos[:, None] - kpos[None, :]) <= WINDOW)
                 & (kpos >= 0)[None, :] & (kpos < seq)[None, :])
        s_ctx = jnp.einsum("bqgrd,bkgd->bgrqk", q_i, k_ctx, preferred_element_type=jnp.float32) * scale
        s_loc = jnp.einsum("bqgrd,bkgd->bgrqk", q_i, k_i, preferred_element_type=jnp.float32) * scale
        s_loc = jnp.where(valid, s_loc, -jnp.inf)
        p = softmax_sink(jnp.concatenate([s_ctx, s_loc], axis=-1), sink, groups, rep).astype(v.dtype)
        return (jnp.einsum("bgrqk,bkgv->bqgrv", p[..., :n_ctx], v_ctx)
                + jnp.einsum("bgrqk,bkgv->bqgrv", p[..., n_ctx:], v_i))

    o = lax.map(block, (jnp.arange(n_blk), qb))
    return jnp.moveaxis(o, 0, 1).reshape(bsz, seq, n_heads, v.shape[-1])

def gated_delta_chunked(q, k, v, g, beta, s0):
    bsz, seq, n_heads, dk = q.shape
    dv = v.shape[-1]
    n = seq // CHUNK
    f32 = jnp.float32

    def ch4(t):
        return t.astype(f32).reshape(bsz, n, CHUNK, n_heads, t.shape[-1]).transpose(1, 0, 3, 2, 4)

    def ch3(t):
        return t.astype(f32).reshape(bsz, n, CHUNK, n_heads).transpose(1, 0, 3, 2)

    qc = ch4(q) * (dk ** -0.5)
    kc, vc = ch4(k), ch4(v)
    gc = jnp.cumsum(ch3(g), axis=-1)
    bc = ch3(beta)
    idx = jnp.arange(CHUNK)
    causal = idx[:, None] >= idx[None, :]
    strict = idx[:, None] > idx[None, :]
    diff = gc[..., :, None] - gc[..., None, :]
    decay = jnp.where(causal, jnp.exp(jnp.where(causal, diff, 0.0)), 0.0)
    kb = kc * bc[..., None]
    a = jnp.where(strict, jnp.einsum("nbhid,nbhjd->nbhij", kb, kc) * decay, 0.0)
    eye = jnp.eye(CHUNK, dtype=f32)
    t_inv = lax.linalg.triangular_solve(a + eye, jnp.broadcast_to(eye, a.shape), left_side=True,
                                        lower=True, unit_diagonal=True)
    u = t_inv @ (vc * bc[..., None])
    w = t_inv @ (kb * jnp.exp(gc)[..., None])
    qk = jnp.where(causal, jnp.einsum("nbhid,nbhjd->nbhij", qc, kc) * decay, 0.0)

    def step(s, xs):
        q_i, k_i, u_i, w_i, qk_i, g_i = xs
        v_new = u_i - w_i @ s
        o_i = (q_i * jnp.exp(g_i)[..., None]) @ s + qk_i @ v_new
        g_last = g_i[..., -1:]
        s = (s * jnp.exp(g_last)[..., None]
             + jnp.einsum("bhcd,bhce->bhde", k_i * jnp.exp(g_last - g_i)[..., None], v_new))
        return s, o_i

    s, o = lax.scan(step, s0.astype(f32), (qc, kc, u, w, qk, gc))
    o = o.transpose(1, 0, 3, 2, 4).reshape(bsz, seq, n_heads, dv)
    return o.astype(v.dtype), s

def delta_bidir(q, k, v, g, beta, s0_f, s0_b):
    o_f, s_f = gated_delta_chunked(q, k, v, g[:, :, 0], beta[:, :, 0], s0_f)
    rev = lambda t: jnp.flip(t, axis=1)
    o_b, s_b = gated_delta_chunked(rev(q), rev(k), rev(v), rev(g[:, :, 1]), rev(beta[:, :, 1]), s0_b)
    return o_f + rev(o_b), s_f, s_b

def even_mixer(h, w_in, conv_w, a_log, dt_bias, sink, out_norm, w_out, ctx):
    bsz, seq, _ = h.shape
    cuts = np.cumsum([A_Q, A_KV, A_KV, B_CONV_CH, B_VW]).tolist()
    qa, ka, va, qkv_b, gate_b, ab = jnp.split(h @ w_in, cuts, axis=-1)
    qa = qa.reshape(bsz, seq, A_HEADS, A_HEAD_DIM)
    ka = ka.reshape(bsz, seq, A_KV_HEADS, A_HEAD_DIM)
    va = va.reshape(bsz, seq, A_KV_HEADS, A_HEAD_DIM)
    qkv_b = jax.nn.silu(dwconv_centred(qkv_b, conv_w))
    qb, kb, vb = jnp.split(qkv_b, [B_QK, 2 * B_QK], axis=-1)
    qb = l2norm(qb.reshape(bsz, seq, B_HEADS, B_DK))
    kb = l2norm(kb.reshape(bsz, seq, B_HEADS, B_DK))
    vb = vb.reshape(bsz, seq, B_HEADS, B_DV)
    ab = ab.astype(jnp.float32).reshape(bsz, seq, 2, 2, B_HEADS)
    g = -jnp.exp(a_log.astype(jnp.float32)) * jax.nn.softplus(ab[:, :, :, 0] + dt_bias.astype(jnp.float32))
    beta = jax.nn.sigmoid(ab[:, :, :, 1])
    scale = A_HEAD_DIM ** -0.5
    if ctx is None:
        oa = dense_attention(qa, ka, va, sink, scale)
        s0 = jnp.zeros((bsz, B_HEADS, B_DK, B_DV), jnp.float32)
        ob, s_f, s_b = delta_bidir(qb, kb, vb, g, beta, s0, s0)
        new_ctx = (ka, va, s_f.astype(h.dtype), s_b.astype(h.dtype))
    else:
        k_ctx, v_ctx, s0_f, s0_b = ctx
        cos, sin = axial_rope_tables(seq, A_HEAD_DIM)
        oa = window_ctx_attention(apply_rope(qa, cos, sin), apply_rope(ka, cos, sin), va,
                                  k_ctx, v_ctx, sink, scale)
        ob, _, _ = delta_bidir(qb, kb, vb, g, beta, s0_f, s0_b)
        new_ctx = None
    ob = rmsnorm(ob, out_norm) * jax.nn.silu(gate_b.reshape(bsz, seq, B_HEADS, B_DV))
    out = jnp.concatenate([oa.reshape(bsz, seq, A_Q), ob.reshape(bsz, seq, B_VW)], axis=-1) @ w_out
    return out, new_ctx

def odd_mixer(h, w_in, q_norm, kv_norm, w_q_up, w_kv_up, w_out, ctx):
    bsz, seq, _ = h.shape
    cq, ckv, kpe = jnp.split(h @ w_in, [C_Q_LORA, C_Q_LORA + C_KV_LORA], axis=-1)
    q = (rmsnorm(cq, q_norm) @ w_q_up).reshape(bsz, seq, C_HEADS, C_NOPE + C_ROPE)
    q_nope, q_pe = q[..., :C_NOPE], q[..., C_NOPE:]
    ckv = rmsnorm(ckv, kv_norm)
    if ctx is None:
        ckv_all, kpe_all = ckv, kpe
        new_ctx = (ckv, kpe)
    else:
        ckv_ctx, kpe_ctx = ctx
        cos, sin = axial_rope_tables(seq, C_ROPE)
        q_pe = apply_rope(q_pe, cos, sin)
        ckv_all = jnp.concatenate([ckv_ctx, ckv], axis=1)
        kpe_all = jnp.concatenate([kpe_ctx, apply_rope(kpe, cos, sin)], axis=1)
        new_ctx = None
    n_keys = ckv_all.shape[1]
    kv = (ckv_all @ w_kv_up).reshape(bsz, n_keys, C_HEADS, C_NOPE + C_V)
    k = jnp.concatenate([kv[..., :C_NOPE],
                         jnp.broadcast_to(kpe_all[:, :, None, :], (bsz, n_keys, C_HEADS, C_ROPE))], axis=-1)
    v = kv[..., C_NOPE:]
    o = dense_attention(jnp.concatenate([q_nope, q_pe], axis=-1), k, v, None, (C_NOPE + C_ROPE) ** -0.5)
    return o.reshape(bsz, seq, C_HEADS * C_V) @ w_out, new_ctx

def conv_ffn(h, w_up, conv_w, w_down):
    u = dwconv_centred(h @ w_up, conv_w)
    a, b = jnp.split(u, 2, axis=-1)
    return (jax.nn.silu(a) * b) @ w_down

def trunk_layer(l, x, cvec, prm, ctx):
    mod = jax.nn.silu(cvec) @ prm["w_mod"][l] + prm["b_mod"][l]
    shift1, scale1, gate1, shift2, scale2, gate2 = jnp.split(mod, N_MOD, axis=-1)
    h = rmsnorm(x, prm["norm_pre"][l, 0]) * (1.0 + scale1) + shift1
    j = l // 2
    if l % 2 == 0:
        mix, new_ctx = even_mixer(h, prm["ev_w_in"][j], prm["ev_conv"][j], prm["ev_a_log"][j],
                                  prm["ev_dt_bias"][j], prm["ev_sink"][j], prm["ev_out_norm"][j],
                                  prm["ev_w_out"][j], ctx)
    else:
        mix, new_ctx = odd_mixer(h, prm["od_w_in"][j], prm["od_q_norm"][j], prm["od_kv_norm"][j],
                                 prm["od_w_q_up"][j], prm["od_w_kv_up"][j], prm["od_w_out"][j], ctx)
    x = x + gate1 * rmsnorm(mix, prm["norm_post"][l, 0])
    h = rmsnorm(x, prm["norm_pre"][l, 1]) * (1.0 + scale2) + shift2
    f = conv_ffn(h, prm["ffn_w_up"][l], prm["ffn_conv"][l], prm["ffn_w_down"][l])
    x = x + gate2 * rmsnorm(f, prm["norm_post"][l, 1])
    return x, new_ctx

def setup_inputs(seed: int = 0) -> dict:
    key = jax.random.key(seed)
    ks = jax.random.split(key, 32)
    f32 = jnp.float32
    ne, no = (DEPTH + 1) // 2, DEPTH // 2

    def nrm(i, shape, scale=1.0):
        return scale * jax.random.normal(ks[i], shape, f32)

    def gain(i, shape):
        return 1.0 + 0.05 * jax.random.normal(ks[i], shape, f32)

    dt = jnp.exp(jax.random.uniform(ks[20], (ne, 2, B_HEADS), f32, math.log(1e-3), math.log(0.1)))
    dt_bias = dt + jnp.log(-jnp.expm1(-dt))
    a_log = jnp.log(jax.random.uniform(ks[19], (ne, 2, B_HEADS), f32, 1.0, 16.0))
    return {
        "x_prompt": nrm(0, (BATCH, SEQ, D_MODEL)),
        "x_sample": nrm(1, (DEC_BATCH, DEC_SEQ, D_MODEL)),
        "cache_attn_k": nrm(2, (DEC_BATCH, ne, PAST_LEN, A_KV_HEADS, A_HEAD_DIM)),
        "cache_attn_v": nrm(3, (DEC_BATCH, ne, PAST_LEN, A_KV_HEADS, A_HEAD_DIM)),
        "state_delta_fwd": nrm(4, (DEC_BATCH, ne, B_HEADS, B_DK, B_DV), B_DK ** -0.5),
        "state_delta_bwd": nrm(5, (DEC_BATCH, ne, B_HEADS, B_DK, B_DV), B_DK ** -0.5),
        "cache_mla_ckv": nrm(6, (DEC_BATCH, no, PAST_LEN, C_KV_LORA)),
        "cache_mla_kpe": nrm(7, (DEC_BATCH, no, PAST_LEN, C_ROPE)),
        "c": nrm(8, (DEC_BATCH, D_MODEL)),
        "c_ctx": nrm(9, (D_MODEL,)),
        "w_mod": nrm(10, (DEPTH, D_MODEL, N_MOD * D_MODEL), 0.5 * D_MODEL ** -0.5),
        "b_mod": nrm(11, (DEPTH, N_MOD * D_MODEL), 0.02),
        "norm_pre": gain(12, (DEPTH, 2, D_MODEL)),
        "norm_post": gain(13, (DEPTH, 2, D_MODEL)),
        "ffn_w_up": nrm(14, (DEPTH, D_MODEL, 2 * D_FF), D_MODEL ** -0.5),
        "ffn_conv": nrm(15, (DEPTH, FFN_CONV, 2 * D_FF), FFN_CONV ** -0.5),
        "ffn_w_down": nrm(16, (DEPTH, D_FF, D_MODEL), D_FF ** -0.5),
        "ev_w_in": nrm(17, (ne, D_MODEL, EVEN_IN), D_MODEL ** -0.5),
        "ev_conv": nrm(18, (ne, SHORT_CONV, B_CONV_CH), SHORT_CONV ** -0.5),
        "ev_a_log": a_log,
        "ev_dt_bias": dt_bias,
        "ev_sink": nrm(21, (ne, A_HEADS), 0.5),
        "ev_out_norm": gain(22, (ne, B_DV)),
        "ev_w_out": nrm(23, (ne, EVEN_OUT, D_MODEL), EVEN_OUT ** -0.5),
        "od_w_in": nrm(24, (no, D_MODEL, ODD_IN), D_MODEL ** -0.5),
        "od_q_norm": gain(25, (no, C_Q_LORA)),
        "od_kv_norm": gain(26, (no, C_KV_LORA)),
        "od_w_q_up": nrm(27, (no, C_Q_LORA, C_HEADS * (C_NOPE + C_ROPE)), C_Q_LORA ** -0.5),
        "od_w_kv_up": nrm(28, (no, C_KV_LORA, C_HEADS * (C_NOPE + C_V)), C_KV_LORA ** -0.5),
        "od_w_out": nrm(29, (no, C_HEADS * C_V, D_MODEL), (C_HEADS * C_V) ** -0.5),
    }

def reference(x_prompt, x_sample, cache_attn_k, cache_attn_v, state_delta_fwd, state_delta_bwd,
              cache_mla_ckv, cache_mla_kpe, c, c_ctx, w_mod, b_mod, norm_pre, norm_post,
              ffn_w_up, ffn_conv, ffn_w_down, ev_w_in, ev_conv, ev_a_log, ev_dt_bias, ev_sink,
              ev_out_norm, ev_w_out, od_w_in, od_q_norm, od_kv_norm, od_w_q_up, od_w_kv_up, od_w_out):
    prm = {
        "w_mod": w_mod, "b_mod": b_mod, "norm_pre": norm_pre, "norm_post": norm_post,
        "ffn_w_up": ffn_w_up, "ffn_conv": ffn_conv, "ffn_w_down": ffn_w_down,
        "ev_w_in": ev_w_in, "ev_conv": ev_conv, "ev_a_log": ev_a_log, "ev_dt_bias": ev_dt_bias,
        "ev_sink": ev_sink, "ev_out_norm": ev_out_norm, "ev_w_out": ev_w_out,
        "od_w_in": od_w_in, "od_q_norm": od_q_norm, "od_kv_norm": od_kv_norm,
        "od_w_q_up": od_w_q_up, "od_w_kv_up": od_w_kv_up, "od_w_out": od_w_out,
    }
    xp = x_prompt
    c_ctx_b = c_ctx[None, None, :]
    attn_k, attn_v, d_fwd, d_bwd, mla_ckv, mla_kpe = [], [], [], [], [], []
    for l in range(DEPTH):
        xp, ctx = trunk_layer(l, xp, c_ctx_b, prm, None)
        if l % 2 == 0:
            attn_k.append(ctx[0])
            attn_v.append(ctx[1])
            d_fwd.append(ctx[2])
            d_bwd.append(ctx[3])
        else:
            mla_ckv.append(ctx[0])
            mla_kpe.append(ctx[1])
    y_prompt = xp
    xs = x_sample
    c_b = c[:, None, :]
    for l in range(DEPTH):
        j = l // 2
        if l % 2 == 0:
            ctx = (cache_attn_k[:, j], cache_attn_v[:, j], state_delta_fwd[:, j], state_delta_bwd[:, j])
        else:
            ctx = (cache_mla_ckv[:, j], cache_mla_kpe[:, j])
        xs, _ = trunk_layer(l, xs, c_b, prm, ctx)
    y_sample = xs
    new_attn_k = jnp.stack(attn_k, axis=1)
    new_attn_v = jnp.stack(attn_v, axis=1)
    new_delta_fwd = jnp.stack(d_fwd, axis=1)
    new_delta_bwd = jnp.stack(d_bwd, axis=1)
    new_mla_ckv = jnp.stack(mla_ckv, axis=1)
    new_mla_kpe = jnp.stack(mla_kpe, axis=1)
    return (y_prompt, y_sample, new_attn_k, new_attn_v, new_delta_fwd, new_delta_bwd, new_mla_ckv, new_mla_kpe)


_drawn_inputs = setup_inputs


def setup_inputs(seed=0):
    import zlib

    import numpy as np

    out = dict(_drawn_inputs(seed))
    spreads = {}
    factors = {'cache_attn_k': 2.737,
     'state_delta_fwd': 3.653,
     'state_delta_bwd': 6.363,
     'cache_mla_kpe': 3.435,
     'ev_sink': 8.0,
     'ev_out_norm': 5.025,
     'od_q_norm': 8.0}
    for name, (base, spread) in spreads.items():
        noise = np.random.default_rng([zlib.crc32(name.encode()), seed]).standard_normal(out[name].shape)
        drawn = base * np.exp(spread * noise) if base else spread * noise
        out[name] = __import__('jax').numpy.asarray(drawn.astype(out[name].dtype))
    for name, factor in factors.items():
        out[name] = (out[name] * factor).astype(out[name].dtype)
    return out
```

```python
from contextlib import ExitStack

import numpy as np
import concourse.bass as bass
from concourse import mybir

ALU = mybir.AluOpType
ACT = mybir.ActivationFunctionType
AX_X = mybir.AxisListType.X
F32 = mybir.dt.float32
F32R = mybir.dt.float32r

P = 128
D = 1024
KD = D // P
PROMPT, SAMPLE, PAST = 128, 512, 128
P0, S0 = 1, 130
TW = 644
HW = TW // 2
CONDS = ((0, P0, P0 + PROMPT), (1, S0, S0 + SAMPLE))
TILES = [P0] + [S0 + P * t for t in range(SAMPLE // P)]
NT = len(TILES)
GRID_W = 64
A_HEADS, A_HD = 8, 64
A_Q, A_KV = 512, 128
B_HEADS = 4
C_HEADS, C_Q, C_KV, C_NOPE, C_ROPE, C_V = 8, 384, 256, 128, 64, 128
D_FF = 2816
FCH = D_FF // P
FH = FCH // 2
EPS = 1e-6
BIG = 1e30
LEVELS = 7
KMAX = FH

V_C, V_PRE, V_POST, V_ECONV, V_QN, V_KVN, V_ON = 0, 16, 48, 80, 116, 119, 121
V_FCONV, V_BMOD = 128, 392
(C_ID, C_ONES, C_SWAP, C_TRIU, C_TRIL) = range(5)
C_AMASK, C_COS, C_SIN = 5, 9, 13
C_LEVEL = 17
N_CONST = C_LEVEL + 2 * LEVELS


def shape_constants():
    i = np.arange(P)
    row, col = i[:, None], i[None, :]
    out = np.zeros((P, N_CONST, P), np.float32)
    out[:, C_ID] = row == col
    out[:, C_ONES] = 1.0
    out[:, C_SWAP] = row == (col ^ 32)
    out[:, C_TRIU] = row <= col
    out[:, C_TRIL] = row >= col
    out[:, C_AMASK] = np.where(col >= row, 0.0, -BIG)
    out[:, C_AMASK + 3] = np.where(col <= row, 0.0, -BIG)
    t = np.arange(SAMPLE)
    n_freq = A_HD // 4
    inv = (np.float32(10000.0) ** (-np.arange(n_freq, dtype=np.float32) / np.float32(n_freq))).astype(np.float32)
    ang = np.concatenate([(t // GRID_W).astype(np.float32)[:, None] * inv,
                          (t % GRID_W).astype(np.float32)[:, None] * inv], axis=-1)
    cos, sin = np.cos(ang), np.sin(ang)
    sign = np.where((i // 32) % 2 == 0, -1.0, 1.0).astype(np.float32)
    out[:, C_COS:C_COS + 4] = cos[:, i % 32].T.reshape(P, 4, P)
    out[:, C_SIN:C_SIN + 4] = (sin[:, i % 32].T * sign[:, None]).reshape(P, 4, P)
    for lv in range(LEVELS):
        s = 1 << lv
        low = ((row // s) % 2 == 1) & (col // s == row // s - 1)
        out[:, C_LEVEL + lv] = -low.astype(np.float32)
        out[:, C_LEVEL + LEVELS + lv] = -low.T.astype(np.float32)
    return out.reshape(P, N_CONST * P)


def block_table():
    blocks = [("even_in", KD)] * 23 + [("even_out", KD)] * 8
    blocks += ([("up", KD)] * (2 * FH) + [("down", FH)] * KD) * 2
    blocks += [("odd_in", KD)] * 6
    for h in range(C_HEADS):
        if h % 2 == 0:
            blocks.append(("q_rope", C_Q // P))
        blocks += [("q", C_Q // P), ("k", C_KV // P), ("v", C_KV // P)]
    blocks += [("odd_out", KD)] * 8
    blocks += ([("up", KD)] * (2 * FH) + [("down", FH)] * KD) * 2
    return blocks


def build(nc, a, outs):
    BL = block_table()
    N0_EVEN_IN, N0_EVEN_OUT, N0_FFN0 = 0, 23, 31
    N0_ODD_IN = N0_FFN0 + 2 * (2 * FH + KD)
    N0_ODD_H = N0_ODD_IN + 6
    N0_ODD_OUT = N0_ODD_H + 28
    N0_FFN = (N0_FFN0, N0_ODD_OUT + 8)
    assert len(BL) == N0_FFN[1] + 2 * (2 * FH + KD)

    y_prompt, y_sample, new_k, new_v, new_fwd, new_bwd, new_ckv, new_kpe = outs

    sems = {}
    stack = ExitStack()

    def S(name):
        if name not in sems:
            sems[name] = stack.enter_context(nc.semaphore(name))
        return sems[name]

    NORMS = (("pre00", KD, 1), ("l2", 8, 8), ("on", 4, 4), ("post00", KD, 1), ("pre01", KD, 1), ("post01", KD, 1),
             ("pre10", KD, 1), ("cq", C_Q // P, 1), ("ckv", C_KV // P, 1), ("post10", KD, 1), ("pre11", KD, 1),
             ("post11", KD, 1))
    CHUNKS = {name: k for name, k, _ in NORMS}

    def of(kind, tag, n):
        before = NORMS[:[name for name, _, _ in NORMS].index(tag)]
        if kind in ("stat", "ln", "rstd"):
            base = sum(s for _, _, s in before)
        elif kind == "sq":
            base = sum(k for _, k, _ in before)
        elif kind == "sum":
            base = sum(k for _, k, s in before if s == 1)
        else:
            group = "post" if kind in ("delta", "x") else "pre"
            base = sum(2 * k for name, k, _ in before if name.startswith(group))
        return S(f"norm_{kind}"), base + n

    def both(kind, c, n):
        return S(kind), 2 * n - 1 + c

    BASE = 16512
    at = [0]

    def al(n):
        return -(-n // 8) * 8

    def region(n):
        o = at[0]
        at[0] += al(n)
        return o

    def place(name, shape, off, dt=F32):
        return nc.alloc_sbuf_tensor_at(name, [P] + shape, dt, offset=BASE + 4 * off)

    R_X = region(KD * TW)
    R_H = region(2 * KD * TW)
    R_G = region(2 * al(FH * TW))
    R_F = region(KD * TW)
    R_RAW = region(2 * KMAX * P)
    R_W = region(4 * KMAX * P)
    R_CONST = region(17 * P)
    R_DC = region((N_CONST - 17) * P)
    R_VC = region(512)
    R_MOD = region(2 * 96 + 4 * 16 + 4 * 16)
    R_EPS = region(8)
    R_SC = region(48)
    R_T = region(6 * al(TW))
    assert BASE + 4 * at[0] <= nc.sbuf_usable_end, (BASE + 4 * at[0], nc.sbuf_usable_end)

    X = place("x_t", [KD, TW], R_X)
    Hh = place("h_hi", [KD, TW], R_H, F32R)
    Hl = place("h_lo", [KD, TW], R_H + KD * TW, F32R)
    Gh = place("g_hi", [FH, TW], R_G, F32R)
    Gl = place("g_lo", [FH, TW], R_G + al(FH * TW), F32R)
    F = place("f_t", [KD, TW], R_F)
    RAW = [place(f"w_raw{s}", [KMAX, P], R_RAW + s * KMAX * P) for s in range(2)]
    WH = [place(f"w_hi{s}", [KMAX, P], R_W + s * KMAX * P, F32R) for s in range(2)]
    WL = [place(f"w_lo{s}", [KMAX, P], R_W + (2 + s) * KMAX * P, F32R) for s in range(2)]
    CT = place("consts", [N_CONST, P], R_CONST)
    VC = place("vec_cols", [512], R_VC)
    MOD = [place(f"mod{l}", [96], R_MOD + 96 * l) for l in range(2)]
    PA = [[place(f"pre_gain{l}{i}", [16], R_MOD + 192 + 16 * (2 * l + i)) for i in range(2)] for l in range(2)]
    PG = [[place(f"post_gain{l}{i}", [16], R_MOD + 256 + 16 * (2 * l + i)) for i in range(2)] for l in range(2)]

    EPSC = place("eps", [8], R_EPS)

    def tslot(name, i, shape=None):
        return place(name, shape or [TW], R_T + i * al(TW))

    SQ = [tslot("sq0", 0), tslot("sq1", 1)]
    ACC = tslot("sq_sum", 2)
    RST = tslot("rstd", 3)
    TN = [tslot("scaled0", 4), tslot("scaled1", 5)]
    U = [tslot("u0", 0), tslot("u1", 1)]
    Y = [tslot("conv0", 2), tslot("conv1", 3)]
    SILU_A = tslot("silu_a", 4)
    GP = tslot("gated", 5)
    MWS = [place("w_shift", [KD, D], R_H), place("w_scale", [KD, D], R_G + NT * D)]
    XR = [place(f"x_rows{t}", [D], R_G + D * t) for t in range(NT)]
    MROW0 = place("mod_first_rows", [2 * D], R_T + 1024)
    VR = [place(f"vec_rows{b}", [P], R_T + P * b) for b in range(4)]
    SCX = place("silu_c", [16], R_SC)
    SCE = place("silu_e", [16], R_SC + 16)
    SCR = place("silu_r", [16], R_SC + 32)
    QA = place("qa_ka_va", [6, TW], R_G)
    QKV = place("qkv_b", [12, TW], R_G + 6 * TW)
    SG = place("silu_gate", [4, TW], R_G + 18 * TW)
    AB = tslot("ab_rows", 4)
    KTOK = place("k_tok", [NT, 4, P], R_F)
    VTOK = place("v_tok", [NT, 4, P], R_F + NT * 4 * P)
    gate_at = [R_T + 5 * al(TW)]

    def gate(name, n):
        o = gate_at[0]
        gate_at[0] += al(n)
        assert gate_at[0] <= R_T + 6 * al(TW)
        return place(name, [n], o)

    ABC = gate("ab_cols", NT * 16)
    ZG = gate("gate_z", NT * 8)
    ZA = gate("gate_t", NT * 8)
    G = gate("log_decay", NT * 8)
    BETA = gate("beta", NT * 8)
    GC = gate("decay_sum", NT * 8)
    GT = gate("decay_total", NT * 8)
    EB = gate("beta_decay", NT * 8)
    EK = gate("key_decay", NT * 8)
    DTB = gate("dt_bias_b", 8)
    EAL = gate("neg_exp_a_log", 8)
    ELC = [gate(f"tile_decay{c}", 4) for c in range(2)]

    def hslot(name, i, dt=F32):
        return place(name, [4, P], R_H + 512 * i, dt)

    DA = [hslot(f"d_a{c}", 9 * c + 0) for c in range(2)]
    DQ = [hslot(f"d_qk{c}", 9 * c + 1) for c in range(2)]
    QG = [hslot(f"q_decay{c}", 9 * c + 2) for c in range(2)]
    BS = [[hslot(f"level_b{c}{x}", 9 * c + (3, 7)[x]) for x in range(2)] for c in range(2)]
    VB = [hslot(f"v_beta{c}", 9 * c + 3) for c in range(2)]
    KBE = [hslot(f"k_beta_decay{c}", 9 * c + 7) for c in range(2)]
    ZS = [hslot(f"level_z{c}", 9 * c + 4) for c in range(2)]
    TS = [hslot(f"t_inv{c}", 9 * c + 5) for c in range(2)]
    UU = [hslot(f"u_tok{c}", 9 * c + 5) for c in range(2)]
    RS = [hslot(f"r_inv{c}", 9 * c + 6) for c in range(2)]
    WT = [hslot(f"w_t{c}", 9 * c + 6) for c in range(2)]
    KL = [hslot(f"k_state{c}", 9 * c + 8) for c in range(2)]
    ST = [hslot(f"state{c}", 18 + c) for c in range(2)]
    OD = place("o_delta", [4, TW], R_G + 14 * TW)
    MW = [place(f"w_mod_raw{s}", [KD, 2 * P], R_G + 6 * TW + s * 2 * KD * P) for s in range(2)]
    MROW = [place(f"mod_rows{s}", [2 * P], R_T + 3328 + 2 * P * s) for s in range(2)]
    SM = [place(f"scores{s}", [512], R_T + 512 * s) for s in range(2)]
    PR = [place(f"probs{s}", [512], R_T + 1024 + 512 * s) for s in range(2)]
    PT = [place(f"probs_t{s}", [512], R_T + 2048 + 512 * s) for s in range(2)]
    ASM = place("attn_small", [256], R_T + 3072)
    OA = [place(f"o_attn{s}", [512], R_F + 512 * s) for s in range(2)]
    KW = PAST + TW
    AKT = [place(f"k_attn{g}", [KW], R_F + 1024 + g * al(KW)) for g in range(2)]
    AV = place("v_attn_tok", [NT + 1, P], R_F + 1024 + 2 * al(KW))
    AKC = place("k_ctx_rows", [P], R_F + 1024 + 2 * al(KW) + (NT + 1) * P)
    AKO = place("k_out_rows", [P], R_F + 1024 + 2 * al(KW) + (NT + 2) * P)
    SNK = place("sink_b", [8], R_F + 1024 + 2 * al(KW) + (NT + 3) * P)
    SNK8 = place("sink_scaled", [8], R_F + 1024 + 2 * al(KW) + (NT + 3) * P + 8)
    g = [R_G]

    def gslot(name, shape, dt=F32):
        o = g[0]
        g[0] += al(int(np.prod(shape)))
        assert g[0] <= R_G + 2 * al(FH * TW) + KD * TW
        return place(name, shape, o, dt)

    CQ = gslot("cq", [3, TW])
    CKV = gslot("ckv", [2, KW])
    CQh = gslot("cq_hi", [3, TW], F32R)
    CQl = gslot("cq_lo", [3, TW], F32R)
    CKh = gslot("ckv_hi", [2, KW], F32R)
    CKl = gslot("ckv_lo", [2, KW], F32R)
    KPT = gslot("kpe_two", [KW])
    KPE = [gslot(f"kpe{r}", [KW]) for r in range(2)]
    QPE = [gslot(f"q_rope{s}", [TW]) for s in range(2)]
    QN = [gslot(f"q_nope{s}", [TW]) for s in range(2)]
    KN = [gslot(f"k_nope{s}", [KW]) for s in range(2)]
    VO = [gslot(f"v_head{s}", [NT + 1, P]) for s in range(2)]
    CROW = gslot("ckv_rows", [2, P])
    KROW = gslot("kpe_rows", [P])
    CP = [place(f"c_probs{s}", [640], R_T + 640 * s) for s in range(2)]
    CPT = [place(f"c_probs_t{s}", [640], R_T + 1280 + 640 * s) for s in range(2)]
    CSM = place("c_small", [256], R_T + 2560)
    ROT = place("rotated", [512], R_T + 2816)

    PS = stack.enter_context(nc.psum_tensor("ps", [P, 8 * 512], F32))

    def bank(b, n=512, p=P):
        return PS[0:p, b * 512:b * 512 + n]

    def pair(b, n=HW, p=P):
        return PS[0:p, b * 512:(b + 2) * 512].rearrange("p (h c) -> p h c", c=512)[:, :, 0:n]

    def halves(ap):
        return ap.rearrange("p (h c) -> p h c", h=2)

    def const(c, n=1):
        return CT[:, c, :] if n == 1 else CT[:, c:c + n, :]

    IDENT, ONES = const(C_ID), const(C_ONES)

    w_hi, w_lo, proj_done = S("w_hi_written"), S("w_lo_written"), S("proj_done")
    evac_a, evac_v = S("evacuated_a"), S("evacuated_v")

    def before(n, by_vector):
        return sum((name in ("even_out", "down", "odd_out")) == by_vector for name, _ in BL[:n])

    def evacuated(n):
        by_vector = before(n + 1, True) > before(n, True)
        return (evac_v if by_vector else evac_a), before(n + 1, by_vector)
    w_landed = [S("w_landed0"), S("w_landed1")]

    up_v = [a["ffn_w_up"][l].rearrange("(k p) f -> p k f", p=P) for l in range(2)]
    down_v = [a["ffn_w_down"][l].rearrange("(k p) n -> p k n", p=P) for l in range(2)]
    ein_v = a["ev_w_in"][0].rearrange("(k p) f -> p k f", p=P)
    eout_v = a["ev_w_out"][0].rearrange("(k p) n -> p k n", p=P)
    oin_v = a["od_w_in"][0].rearrange("(k p) f -> p k f", p=P)
    oout_v = a["od_w_out"][0].rearrange("(k p) n -> p k n", p=P)
    qup_v = a["od_w_q_up"][0].rearrange("(k p) f -> p k f", p=P)
    kvup_v = a["od_w_kv_up"][0].rearrange("(k p) f -> p k f", p=P)

    in_two = set(range(4)) | {N0_ODD_IN + 5} | {N0_ODD_H + 7 * h for h in range(C_HEADS // 2)}

    def landed_by(n):
        return 16 * sum(2 if m in in_two else 1 for m in range(n % 2, n + 1, 2))

    def odd_blocks(h):
        n = N0_ODD_H + 7 * (h // 2)
        return (n, n + 1, n + 2, n + 3) if h % 2 == 0 else (n, n + 4, n + 5, n + 6)

    def tile_of(r, c):
        return 0 if r == NT - 1 else (1 + r if c == 0 else NT - 1 - r)

    ATT = list(range(1, NT)) + [0]

    def att_local(t):
        return (128, 256) if t == 0 else (128 if t == 1 else 0, 384 if t == NT - 1 else 512)

    def att_tiles(t):
        if t == 0:
            return [(128, 0)]
        return ([(0, t - 1)] if t > 1 else []) + [(128, t), (256, NT)] + ([(384, t + 1)] if t < NT - 1 else [])

    def cols(m, s, odd):
        return m[:, :, :].rearrange("p h (b two s) -> p (h b) two s", two=2, s=s)[:, :, odd, :]

    def cols1(m, h, s, odd):
        return m[:, h, :].rearrange("p (b two s) -> p b two s", two=2, s=s)[:, :, odd, :]

    def compact(b, s, h=None):
        ap = bank(b, 256) if h is None else PS[:, b * 512 + 64 * h:b * 512 + 64 * h + 64]
        return ap.rearrange("p (b s) -> p b s", s=s)

    def per_head(m, g0):
        return m[:, g0:g0 + 4].unsqueeze(2).broadcast_to([P, 4, P])

    ALLU = [(t, h) for t in ATT for h in range(A_HEADS)]
    ODDU = [(h, t) for h in range(C_HEADS) for t in ATT]

    def row(m, j):
        return m[:, j, :] if isinstance(j, int) else m[:, bass.ds(j, 1), :].rearrange("p o c -> p (o c)")

    def vcol(base, j):
        return VC[:, base + j:base + j + 1] if isinstance(j, int) else VC[:, bass.ds(j + base, 1)]

    def q4(ap):
        return ap.rearrange("p (h c) -> p h c", c=P)

    def gates(t):
        return t[:, :].rearrange("p (t d h) -> p t d h", d=2, h=4)

    def abv(kind):
        return ABC[:, :].rearrange("p (t d k h) -> p t d k h", d=2, k=2, h=4)[:, :, :, kind, :]

    def att_copy_a(act, u):
        t, h = ALLU[u]
        c0, c1 = att_local(t)
        act.wait_ge(S("a_turned"), u + 1)
        if u >= 2:
            act.wait_ge(S("a_pv"), u - 1)
        act.activation(PT[u % 2][:, c0:c1], PS[:, 1024 + 512 * (u % 2) + c0:1024 + 512 * (u % 2) + c1], ACT.Copy
                       ).then_inc(S("a_pt"), 1)

    CSC, CTP, COUT = 4 * 512, 6 * 512, PS[:, 7 * 512 + 256:7 * 512 + 384]

    def odd_out_hi(act, u):
        h, t = ODDU[u]
        act.wait_ge(S("c_pv"), u + 1)
        act.activation(Hh[:, h, TILES[t]:TILES[t] + P], COUT, ACT.Copy).then_inc(S("c_out_hi"), 1)

    with stack:
        block = stack.enter_context(nc.Block())

        @block.sync
        def _(sp):
            def raw_free(n):
                if not isinstance(n, int) or n >= 2:
                    sp.wait_ge(w_lo, n - 1)

            def load(n, src, slot=None, k=None):
                slot = n % 2 if slot is None else slot
                k = BL[n][1] if k is None else k
                raw_free(n)
                sp.dma_start(RAW[slot][:, 0:k, 0:src.shape[-1]], src).then_inc(w_landed[slot], 16)

            def load_two(n, srcs):
                raw_free(n)
                for r in range(2):
                    sp.dma_start(RAW[n % 2][:, 0:BL[n][1], 64 * r:64 * r + 64], srcs[r]).then_inc(w_landed[n % 2], 16)

            def rows(dst, r0, src):
                sp.dma_start(dst[r0:r0 + src.shape[0], :], src).then_inc(S("vec_landed"), 16)

            consts = a["consts"].rearrange("p (c n) -> p c n", n=P)
            sp.dma_start(CT[:, 0:C_LEVEL, :], consts[:, 0:C_LEVEL, :]).then_inc(S("consts_landed"), 16)
            rows(VR[0], V_C, a["c_ctx"].rearrange("(k p) -> k p", p=P))
            rows(VR[0], V_C + 8, a["c"].rearrange("b (k p) -> (b k) p", p=P))
            rows(VR[0], V_PRE, a["norm_pre"].rearrange("l i (k p) -> (l i k) p", p=P))
            rows(VR[0], V_POST, a["norm_post"].rearrange("l i (k p) -> (l i k) p", p=P))
            rows(VR[0], V_ECONV, a["ev_conv"].rearrange("j t (k p) -> (j t k) p", p=P))
            rows(VR[0], V_QN, a["od_q_norm"].rearrange("j (k p) -> (j k) p", p=P))
            rows(VR[0], V_KVN, a["od_kv_norm"].rearrange("j (k p) -> (j k) p", p=P))
            rows(VR[0], V_ON, a["ev_out_norm"])
            fc = a["ffn_conv"].rearrange("l t (m p) -> (l t m) p", p=P)
            rows(VR[1], 0, fc[0:128, :])
            rows(VR[2], 0, fc[128:256, :])
            rows(VR[3], 0, fc[256:264, :])
            rows(VR[3], 8, a["b_mod"].rearrange("l (m p) -> (l m) p", p=P))
            for t in range(NT):
                src = a["x_prompt"][0] if t == 0 else a["x_sample"][0, (t - 1) * P:t * P, :]
                sp.dma_start(XR[t][:, :], src).then_inc(S("x_landed"), 16)
            wm = [a["w_mod"][l].rearrange("(k p) m -> p k m", p=P) for l in range(2)]
            for part in range(2):
                for q in range(2):
                    m0 = part * D + q * D // 2
                    sp.dma_start(MWS[part][:, :, q * D // 2:(q + 1) * D // 2], wm[0][:, :, m0:m0 + D // 2]
                                 ).then_inc(S(f"mod_landed{2 + 2 * part + q}"), 16)
            for c in range(4):
                load_two(c, [ein_v[:, :, 64 * h:64 * h + 64] for h in (c, c + 4)])
            for c in range(4, 22):
                load(c, ein_v[:, :, c * P:(c + 1) * P])
            load(22, ein_v[:, :, 22 * P:22 * P + 16])
            sp.dma_start(CT[:, C_LEVEL:, :], consts[:, C_LEVEL:, :]).then_inc(S("consts_landed"), 16)
            for m in range(2):
                load(N0_EVEN_OUT + m, eout_v[:, :, m * P:(m + 1) * P])
            sp.wait_ge(proj_done, N0_EVEN_IN + 23)
            for c, name in enumerate(("state_delta_fwd", "state_delta_bwd")):
                sp.dma_start(ST[c][:, :, :], a[name][0, 0].rearrange("h k v -> k h v")).then_inc(S("side_landed"), 16)
            sp.wait_ge(S("l2_done"), 8)
            for dst, name in ((DTB, "ev_dt_bias"), (EAL, "ev_a_log")):
                src = a[name][0].rearrange("(o d) h -> o (d h)", o=1).broadcast_to([P, 8])
                sp.dma_start(dst[:, :], src).then_inc(S("side_landed"), 16)
            for c, dst in enumerate((new_fwd, new_bwd)):
                sp.wait_ge(*both("state_done", c, NT))
                sp.dma_start(dst[0, 0].rearrange("h k v -> k h v"), ST[c][:, :, :]).then_inc(S("out_written"), 16)
            for c in range(2):
                sp.wait_ge(*both("o_done", c, NT))
            sp.dma_start(AKC[:, :], a["cache_attn_k"][0, 0].rearrange("t g d -> t (g d)")).then_inc(S("side_landed"), 16)
            sp.dma_start(AV[:, NT, :], a["cache_attn_v"][0, 0].rearrange("t g d -> t (g d)")).then_inc(S("side_landed"), 16)
            sp.dma_start(SNK[:, :], a["ev_sink"].broadcast_to([P, 8])).then_inc(S("side_landed"), 16)
            sp.wait_ge(S("k_out_rows"), 1)
            sp.dma_start(new_k[0, 0].rearrange("t g d -> t (g d)"), AKO[:, :]).then_inc(S("out_written"), 16)
            sp.wait_ge(S("v_rows"), 1)
            sp.dma_start(new_v[0, 0].rearrange("t g d -> t (g d)"), AV[:, 0, :]).then_inc(S("out_written"), 16)
            for l, first, count, done in ((0, 2 * D, 8, 0), (1, 0, 12, 16)):
                for s in range(2):
                    if l:
                        sp.wait_ge(S("mod_rows_done"), 4 + done + s - 1)
                    m0 = first + 2 * P * s
                    sp.dma_start(MW[s][:, :, :], wm[l][:, :, m0:m0 + 2 * P]).then_inc(S(f"mod_landed{s}"), 16)
                with sp.Fori(1, count) as i:
                    for s in range(2):
                        sp.wait_ge(S("mod_rows_done"), 2 * i + (4 + done + s - 1))
                        sp.dma_start(MW[s][:, :, :], wm[l][:, :, bass.ds(i * 4 * P + (first + 2 * P * s), 2 * P)]
                                     ).then_inc(S(f"mod_landed{s}"), 16)
            for m in range(2, 8):
                load(N0_EVEN_OUT + m, eout_v[:, :, m * P:(m + 1) * P])

            def ffn_loads(l):
                for half in range(2):
                    n0, j0 = N0_FFN[l] + half * (2 * FH + KD), half * FH
                    with sp.Fori(0, FH) as j:
                        for b in range(2):
                            load(n0 + b + 2 * j, up_v[l][:, :, bass.ds(j * P + (b * D_FF + j0 * P), P)],
                                 slot=(n0 + b) % 2, k=KD)
                    n1 = n0 + 2 * FH
                    with sp.Fori(0, KD // 2) as i:
                        for b in range(2):
                            load(n1 + b + 2 * i, down_v[l][:, j0:j0 + FH, bass.ds(i * 2 * P + b * P, P)],
                                 slot=(n1 + b) % 2, k=FH)

            ffn_loads(0)
            for c in range(2):
                load(N0_ODD_IN + c, oin_v[:, :, c * P:(c + 1) * P])
            sp.wait_ge(*of("x", "post01", 2 * KD))
            sp.dma_start(CROW[:, :, :], a["cache_mla_ckv"][0, 0].rearrange("t (k c) -> t k c", c=P)).then_inc(S("side_landed"), 16)
            for r in range(2):
                sp.dma_start(KROW[:, 64 * r:64 * r + 64], a["cache_mla_kpe"][0, 0]).then_inc(S("side_landed"), 16)
            for c in range(2, 5):
                load(N0_ODD_IN + c, oin_v[:, :, c * P:(c + 1) * P])
            load_two(N0_ODD_IN + 5, [oin_v[:, :, 640:704]] * 2)
            for h in range(C_HEADS):
                nr, nq, nk, nv = odd_blocks(h)
                c0 = h * (C_NOPE + C_ROPE)
                if h % 2 == 0:
                    c1 = c0 + C_NOPE
                    load_two(nr, [qup_v[:, :, c:c + 64] for c in (c1, c1 + C_NOPE + C_ROPE)])
                load(nq, qup_v[:, :, c0:c0 + P])
                load(nk, kvup_v[:, :, 2 * P * h:2 * P * h + P])
                load(nv, kvup_v[:, :, 2 * P * h + P:2 * P * h + 2 * P])
                if h == 0:
                    sp.wait_ge(S("c_out_rows"), 2)
                    sp.dma_start(new_ckv[0, 0].rearrange("t (k c) -> t k c", c=P), CROW[:, :, :]).then_inc(S("out_written"), 16)
                    sp.dma_start(new_kpe[0, 0], KROW[:, 0:64]).then_inc(S("out_written"), 16)
            for m in range(8):
                load(N0_ODD_OUT + m, oout_v[:, :, m * P:(m + 1) * P])
            ffn_loads(1)
            for t in range(NT):
                sp.wait_ge(S("y_rows_a"), t + 1)
                sp.wait_ge(S("y_rows_v"), t + 1)
                dst = y_prompt[0] if t == 0 else y_sample[0, (t - 1) * P:t * P, :]
                sp.dma_start(dst, XR[t][:, :]).then_inc(S("out_written"), 16)
            sp.wait_ge(S("out_written"), 16 * (2 + 2 + 2 + NT))

        @block.gpsimd
        def _(pool):
            def lo(n, slot=None, k=None):
                slot = n % 2 if slot is None else slot
                k = BL[n][1] if k is None else k
                pool.wait_ge(w_hi, n + 1)
                pool.tensor_tensor(WL[slot][:, 0:k, :], RAW[slot][:, 0:k, :], WH[slot][:, 0:k, :].bitcast(F32),
                                   ALU.subtract).then_inc(w_lo, 1)

            def zero_gaps(sem, *matrices):
                for x in matrices:
                    pool.memset(x[:, :, 0:1], 0.0)
                    pool.memset(x[:, :, P0 + PROMPT:S0], 0.0)
                    last = pool.memset(x[:, :, S0 + SAMPLE:TW], 0.0)
                last.then_inc(sem, 1)

            H2 = (Hh[:, :, :].bitcast(F32), Hl[:, :, :].bitcast(F32))

            pool.memset(EPSC[:, :], EPS).then_inc(S("eps_set"), 1)
            pool.wait_ge(S("mod_rows_done"), 4)
            zero_gaps(S("gap_zeroed_e"), *H2)
            lo(0)
            lo(1)
            for n in range(N0_EVEN_IN, N0_EVEN_IN + 23):
                lo(n + 2)
                if n == 2:
                    pool.wait_ge(S("x_turned"), 2 * NT)
                    pool.memset(QKV[:, :, 0:1], 0.0)
                    pool.memset(QKV[:, :, TW - 1:TW], 0.0).then_inc(S("qkv_edges"), 1)
            pool.wait_ge(S("kv_turned"), 2 * NT)
            zero_gaps(S("od_gaps"), OD[:, :, :])
            pool.wait_ge(S("consts_landed"), 32)
            for r in range(NT):
                def level(lv):
                    for c in range(2):
                        if lv == 0:
                            pool.wait_ge(*both("a_ready", c, r + 1))
                            if r > 0:
                                pool.wait_ge(*both("os_done", c, r))
                        elif lv == 1:
                            if r > 0:
                                pool.wait_ge(*both("uw_done", c, r))
                        else:
                            pool.wait_ge(*both("z_done", c, LEVELS * r + lv - 1))
                            if lv == 2:
                                pool.wait_ge(*both("t_written", c, (LEVELS - 1) * r + 1))
                        mask = CT[:, C_LEVEL + LEVELS * c + lv:C_LEVEL + LEVELS * c + lv + 1, :].broadcast_to([P, 4, P])
                        pool.tensor_tensor(BS[c][lv % 2][:, :, :], DA[c][:, :, :], mask, ALU.mult).then_inc(S("level_ready"), 1)
                level(0)
                level(1)
                for c in range(2):
                    mask = CT[:, (C_TRIU, C_TRIL)[c]:(C_TRIU, C_TRIL)[c] + 1, :].broadcast_to([P, 4, P])
                    pool.tensor_tensor(DQ[c][:, :, :], DQ[c][:, :, :], mask, ALU.mult).then_inc(S("decay_masked"), 1)
                level(2)
                if r == 0:
                    pool.wait_ge(S("k_tok"), NT)
                    pool.wait_ge(S("gates_ready"), 1)
                for c in range(2):
                    t = tile_of(r, c)
                    pool.tensor_tensor(KL[c][:, :, :], KTOK[:, t, :, :], per_head(EK, 8 * t + 4 * c), ALU.mult
                                       ).then_inc(S("kl_ready"), 1)
                for lv in range(3, LEVELS):
                    level(lv)
                for c in range(2):
                    t = tile_of(r, c)
                    pool.wait_ge(*both("z_done", c, LEVELS * r + LEVELS - 1))
                    pool.tensor_tensor(KBE[c][:, :, :], KTOK[:, t, :, :], per_head(EB, 8 * t + 4 * c), ALU.mult
                                       ).then_inc(S("kb_ready"), 1)
            for c in range(2):
                pool.wait_ge(*both("o_done", c, NT))
            zero_gaps(S("o_attn_gaps"), *(x[:, 0:4, :] for x in H2))
            for n in range(N0_EVEN_OUT, N0_EVEN_OUT + 8):
                lo(n + 2)

            def ffn(l):
                pool.wait_ge(proj_done, N0_FFN[l])
                zero_gaps(S(f"gap_zeroed{l}"), *H2)
                for x in (Gh, Gl):
                    x = x[:, :, :].bitcast(F32)
                    pool.memset(x[:, :, 0:1], 0.0)
                    last = pool.memset(x[:, :, TW - 1:TW], 0.0)
                last.then_inc(S(f"g_edges{l}"), 1)
                for half in range(2):
                    n0 = N0_FFN[l] + half * (2 * FH + KD)
                    c0 = FH * (2 * l + half)

                    def body(j, ks):
                        for b in range(2):
                            lo(n0 + 2 + b + 2 * j, slot=(n0 + b) % 2, k=ks)
                        pool.wait_ge(S("g_hi_written"), c0 + 1 + j)
                        pool.tensor_tensor(row(Gl, j)[:, 1:643], GP[:, 1:643], row(Gh, j)[:, 1:643].bitcast(F32),
                                           ALU.subtract).then_inc(S("g_lo_written"), 1)
                    with pool.Fori(0, FH - 1) as j:
                        body(j, KD)
                    body(FH - 1, FH)
                    n1 = n0 + 2 * FH
                    with pool.Fori(0, KD // 2 - 1) as i:
                        for b in range(2):
                            lo(n1 + 2 + b + 2 * i, slot=(n1 + b) % 2, k=FH)
                    for n in (n1 + KD, n1 + KD + 1):
                        if n < len(BL):
                            lo(n)
            ffn(0)
            for n in range(N0_ODD_IN + 2, N0_FFN[1] + 2):
                lo(n)
            ffn(1)

        @block.scalar
        def _(act):
            def hi(n, slot=None, k=None, landed=None):
                slot = n % 2 if slot is None else slot
                k = BL[n][1] if k is None else k
                act.wait_ge(w_landed[slot], landed_by(n) if landed is None else landed)
                if not isinstance(n, int) or n >= 2:
                    act.wait_ge(proj_done, n - 1)
                act.activation(WH[slot][:, 0:k, :], RAW[slot][:, 0:k, :], ACT.Copy).then_inc(w_hi, 1)

            def squares(tag, src, ready, count):
                for k in range(count):
                    ready(k)
                    if k >= 2:
                        act.wait_ge(*of("sum", tag, k - 1))
                    act.activation(SQ[k % 2][:, 0:TW], src(k), ACT.Square).then_inc(S("norm_sq"), 1)

            def rstd(tag, features):
                act.wait_ge(*of("stat", tag, 1))
                act.activation(halves(RST[:, :]), pair(4), ACT.Ln, scale=1.0 / features, bias=EPSC[:, 0:1]
                               ).then_inc(S("norm_ln"), 1)
                act.wait_ge(*of("ln", tag, 1))
                act.activation(RST[:, :], RST[:, :], ACT.Exp, scale=-0.5).then_inc(S("norm_rstd"), 1)

            def pre_norm(tag, l, i, ready):
                squares(tag, lambda k: X[:, k, :], ready, KD)
                rstd(tag, D)
                for k in range(KD):
                    for q, c0, c1 in CONDS:
                        act.wait_ge(*of("scaled", tag, 2 * k + q + 1))
                        col = 2 * (3 * i * 8 + k) + q
                        act.activation(Hh[:, k, c0:c1], TN[k % 2][:, c0:c1], ACT.Identity,
                                       bias=MOD[l][:, col:col + 1]).then_inc(S("norm_hh"), 1)

            def post_norm(tag, n0):
                squares(tag, lambda k: F[:, k, :], lambda k: act.wait_ge(*evacuated(n0 + k)), KD)
                rstd(tag, D)

            act.preload_act_table_set("natural_log_exp_and_others")
            act.wait_ge(S("vec_cols"), 2)
            act.activation(SCE[:, :], VC[:, 0:16], ACT.Exp, scale=-1.0).then_inc(S("exp_c"), 1)
            for t in range(NT):
                act.wait_ge(S("x_turned"), 2 * t + 1)
                act.activation(X[:, 0:4, TILES[t]:TILES[t] + P], bank(6).rearrange("p (k c) -> p k c", c=P),
                               ACT.Copy).then_inc(S("x_evac_a"), 1)
            act.wait_ge(S("mod_ready"), 1)
            act.wait_ge(S("x_evac_a"), NT)
            act.wait_ge(S("x_evac_v"), NT)
            act.wait_ge(S("eps_set"), 1)
            pre_norm("pre00", 0, 0, lambda k: None)
            hi(0)
            hi(1)

            for n in range(23):
                act.wait_ge(proj_done, n + 1)
                hi(n + 2)
                b = 2 * (n % 2)
                c = n - 6
                if n < 6:
                    act.activation(halves(QA[:, n, :]), pair(b), ACT.Copy).then_inc(evac_a, 1)
                elif n < 18:
                    if c >= 2:
                        act.wait_ge(S("e_conv"), 2 * (c - 1))
                        act.wait_ge(S("e_silu"), c - 1)
                    act.activation(halves(U[c % 2][:, :]), pair(b), ACT.Copy).then_inc(S("e_u"), 1)
                    act.activation(halves(Y[c % 2][:, :]), pair(b), ACT.Copy,
                                   scale=VC[:, V_ECONV + 12 + c:V_ECONV + 13 + c]).then_inc(evac_a, 1)
                if 1 <= c <= 12:
                    act.wait_ge(S("e_conv"), 2 * c)
                    act.activation(QKV[:, c - 1, 1:643], Y[(c - 1) % 2][:, 1:643], ACT.Silu).then_inc(S("e_silu"), 1)
                if 18 <= n < 22:
                    act.activation(halves(SG[:, n - 18, :]), pair(b), ACT.Silu).then_inc(evac_a, 1)
                elif n == 22:
                    act.activation(halves(AB[0:16, :]), pair(b, p=16), ACT.Copy).then_inc(evac_a, 1)

            act.preload_act_table_set("natural_log_exp_and_others")
            RL = [ACC, RST]

            def l2_square(c):
                act.wait_ge(S("e_silu"), 12)
                act.wait_ge(S("qkv_edges"), 1)
                if c >= 2:
                    act.wait_ge(*of("stat", "l2", c - 1))
                act.activation(SQ[c % 2][:, :], QKV[:, c, :], ACT.Square).then_inc(S("norm_sq"), 1)
            l2_square(0)
            l2_square(1)
            for c in range(8):
                act.wait_ge(*of("stat", "l2", c + 1))
                if c >= 2:
                    act.wait_ge(S("l2_done"), c - 1)
                act.activation(halves(RL[c % 2][:, :]), pair(4 + 2 * (c % 2)), ACT.Ln, bias=EPSC[:, 0:1]).then_inc(S("norm_ln"), 1)
                act.wait_ge(*of("ln", "l2", c + 1))
                act.activation(RL[c % 2][:, :], RL[c % 2][:, :], ACT.Exp, scale=-0.5).then_inc(S("norm_rstd"), 1)
                if c + 2 < 8:
                    l2_square(c + 2)

            act.wait_ge(S("gate_z"), 1)
            act.activation(ZA[:, :], ZG[:, :], ACT.Abs).then_inc(S("gate_act"), 1)
            act.wait_ge(S("gate_act"), 1)
            act.activation(ZA[:, :], ZA[:, :], ACT.Exp, scale=-1.0).then_inc(S("gate_act"), 1)
            act.wait_ge(S("gate_act"), 2)
            act.activation(ZA[:, :], ZA[:, :], ACT.Ln, bias=1.0).then_inc(S("gate_act"), 1)
            act.activation(gates(BETA), abv(1), ACT.Exp, scale=-1.0).then_inc(S("gate_act"), 1)
            act.activation(EAL[:, :], EAL[:, :], ACT.Exp).then_inc(S("gate_act"), 1)
            for t in range(NT):
                act.wait_ge(S("kv_turned"), 2 * t + 1)
                act.activation(KTOK[:, t, :, :], bank(4 + 2 * (t % 2)).rearrange("p (h c) -> p h c", c=P), ACT.Copy
                               ).then_inc(S("k_tok"), 1)
            act.wait_ge(S("decay_sums"), 1)
            act.activation(EB[:, :], GC[:, :], ACT.Exp).then_inc(S("gate_exp"), 1)
            act.activation(EK[:, :], GT[:, :], ACT.Exp).then_inc(S("gate_exp"), 1)

            act.wait_ge(S("v_tok"), NT)
            act.wait_ge(S("gates_ready"), 1)
            for r in range(NT):
                for c in range(2):
                    act.wait_ge(*both("d_args", c, r + 1))
                    act.activation(DQ[c][:, :, :], DQ[c][:, :, :], ACT.Abs).then_inc(S("d_abs"), 1)
                    if r > 0:
                        act.wait_ge(*both("os_done", c, r))
                    act.activation(QG[c][:, :, :], q4(bank(4 * c + 2)), ACT.Exp).then_inc(S("eg"), 1)
                    act.wait_ge(*both("d_abs", c, r + 1))
                    act.activation(DQ[c][:, :, :], DQ[c][:, :, :], ACT.Exp, scale=-1.0).then_inc(S("d_exp"), 1)
                for lv in range(1, LEVELS):
                    for c in range(2):
                        act.wait_ge(*both("z_done", c, LEVELS * r + lv + 1))
                        act.activation(ZS[c][:, :, :], q4(bank(4 * c)), ACT.Copy).then_inc(S("z_written"), 1)
                for c in range(2):
                    t = tile_of(r, c)
                    g0 = 8 * t + 4 * c
                    for h in range(4):
                        last = act.activation(VB[c][:, h, :], VTOK[:, t, h, :], ACT.Copy, scale=BETA[:, g0 + h:g0 + h + 1])
                    last.then_inc(S("vb_ready"), 1)
                if r < NT - 1:
                    for c in range(2):
                        act.wait_ge(*both("uw_done", c, r + 1))
                        act.activation(UU[c][:, :, :], q4(bank(4 * c + 2)), ACT.Copy).then_inc(S("u_written"), 1)

            def on_square(h):
                for c in range(2):
                    act.wait_ge(*both("o_done", c, NT))
                act.wait_ge(S("od_gaps"), 1)
                if h >= 2:
                    act.wait_ge(*of("stat", "on", h - 1))
                act.activation(SQ[h % 2][:, :], OD[:, h, :], ACT.Square).then_inc(S("norm_sq"), 1)
            on_square(0)
            on_square(1)
            for h in range(4):
                act.wait_ge(*of("stat", "on", h + 1))
                if h >= 2:
                    act.wait_ge(S("on_gated"), 2 * (h - 1))
                act.activation(halves(RL[h % 2][:, :]), pair(4 + 2 * (h % 2)), ACT.Ln, scale=1.0 / P, bias=EPSC[:, 0:1]
                               ).then_inc(S("norm_ln"), 1)
                act.wait_ge(*of("ln", "on", h + 1))
                act.activation(RL[h % 2][:, :], RL[h % 2][:, :], ACT.Exp, scale=-0.5).then_inc(S("norm_rstd"), 1)
                if h + 2 < 4:
                    on_square(h + 2)
                act.wait_ge(S("on_gated"), 2 * h + 2)
                act.activation(Hh[:, 4 + h, :], OD[:, h, :], ACT.Copy).then_inc(S("on_hi"), 1)

            for t in range(NT):
                act.wait_ge(S("va_turned"), t + 1)
                act.activation(AV[:, t, :], bank(6 + t % 2, P), ACT.Copy).then_inc(S("v_rows"), 1)

            def att_out(i, sem):
                t = ATT[i]
                act.wait_ge(S("oa_turned"), i + 1)
                act.activation(Hh[:, 0:4, TILES[t]:TILES[t] + P], q4(bank(6)), ACT.Copy).then_inc(S(sem), 1)

            for u, (t, h) in enumerate(ALLU):
                s = u % 2
                c0, c1 = att_local(t)
                act.wait_ge(S("a_max"), u + 1)
                if u >= 2:
                    act.wait_ge(S("a_turned"), u - 1)
                act.activation(PR[s][:, c0:c1], SM[s][:, c0:c1], ACT.Exp, bias=ASM[:, 64 + u:65 + u],
                               scale=A_HD ** -0.5, accum_out=ASM[:, 128 + u:129 + u]).then_inc(S("a_exp"), 1)
                act.activation(ASM[:, 192 + u:193 + u], SNK[:, h:h + 1], ACT.Exp, bias=ASM[:, 64 + u:65 + u]
                               ).then_inc(S("a_sink"), 1)
                if u >= 1:
                    att_copy_a(act, u - 1)
                if h == 3 and t != ATT[0]:
                    att_out(ATT.index(t) - 1, "oa_hi")
            att_copy_a(act, len(ALLU) - 1)
            att_out(NT - 1, "oa_hi")

            def out_proj(n0):
                for m in range(8):
                    act.wait_ge(proj_done, n0 + m + 1)
                    hi(n0 + m + 2)
            out_proj(N0_EVEN_OUT)
            act.preload_act_table_set("natural_log_exp_and_others")
            post_norm("post00", N0_EVEN_OUT)

            def ffn(l):
                for half in range(2):
                    n0 = N0_FFN[l] + half * (2 * FH + KD)
                    c0 = FH * (2 * l + half)
                    v0 = V_FCONV + (3 * l + 1) * 2 * FCH + half * FH

                    def body(j, ks):
                        c = c0 + j
                        for b in range(2):
                            n = n0 + b + 2 * j
                            slot = (n0 + b) % 2
                            act.wait_ge(proj_done, n + 1)
                            hi(n + 2, slot=slot, k=ks, landed=landed_by(n0 + b + 2) + 16 * j)
                            if not (isinstance(j, int) and c == 0):
                                act.wait_ge(S(f"f_conv{b}"), 2 * c)
                                act.wait_ge(S("f_silu"), c)
                                act.wait_ge(S("f_gated"), c)
                            act.activation(halves(U[b][:, :]), pair(2 * slot), ACT.Copy).then_inc(S("f_u"), 1)
                            act.activation(halves(Y[b][:, :]), pair(2 * slot), ACT.Copy, scale=vcol(v0 + b * FCH, j)
                                           ).then_inc(evac_a, 1)
                        act.wait_ge(S("f_conv0"), 2 * c + 2)
                        act.activation(SILU_A[:, 1:643], Y[0][:, 1:643], ACT.Silu).then_inc(S("f_silu"), 1)
                        act.wait_ge(S("f_gated"), c + 1)
                        act.activation(row(Gh, j)[:, 1:643], GP[:, 1:643], ACT.Copy).then_inc(S("g_hi_written"), 1)
                    body(0, KD)
                    with act.Fori(1, FH - 1) as j:
                        body(j, KD)
                    body(FH - 1, FH)
                    n1 = n0 + 2 * FH
                    with act.Fori(0, KD // 2 - 1) as i:
                        for b in range(2):
                            act.wait_ge(proj_done, n1 + b + 1 + 2 * i)
                            hi(n1 + b + 2 + 2 * i, slot=(n1 + b) % 2, k=FH, landed=landed_by(n1 + b + 2) + 16 * i)
                    for b in range(2):
                        n = n1 + KD - 2 + b
                        act.wait_ge(proj_done, n + 1)
                        if n + 2 < len(BL):
                            hi(n + 2)

            pre_norm("pre01", 0, 1, lambda k: act.wait_ge(*of("x", "post00", 2 * k + 2)))
            ffn(0)
            act.preload_act_table_set("natural_log_exp_and_others")
            post_norm("post01", N0_ODD_IN - KD)
            pre_norm("pre10", 1, 0, lambda k: act.wait_ge(*of("x", "post01", 2 * k + 2)))

            act.wait_ge(S("c_ctx_turned"), 1)
            act.activation(CKV[:, :, 0:PAST], bank(6, 256).rearrange("p (k c) -> p k c", c=P), ACT.Copy).then_inc(S("c_ctx"), 1)
            act.activation(KPT[:, 0:PAST], PS[:, 6 * 512 + 256:6 * 512 + 384], ACT.Copy).then_inc(S("c_ctx"), 1)
            for m in range(6):
                n = N0_ODD_IN + m
                act.wait_ge(proj_done, n + 1)
                hi(n + 2)
                dst = CQ[:, m, :] if m < 3 else CKV[:, m - 3, PAST:KW] if m < 5 else KPT[:, PAST:KW]
                act.activation(halves(dst), pair(2 * (n % 2)), ACT.Copy).then_inc(evac_a, 1)
                if m == 2:
                    squares("cq", lambda k: CQ[:, k, :], lambda k: act.wait_ge(*evacuated(N0_ODD_IN + k)), 3)
                    rstd("cq", C_Q)
                    for k in range(3):
                        act.wait_ge(S("cq_scaled"), k + 1)
                        act.activation(CQh[:, k, :], CQ[:, k, :], ACT.Copy).then_inc(S("cq_hi"), 1)
            act.wait_ge(*evacuated(N0_ODD_IN + 4))
            act.wait_ge(*of("stat", "cq", 1))
            squares("ckv", lambda k: CKV[:, k, PAST:KW], lambda k: act.wait_ge(S("cq_scaled"), 3), 2)
            rstd("ckv", C_KV)
            for k in range(2):
                act.wait_ge(S("ckv_scaled"), k + 1)
                act.activation(CKh[:, k, :], CKV[:, k, :], ACT.Copy).then_inc(S("ckv_hi"), 1)

            def head_evac(h):
                nr, nq, nk, nv = odd_blocks(h)
                if h >= 2:
                    act.wait_ge(S("c_pv"), NT * (h - 1))
                todo = [(nq, halves(QN[h % 2][:, :]), pair(2 * (nq % 2))),
                        (nk, halves(KN[h % 2][:, :]), pair(2 * (nk % 2), KW // 2)),
                        (nv, VO[h % 2][:, :, :].rearrange("p t c -> p (t c)"), PS[:, 1024 * (nv % 2):1024 * (nv % 2) + 768])]
                if h % 2 == 0:
                    todo.insert(0, (nr, halves(QPE[h // 2 % 2][:, :]), pair(2 * (nr % 2))))
                for n, dst, src in todo:
                    act.wait_ge(proj_done, n + 1)
                    hi(n + 2)
                    act.activation(dst, src, ACT.Copy).then_inc(evac_a, 1)

            def odd_turned_copy(u):
                h, t = ODDU[u]
                s = u % 2
                act.wait_ge(S("c_turned"), u + 1)
                if u >= 2:
                    act.wait_ge(S("c_pv"), u - 1)
                if t != 0:
                    act.activation(CPT[s][:, 512:640], PS[:, CTP + 512:CTP + 640], ACT.Copy).then_inc(S("c_pt7"), 1)
                w = P if t == 0 else 512
                act.activation(CPT[s][:, 0:w], PS[:, CTP:CTP + w], ACT.Copy).then_inc(S("c_pt"), 1)
            head_evac(0)
            for u, (h, t) in enumerate(ODDU):
                s = u % 2
                w = P if t == 0 else 640
                if u >= 1:
                    odd_turned_copy(u - 1)
                act.wait_ge(S("c_max"), u + 1)
                if u >= 2:
                    act.wait_ge(S("c_turned"), u - 1)
                act.activation(CP[s][:, 0:w], PS[:, CSC:CSC + w], ACT.Exp, bias=CSM[:, 64 + u:65 + u],
                               scale=(C_NOPE + C_ROPE) ** -0.5, accum_out=CSM[:, 128 + u:129 + u]).then_inc(S("c_exp"), 1)
                if u >= 2:
                    odd_out_hi(act, u - 2)
                if t == ATT[1] and h + 1 < C_HEADS:
                    head_evac(h + 1)
            odd_turned_copy(len(ODDU) - 1)
            odd_out_hi(act, len(ODDU) - 2)
            odd_out_hi(act, len(ODDU) - 1)

            out_proj(N0_ODD_OUT)
            post_norm("post10", N0_ODD_OUT)
            pre_norm("pre11", 1, 1, lambda k: act.wait_ge(*of("x", "post10", 2 * k + 2)))
            ffn(1)
            act.preload_act_table_set("natural_log_exp_and_others")
            post_norm("post11", len(BL) - KD)
            for t in range(NT):
                act.wait_ge(S("y_turned"), 2 * t + 1)
                act.activation(XR[t][:, 0:512], bank(6), ACT.Copy).then_inc(S("y_rows_a"), 1)

        @block.vector
        def _(dve):
            steps = {}

            def step(ins, signal="dve_step"):
                steps[signal] = steps.get(signal, 0) + 1
                ins.then_inc(S(signal), 1)
                dve.wait_ge(S(signal), steps[signal])

            def sums(tag, count):
                for k in range(count):
                    dve.wait_ge(*of("sq", tag, k + 1))
                    if k == 0:
                        dve.tensor_copy(ACC[:, :], SQ[0][:, :]).then_inc(S("norm_sum"), 1)
                    else:
                        dve.wait_ge(*of("sum", tag, k))
                        dve.tensor_tensor(ACC[:, :], ACC[:, :], SQ[k % 2][:, :], ALU.add).then_inc(S("norm_sum"), 1)

            def pre_norm(tag, l, i):
                sums(tag, KD)
                dve.wait_ge(*of("rstd", tag, 1))

                def lo(k):
                    for q, c0, c1 in CONDS:
                        col = 2 * (3 * i * 8 + k) + q
                        dve.wait_ge(*of("hh", tag, 2 * k + q + 1))
                        dve.scalar_tensor_tensor(Hl[:, k, c0:c1], TN[k % 2][:, c0:c1], MOD[l][:, col:col + 1],
                                                 Hh[:, k, c0:c1].bitcast(F32), ALU.add, ALU.subtract
                                                 ).then_inc(S("norm_hl"), 1)
                for k in range(KD):
                    for q, c0, c1 in CONDS:
                        if k >= 2:
                            dve.wait_ge(*of("hl", tag, 2 * (k - 2) + q + 1))
                        dve.scalar_tensor_tensor(TN[k % 2][:, c0:c1], X[:, k, c0:c1], PA[l][i][:, 2 * k + q:2 * k + q + 1],
                                                 RST[:, c0:c1], ALU.mult, ALU.mult).then_inc(S("norm_scaled"), 1)
                    if k >= 1:
                        lo(k - 1)
                lo(KD - 1)

            def post_norm(tag, l, i):
                sums(tag, KD)
                dve.wait_ge(*of("rstd", tag, 1))
                for k in range(KD + 1):
                    if k < KD:
                        for q, c0, c1 in CONDS:
                            if k >= 2:
                                dve.wait_ge(*of("x", tag, 2 * (k - 2) + q + 1))
                            dve.scalar_tensor_tensor(TN[k % 2][:, c0:c1], F[:, k, c0:c1],
                                                     PG[l][i][:, 2 * k + q:2 * k + q + 1], RST[:, c0:c1],
                                                     ALU.mult, ALU.mult).then_inc(S("norm_delta"), 1)
                    if k >= 1:
                        for q, c0, c1 in CONDS:
                            dve.wait_ge(*of("delta", tag, 2 * (k - 1) + q + 1))
                            dve.tensor_tensor(X[:, k - 1, c0:c1], X[:, k - 1, c0:c1], TN[(k - 1) % 2][:, c0:c1], ALU.add
                                              ).then_inc(S("norm_x"), 1)

            def mod_columns(l, m0, m1, b, c0):
                step(dve.tensor_tensor(MOD[l][:, 2 * m0:2 * m1].rearrange("p (m q) -> p m q", q=2),
                                       PS[:, b * 512 + c0:b * 512 + c0 + 2 * (m1 - m0)].rearrange("p (m q) -> p m q", q=2),
                                       VC[:, V_BMOD + 48 * l + m0:V_BMOD + 48 * l + m1].unsqueeze(2).broadcast_to([P, m1 - m0, 2]),
                                       ALU.add))

            def gains(l, i, part, signal="dve_step"):
                dst, vec, op = ((PA, V_PRE, ALU.add), (PG, V_POST, ALU.mult))[part - 1]
                m0 = 2 * 8 * (3 * i + part)
                v0 = vec + (2 * l + i) * 8
                step(dve.scalar_tensor_tensor(
                    dst[l][i][:, :].rearrange("p (k q) -> p k q", q=2),
                    MOD[l][:, m0:m0 + 16].rearrange("p (k q) -> p k q", q=2), 1.0,
                    VC[:, v0:v0 + 8].unsqueeze(2).broadcast_to([P, 8, 2]), op, ALU.mult), signal)

            dve.memset(X[:, :, 0:1], 0.0)
            dve.memset(X[:, :, P0 + PROMPT:S0], 0.0)
            dve.memset(X[:, :, S0 + SAMPLE:TW], 0.0)
            dve.wait_ge(S("vec_turned"), 4)
            dve.tensor_copy(VC[:, 0:122], bank(4, 122)).then_inc(S("vec_cols"), 1)
            dve.tensor_copy(VC[:, 128:488], PS[:, 4 * 512 + 128:4 * 512 + 488]).then_inc(S("vec_cols"), 1)
            dve.wait_ge(S("exp_c"), 1)
            step(dve.tensor_scalar(SCR[:, :], SCE[:, :], 1.0, None, ALU.add))
            step(dve.reciprocal(SCR[:, :], SCR[:, :]))
            dve.tensor_tensor(SCX[:, :], SCR[:, :], VC[:, 0:16], ALU.mult).then_inc(S("silu_c"), 1)
            for t in range(NT):
                dve.wait_ge(S("x_turned"), 2 * t + 2)
                dve.tensor_copy(X[:, 4:8, TILES[t]:TILES[t] + P], q4(bank(7))).then_inc(S("x_evac_v"), 1)
            dve.wait_ge(S("eps_set"), 1)
            for q in range(4):
                dve.wait_ge(S("mod_rows_done"), q + 1)
                dve.tensor_copy(MROW0[0:2, 512 * q:512 * q + 512], bank(q, p=2)).then_inc(S("mod_rows"), 1)
            dve.wait_ge(S("mod_turned"), 4)
            mod_columns(0, 0, 16, 5, 0)
            gains(0, 0, 1, "mod_ready")
            pre_norm("pre00", 0, 0)

            for c in range(12):
                y, u = Y[c % 2], U[c % 2]
                dve.wait_ge(S("e_u"), c + 1)
                dve.wait_ge(*evacuated(6 + c))
                dve.scalar_tensor_tensor(y[:, 1:643], u[:, 0:642], VC[:, V_ECONV + c:V_ECONV + c + 1], y[:, 1:643],
                                         ALU.mult, ALU.add).then_inc(S("e_conv"), 1)
                dve.wait_ge(S("e_conv"), 2 * c + 1)
                dve.scalar_tensor_tensor(y[:, 1:643], u[:, 2:644], VC[:, V_ECONV + 24 + c:V_ECONV + 25 + c], y[:, 1:643],
                                         ALU.mult, ALU.add).then_inc(S("e_conv"), 1)

            for c in range(8):
                dve.wait_ge(*of("rstd", "l2", c + 1))
                dve.scalar_tensor_tensor(QKV[:, c, 1:643], QKV[:, c, 1:643], P ** -0.5 if c < 4 else 1.0,
                                         [ACC, RST][c % 2][:, 1:643], ALU.mult, ALU.mult).then_inc(S("l2_done"), 1)

            dve.wait_ge(S("ab_turned"), NT)
            step(dve.tensor_copy(ABC[:, :], bank(6, NT * 16)))
            dve.wait_ge(S("side_landed"), 64)
            for t in range(NT):
                last = dve.tensor_tensor(gates(ZG)[:, t], abv(0)[:, t], DTB[:, :].rearrange("p (d h) -> p d h", d=2), ALU.add)
            last.then_inc(S("gate_z"), 1)
            dve.wait_ge(S("gate_z"), 1)
            dve.wait_ge(S("gate_act"), 5)
            step(dve.tensor_scalar(BETA[:, :], BETA[:, :], 1.0, None, ALU.add))
            step(dve.reciprocal(BETA[:, :], BETA[:, :]))
            step(dve.tensor_scalar(EAL[:, :], EAL[:, :], -1.0, None, ALU.mult))
            step(dve.scalar_tensor_tensor(G[:, :], ZG[:, :], 0.0, ZA[:, :], ALU.max, ALU.add))
            for t in range(NT):
                last = dve.tensor_tensor(G[:, 8 * t:8 * t + 8], G[:, 8 * t:8 * t + 8], EAL[:, :], ALU.mult)
            last.then_inc(S("log_decay"), 1)
            for t in range(NT):
                dve.wait_ge(S("kv_turned"), 2 * t + 2)
                dve.tensor_copy(VTOK[:, t, :, :], q4(bank(5 + 2 * (t % 2)))).then_inc(S("v_tok"), 1)
            dve.wait_ge(S("decay_cols"), 1)
            for d in range(2):
                dve.tensor_copy(gates(GC)[:, :, d, :], PS[:, 20 * d:20 * d + 20].rearrange("p (t h) -> p t h", h=4))
            step(dve.tensor_copy(GT[:, :], PS[:, 40:80]))
            step(dve.tensor_tensor(GT[:, :], GT[:, :], GC[:, :], ALU.subtract), "decay_sums")
            dve.wait_ge(S("gate_exp"), 2)
            step(dve.tensor_tensor(EB[:, :], EB[:, :], BETA[:, :], ALU.mult), "gates_ready")

            ident4 = CT[:, C_ID:C_ID + 1, :].broadcast_to([P, 4, P])
            for r in range(NT):
                n0, t0 = LEVELS * r, (LEVELS - 1) * r
                for c in range(2):
                    g0 = 8 * tile_of(r, c) + 4 * c
                    dve.wait_ge(*both("gc_row", c, r + 1))
                    if r > 0:
                        dve.wait_ge(*both("os_done", c, r))
                    dve.tensor_tensor(DQ[c][:, :, :], q4(bank(4 * c + 2)), per_head(GC, g0), ALU.subtract).then_inc(S("d_args"), 1)
                for c in range(2):
                    g0 = 8 * tile_of(r, c) + 4 * c
                    dve.wait_ge(*both("d_exp", c, r + 1))
                    dve.wait_ge(*both("kk_done", c, r + 1))
                    if r > 0:
                        dve.wait_ge(*both("level_ready", c, n0))
                    for h in range(4):
                        last = dve.scalar_tensor_tensor(DA[c][:, h, :], PS[:, 4 * c * 512 + P * h:4 * c * 512 + P * h + P],
                                                        BETA[:, g0 + h:g0 + h + 1], DQ[c][:, h, :], ALU.mult, ALU.mult)
                    last.then_inc(S("a_ready"), 1)
                for c in range(2):
                    dve.wait_ge(*both("level_ready", c, n0 + 1))
                    dve.tensor_tensor(TS[c][:, :, :], BS[c][0][:, :, :], ident4, ALU.add).then_inc(S("t_written"), 1)
                    dve.wait_ge(*both("z_done", c, n0 + 1))
                    dve.tensor_tensor(RS[c][:, :, :], q4(bank(4 * c)), ident4, ALU.add).then_inc(S("r_written"), 1)
                for lv in range(1, LEVELS):
                    s = 1 << lv
                    for c in range(2):
                        dve.wait_ge(*both("tr_done", c, t0 + lv))
                        dve.wait_ge(*both("r_written", c, n0 + lv))
                        dve.tensor_tensor(cols(RS[c], s, 1 - c), cols(RS[c], s, 1 - c), compact(4 * c + 3, s), ALU.add
                                          ).then_inc(S("r_written"), 1)
                        if lv < LEVELS - 1:
                            dve.wait_ge(*both("t_written", c, t0 + lv))
                            dve.tensor_tensor(cols(TS[c], s, c), cols(TS[c], s, c), compact(4 * c + 2, s), ALU.add
                                              ).then_inc(S("t_written"), 1)
                    if lv == 1:
                        for c in range(2):
                            T0 = TILES[tile_of(r, c)]
                            dve.wait_ge(*both("decay_masked", c, r + 1))
                            dve.wait_ge(*both("kq_done", c, r + 1))
                            dve.tensor_tensor(DQ[c][:, :, :], q4(bank(4 * c + 1)), DQ[c][:, :, :], ALU.mult
                                              ).then_inc(S("qk_ready"), 1)
                            dve.wait_ge(*both("eg", c, r + 1))
                            col = P - 1 if c == 0 else 0
                            if r > 0:
                                dve.wait_ge(*both("state_done", c, r))
                            step(dve.tensor_copy(ELC[c][:, :].unsqueeze(2), QG[c][:, :, col:col + 1]))
                            dve.tensor_tensor(QG[c][:, :, :], QG[c][:, :, :], QKV[:, 0:4, T0:T0 + P], ALU.mult
                                              ).then_inc(S("q_ready"), 1)
                for c in range(2):
                    dve.wait_ge(*both("uw_done", c, r + 1))
                    if r < NT - 1:
                        dve.tensor_copy(WT[c][:, :, :], q4(bank(4 * c + 3))).then_inc(S("w_written"), 1)
                for c in range(2):
                    if r < NT - 1:
                        dve.wait_ge(*both("ws_done", c, r + 1))
                        dve.wait_ge(*both("u_written", c, r + 1))
                        dve.tensor_tensor(VB[c][:, :, :], UU[c][:, :, :], q4(bank(4 * c)), ALU.subtract).then_inc(S("v_new"), 1)
                    else:
                        dve.tensor_copy(VB[c][:, :, :], q4(bank(4 * c + 2))).then_inc(S("v_new"), 1)
                for c in range(2):
                    t = tile_of(r, c)
                    T0 = TILES[t]
                    dve.wait_ge(*both("os_done", c, r + 1))
                    if r < NT - 1:
                        for h in range(4):
                            q0 = (4 * c + 2) * 512 + P * h
                            last = dve.scalar_tensor_tensor(ST[c][:, h, :], ST[c][:, h, :], ELC[c][:, h:h + 1],
                                                            PS[:, q0:q0 + P], ALU.mult, ALU.add)
                        last.then_inc(S("state_done"), 1)
                    else:
                        dve.tensor_copy(ST[c][:, :, :], q4(bank(4 * c + 2))).then_inc(S("state_done"), 1)
                    dst = OD[:, :, T0:T0 + P]
                    first = r < 2 or (r == NT - 1 and c == 0)
                    if first:
                        dve.tensor_copy(dst, q4(bank(4 * c + 1))).then_inc(S("o_done"), 1)
                    else:
                        for cc in range(2):
                            if r == NT - 1 and cc == 1:
                                continue
                            dve.wait_ge(*both("o_done", cc, 2 if r < NT - 1 else NT))
                        dve.tensor_tensor(dst, dst, q4(bank(4 * c + 1)), ALU.add).then_inc(S("o_done"), 1)

            dve.wait_ge(S("out_written"), 32)
            for h in range(4):
                RL = [ACC, RST][h % 2]
                dve.wait_ge(*of("rstd", "on", h + 1))
                dve.scalar_tensor_tensor(OD[:, h, :], OD[:, h, :], VC[:, V_ON:V_ON + 1], RL[:, :],
                                         ALU.mult, ALU.mult).then_inc(S("on_gated"), 1)
                dve.wait_ge(S("on_gated"), 2 * h + 1)
                dve.tensor_tensor(OD[:, h, :], OD[:, h, :], SG[:, h, :], ALU.mult).then_inc(S("on_gated"), 1)
                if h > 0:
                    dve.wait_ge(S("on_hi"), h)
                    dve.tensor_tensor(Hl[:, 3 + h, :], OD[:, h - 1, :], Hh[:, 3 + h, :].bitcast(F32), ALU.subtract)
            dve.wait_ge(S("on_hi"), 4)
            dve.tensor_tensor(Hl[:, 7, :], OD[:, 3, :], Hh[:, 7, :].bitcast(F32), ALU.subtract).then_inc(S("on_lo"), 1)

            def rope(dst, b, turned, n):
                dve.wait_ge(turned, n)
                step(dve.tensor_tensor(ROT[:, :], bank(b), CT[:, C_SIN:C_SIN + 4, :].rearrange("p a b -> p (a b)"), ALU.mult))
                step(dve.tensor_tensor(dst, dst, CT[:, C_COS:C_COS + 4, :].rearrange("p a b -> p (a b)"), ALU.mult))
                return dve.tensor_tensor(dst, dst, ROT[:, :], ALU.add)

            dve.wait_ge(S("ka_turned"), 1)
            dve.tensor_copy(AKO[:, :], PS[:, 5 * 512 + P:5 * 512 + 2 * P]).then_inc(S("k_out_rows"), 1)
            for c in range(5):
                step(rope(QA[:, c, S0:S0 + SAMPLE], c % 4, S("a_swapped"), c + 1), "a_roped")
            dve.wait_ge(S("side_landed"), 16 * 7)
            for g2 in range(2):
                z = slice(64 * (1 - g2), 64 * (1 - g2) + 64)
                o = slice(64 * g2, 64 * g2 + 64)
                dve.memset(AKT[g2][z, :], 0.0)
                dve.tensor_copy(AKT[g2][o, 0:PAST], PS[o, 5 * 512:5 * 512 + P])
                for q, c0, c1 in CONDS:
                    dve.tensor_copy(AKT[g2][o, PAST + c0:PAST + c1], QA[o, 4, c0:c1])
            step(dve.tensor_scalar(SNK8[:, :], SNK[:, :], A_HD ** 0.5, None, ALU.mult), "k_attn")

            def att_scale(u):
                t, h = ALLU[u]
                i = ATT.index(t)
                dve.wait_ge(S("a_sink"), u + 1)
                step(dve.tensor_tensor(ASM[:, u:u + 1], ASM[:, 128 + u:129 + u], ASM[:, 192 + u:193 + u], ALU.add))
                step(dve.reciprocal(ASM[:, u:u + 1], ASM[:, u:u + 1]))
                dve.wait_ge(S("a_pv"), u + 1)
                if h == 0 and i >= 2:
                    dve.wait_ge(S("oa_turned"), i - 1)
                q0 = (4 + u % 2) * 512 + 64 * h
                dve.tensor_scalar(OA[i % 2][:, 64 * h:64 * h + 64], PS[:, q0:q0 + 64], ASM[:, u:u + 1], None, ALU.mult
                                  ).then_inc(S("oa_scaled"), 1)

            def att_lo(i):
                t = ATT[i]
                dve.wait_ge(S("oa_hi"), i + 1)
                dve.tensor_tensor(Hl[:, 0:4, TILES[t]:TILES[t] + P], q4(bank(6)),
                                  Hh[:, 0:4, TILES[t]:TILES[t] + P].bitcast(F32), ALU.subtract).then_inc(S("oa_lo"), 1)

            def mod_rows(u):
                dve.wait_ge(S("mod_rows_done"), 4 + u + 1)
                if u >= 2:
                    dve.wait_ge(S("mod_turned"), 4 + u - 1)
                dve.tensor_copy(MROW[u % 2][0:2, :], bank(7, 256, 2)).then_inc(S("mod_rows"), 1)

            for u, (t, h) in enumerate(ALLU):
                s = u % 2
                c0, c1 = att_local(t)
                dve.wait_ge(S("a_scores"), u + 1)
                if u >= 2:
                    dve.wait_ge(S("a_exp"), u - 1)
                dve.tensor_tensor_reduce(SM[s][:, c0:c1], PS[:, 512 * s + c0:512 * s + c1],
                                         CT[:, C_AMASK:C_AMASK + 4, :].rearrange("p a b -> p (a b)")[:, c0:c1],
                                         1.0, SNK8[:, h:h + 1], ALU.add, ALU.max, ASM[:, u:u + 1]).then_inc(S("a_rowmax"), 1)
                dve.wait_ge(S("a_rowmax"), u + 1)
                dve.tensor_scalar(ASM[:, 64 + u:65 + u], ASM[:, u:u + 1], -A_HD ** -0.5, None, ALU.mult).then_inc(S("a_max"), 1)
                if u >= 2:
                    att_scale(u - 2)
                if u >= 1:
                    mod_rows(u - 1)
                if h == 4 and t != ATT[0]:
                    att_lo(ATT.index(t) - 1)
            mod_rows(39)
            att_scale(len(ALLU) - 2)
            att_scale(len(ALLU) - 1)
            att_lo(NT - 1)
            dve.wait_ge(S("mod_turned"), 4 + 40)
            mod_columns(0, 16, 48, 7, 352)
            mod_columns(1, 0, 48, 7, 352 + 64)
            for l in range(2):
                for i in range(2):
                    if (l, i) != (0, 0):
                        gains(l, i, 1)
                    gains(l, i, 2)

            def out_evac(n0):
                for m in range(8):
                    dve.wait_ge(proj_done, n0 + m + 1)
                    dve.tensor_copy(halves(F[:, m, :]), pair(2 * ((n0 + m) % 2))).then_inc(evac_v, 1)

            def ffn(l):
                for half in range(2):
                    n0 = N0_FFN[l] + half * (2 * FH + KD)
                    c0 = FH * (2 * l + half)
                    v0 = V_FCONV + 3 * l * 2 * FCH + half * FH

                    def body(j):
                        c = c0 + j
                        for b in range(2):
                            dve.wait_ge(evac_a, before(n0, False) + b + 1 + 2 * j)
                            y, u = Y[b], U[b]
                            dve.scalar_tensor_tensor(y[:, 1:643], u[:, 0:642], vcol(v0 + b * FCH, j), y[:, 1:643],
                                                     ALU.mult, ALU.add).then_inc(S(f"f_conv{b}"), 1)
                            dve.wait_ge(S(f"f_conv{b}"), 2 * c + 1)
                            last = dve.scalar_tensor_tensor(y[:, 1:643], u[:, 2:644], vcol(v0 + b * FCH + 4 * FCH, j), y[:, 1:643],
                                                            ALU.mult, ALU.add)
                            last.then_inc(S(f"f_conv{b}"), 1)
                        dve.wait_ge(S("f_silu"), c + 1)
                        dve.wait_ge(S("f_conv1"), 2 * c + 2)
                        if not (isinstance(j, int) and c == 0):
                            dve.wait_ge(S("g_lo_written"), c)
                        dve.tensor_tensor(GP[:, 1:643], SILU_A[:, 1:643], Y[1][:, 1:643], ALU.mult).then_inc(S("f_gated"), 1)
                    body(0)
                    with dve.Fori(1, FH) as j:
                        body(j)
                    n1 = n0 + 2 * FH
                    if half == 1:
                        dve.wait_ge(evac_v, before(n1, True))

                    def down(i):
                        for b in range(2):
                            slot = (n1 + b) % 2
                            m = 2 * i + b
                            dve.wait_ge(proj_done, n1 + b + 1 + 2 * i)
                            if half == 0:
                                dve.tensor_copy(halves(row(F, m)), pair(2 * slot)).then_inc(evac_v, 1)
                            else:
                                dve.tensor_tensor(halves(row(F, m)), pair(2 * slot), halves(row(F, m)), ALU.add
                                                  ).then_inc(evac_v, 1)
                    with dve.Fori(0, KD // 2) as i:
                        down(i)

            out_evac(N0_EVEN_OUT)
            post_norm("post00", 0, 0)
            pre_norm("pre01", 0, 1)
            ffn(0)
            post_norm("post01", 0, 1)
            pre_norm("pre10", 1, 0)

            sums("cq", 3)
            dve.wait_ge(*of("rstd", "cq", 1))
            for k in range(3):
                dve.scalar_tensor_tensor(CQ[:, k, :], CQ[:, k, :], VC[:, V_QN + k:V_QN + k + 1], RST[:, :], ALU.mult, ALU.mult
                                         ).then_inc(S("cq_scaled"), 1)
            for k in range(3):
                dve.wait_ge(S("cq_hi"), k + 1)
                dve.tensor_tensor(CQl[:, k, :], CQ[:, k, :], CQh[:, k, :].bitcast(F32), ALU.subtract).then_inc(S("cq_lo"), 1)
            sums("ckv", 2)
            dve.wait_ge(*of("rstd", "ckv", 1))
            for k in range(2):
                dve.scalar_tensor_tensor(CKV[:, k, PAST:KW], CKV[:, k, PAST:KW], VC[:, V_KVN + k:V_KVN + k + 1], RST[:, :],
                                         ALU.mult, ALU.mult).then_inc(S("ckv_scaled"), 1)
            for k in range(2):
                dve.wait_ge(S("ckv_hi"), k + 1)
                dve.tensor_tensor(CKl[:, k, :], CKV[:, k, :], CKh[:, k, :].bitcast(F32), ALU.subtract).then_inc(S("ckv_lo"), 1)
            dve.wait_ge(S("c_out_turned"), 1)
            dve.tensor_copy(CROW[:, :, :], bank(6, 256).rearrange("p (k c) -> p k c", c=P)).then_inc(S("c_out_rows"), 1)
            dve.tensor_copy(KROW[:, :], PS[:, 6 * 512 + 256:6 * 512 + 384]).then_inc(S("c_out_rows"), 1)
            step(rope(KPT[:, PAST + S0:PAST + S0 + SAMPLE], 7, S("k_swapped"), 1))
            for r in range(2):
                dve.memset(KPE[r][64 * (1 - r):64 * (1 - r) + 64, :], 0.0)
                last = dve.tensor_copy(KPE[r][64 * r:64 * r + 64, :], KPT[64 * r:64 * r + 64, :])
            last.then_inc(S("kpe_ready"), 1)

            def rope_q(i):
                step(rope(QPE[i % 2][:, S0:S0 + SAMPLE], 6, S("q_swapped"), i + 1), "q_roped")
            rope_q(0)

            def odd_lo(u):
                h, t = ODDU[u]
                dve.wait_ge(S("c_out_hi"), u + 1)
                dve.tensor_tensor(Hl[:, h, TILES[t]:TILES[t] + P], COUT, Hh[:, h, TILES[t]:TILES[t] + P].bitcast(F32),
                                  ALU.subtract).then_inc(S("c_out_lo"), 1)

            for u, (h, t) in enumerate(ODDU):
                s = u % 2
                w = P if t == 0 else 640
                dve.wait_ge(S("c_scores"), u + 1)
                dve.tensor_reduce(CSM[:, u:u + 1], PS[:, CSC:CSC + w], AX_X, ALU.max).then_inc(S("c_rowmax"), 1)
                dve.wait_ge(S("c_rowmax"), u + 1)
                dve.tensor_scalar(CSM[:, 64 + u:65 + u], CSM[:, u:u + 1], -(C_NOPE + C_ROPE) ** -0.5, None, ALU.mult
                                  ).then_inc(S("c_max"), 1)
                dve.wait_ge(S("c_exp"), u + 1)
                step(dve.reciprocal(CSM[:, 192 + u:193 + u], CSM[:, 128 + u:129 + u]))
                dve.tensor_scalar(CP[s][:, 0:w], CP[s][:, 0:w], CSM[:, 192 + u:193 + u], None, ALU.mult).then_inc(S("c_normed"), 1)
                if u >= 2:
                    odd_lo(u - 2)
                if h % 2 == 1 and t == 0 and h + 1 < C_HEADS:
                    rope_q((h + 1) // 2)
            odd_lo(len(ODDU) - 2)
            odd_lo(len(ODDU) - 1)

            out_evac(N0_ODD_OUT)
            post_norm("post10", 1, 0)
            pre_norm("pre11", 1, 1)
            ffn(1)
            post_norm("post11", 1, 1)
            for t in range(NT):
                dve.wait_ge(S("y_turned"), 2 * t + 2)
                dve.tensor_copy(XR[t][:, 512:1024], bank(7)).then_inc(S("y_rows_v"), 1)

        @block.tensor
        def _(pe):
            def split_mm(outs, w_of, x_of, ks):
                last = None
                for k in range(ks):
                    for p, (wi, xi) in enumerate(((0, 0), (0, 1), (1, 0))):
                        for i, out in enumerate(outs):
                            last = pe.matmul(out, w_of(k, wi), x_of(k, xi, i), start=(k == 0 and p == 0),
                                             stop=(k == ks - 1 and p == 2))
                return last

            def proj(n, x, slot=None, k=None, width=HW, free=None):
                slot = n % 2 if slot is None else slot
                k = BL[n][1] if k is None else k
                pe.wait_ge(w_lo, n + 1)
                if free is None:
                    free = [evacuated(n - 2)] if n >= 2 else []
                for sem, value in free:
                    pe.wait_ge(sem, value)
                w = (WH[slot], WL[slot])
                b = 2 * slot
                split_mm([bank(b, width), bank(b + 1, width)], lambda kk, i: w[i][:, kk, :],
                         lambda kk, i, hf: x[i][:, kk, hf * width:(hf + 1) * width], k).then_inc(proj_done, 1)

            def stat(sem, src, b=4):
                for hf in range(2):
                    last = pe.matmul(bank(b + hf, HW), ONES, src[:, hf * HW:(hf + 1) * HW], start=True, stop=True)
                last.then_inc(sem, 1)

            def norm_stat(tag):
                pe.wait_ge(*of("sum", tag, CHUNKS[tag]))
                stat(S("norm_stat"), ACC)

            def turn(out, src, rows=P):
                return pe.transpose(out, src, IDENT[0:rows, 0:rows])

            def mod_part(w, c0, n, b):
                for k in range(KD):
                    last = pe.matmul(bank(b, n, 2), SCX[:, k:16:8], w[:, k, c0:c0 + n], start=(k == 0), stop=(k == KD - 1))
                last.then_inc(S("mod_rows_done"), 1)

            def mod_turn(q, rows, n, b, c0):
                pe.wait_ge(S("mod_rows"), q + 1)
                for j in range(n):
                    last = turn(PS[:, b * 512 + c0 + 2 * j:b * 512 + c0 + 2 * j + 2], rows[0:2, P * j:P * j + P], 2)
                last.then_inc(S("mod_turned"), 1)

            pe.wait_ge(S("consts_landed"), 16)
            pe.wait_ge(S("vec_landed"), 16 * 12)
            for b, n in enumerate((122, 128, 128, 104)):
                turn(PS[:, 4 * 512 + 128 * b:4 * 512 + 128 * b + n], VR[b][0:n, :], n).then_inc(S("vec_turned"), 1)
            pe.wait_ge(S("x_landed"), 16 * NT)
            for t in range(NT):
                for part, sem in ((0, "x_evac_a"), (1, "x_evac_v")):
                    if t:
                        pe.wait_ge(S(sem), t)
                    for k in range(4):
                        last = turn(PS[:, (6 + part) * 512 + P * k:(6 + part) * 512 + P * k + P],
                                    XR[t][:, (4 * part + k) * P:(4 * part + k + 1) * P])
                    last.then_inc(S("x_turned"), 1)
            pe.wait_ge(S("silu_c"), 1)
            for q in range(4):
                pe.wait_ge(S(f"mod_landed{2 + q}"), 16)
                mod_part(MWS[q // 2], 512 * (q % 2), 512, q)
            for q in range(4):
                mod_turn(q, MROW0[:, 512 * q:512 * q + 512], 4, 5, 8 * q)
            H = (Hh, Hl)
            pe.wait_ge(S("mod_ready"), 1)
            norm_stat("pre00")
            pe.wait_ge(*of("rstd", "pre00", 1))
            pe.wait_ge(S("gap_zeroed_e"), 1)
            pe.wait_ge(*of("hl", "pre00", 2 * KD))
            for n in range(23):
                proj(n, H)

            for c in range(8):
                if c >= 2:
                    pe.wait_ge(*of("ln", "l2", c - 1))
                pe.wait_ge(*of("sq", "l2", c + 1))
                stat(S("norm_stat"), SQ[c % 2], 4 + 2 * (c % 2))
            pe.wait_ge(*evacuated(22))
            pe.wait_ge(*of("ln", "l2", 8))
            for t in range(NT):
                turn(PS[:, 6 * 512 + 16 * t:6 * 512 + 16 * t + 16], AB[0:16, TILES[t]:TILES[t] + P], 16).then_inc(S("ab_turned"), 1)
            pe.wait_ge(S("l2_done"), 8)
            pe.wait_ge(S("gate_z"), 1)
            for t in range(NT):
                for kind, sem in ((1, "k_tok"), (2, "v_tok")):
                    if t >= 2:
                        pe.wait_ge(S(sem), t - 1)
                    b = 3 + kind + 2 * (t % 2)
                    for h in range(4):
                        last = turn(PS[:, b * 512 + P * h:b * 512 + P * h + P], QKV[:, 4 * kind + h, TILES[t]:TILES[t] + P])
                    last.then_inc(S("kv_turned"), 1)
            pe.wait_ge(S("log_decay"), 1)
            pe.matmul(PS[:, 0:20], const(C_TRIU), gates(G)[:, :, 0, :], start=True, stop=True)
            pe.matmul(PS[:, 20:40], const(C_TRIL), gates(G)[:, :, 1, :], start=True, stop=True)
            pe.matmul(PS[:, 40:80], ONES, G[:, :], start=True, stop=True).then_inc(S("decay_cols"), 1)
            pe.wait_ge(S("gates_ready"), 1)
            pe.wait_ge(S("k_tok"), NT)
            pe.wait_ge(S("v_tok"), NT)
            pe.wait_ge(S("side_landed"), 64)

            def hb(b, h):
                return PS[:, b * 512 + P * h:b * 512 + P * h + P]

            for r in range(NT):
                n0 = LEVELS * r
                for c in range(2):
                    t = tile_of(r, c)
                    T0 = TILES[t]
                    if r > 0:
                        pe.wait_ge(*both("state_done", c, r))
                        pe.wait_ge(*both("o_done", c, r))
                    for h in range(4):
                        g0 = 8 * t + 4 * c + h
                        last = pe.matmul(hb(4 * c + 2, h), G[:, g0:g0 + 1].broadcast_to([P, P]),
                                         const((C_TRIU, C_TRIL)[c]), start=True, stop=True)
                    last.then_inc(S("gc_row"), 1)
                for c in range(2):
                    T0 = TILES[tile_of(r, c)]
                    for h in range(4):
                        kt = QKV[:, 4 + h, T0:T0 + P]
                        last = pe.matmul(hb(4 * c, h), kt, kt, start=True, stop=True)
                    last.then_inc(S("kk_done"), 1)
                for c in range(2):
                    T0 = TILES[tile_of(r, c)]
                    for h in range(4):
                        last = pe.matmul(hb(4 * c + 1, h), QKV[:, 4 + h, T0:T0 + P], QKV[:, h, T0:T0 + P], start=True, stop=True)
                    last.then_inc(S("kq_done"), 1)
                t0 = (LEVELS - 1) * r
                for lv in range(LEVELS):
                    n, s = n0 + lv, 1 << lv
                    for c in range(2):
                        pe.wait_ge(*both("level_ready", c, n + 1))
                        if lv > 0:
                            pe.wait_ge(*both("r_written", c, n))
                        if lv > 1:
                            pe.wait_ge(*both("z_written", c, t0 + lv - 1))
                        for h in range(4):
                            last = pe.matmul(hb(4 * c, h), BS[c][lv % 2][:, h, :], IDENT if lv == 0 else RS[c][:, h, :],
                                             start=True, stop=True)
                        last.then_inc(S("z_done"), 1)
                    if lv == 0:
                        continue
                    for c in range(2):
                        pe.wait_ge(*both("z_written", c, t0 + lv))
                        pe.wait_ge(*both("t_written", c, t0 + lv))
                        if lv == 1:
                            pe.wait_ge(*both("eg", c, r + 1))
                        for h in range(4):
                            last = pe.matmul(compact(4 * c + 3, s, h), TS[c][:, h, :], cols1(ZS[c], h, s, 1 - c), start=True, stop=True)
                        if lv < LEVELS - 1:
                            for h in range(4):
                                last = pe.matmul(compact(4 * c + 2, s, h), ZS[c][:, h, :], cols1(TS[c], h, s, c), start=True, stop=True)
                        last.then_inc(S("tr_done"), 1)
                for c in range(2):
                    pe.wait_ge(*both("r_written", c, n0 + LEVELS))
                    pe.wait_ge(*both("kb_ready", c, r + 1))
                    if r < NT - 1:
                        for h in range(4):
                            pe.matmul(hb(4 * c + 3, h), KBE[c][:, h, :], RS[c][:, h, :], start=True, stop=True)
                    pe.wait_ge(*both("vb_ready", c, r + 1))
                    for h in range(4):
                        last = pe.matmul(hb(4 * c + 2, h), RS[c][:, h, :], VB[c][:, h, :], start=True, stop=True)
                    last.then_inc(S("uw_done"), 1)
                if r < NT - 1:
                    for c in range(2):
                        pe.wait_ge(*both("w_written", c, r + 1))
                        for h in range(4):
                            last = pe.matmul(hb(4 * c, h), WT[c][:, h, :], ST[c][:, h, :], start=True, stop=True)
                        last.then_inc(S("ws_done"), 1)
                for c in range(2):
                    pe.wait_ge(*both("v_new", c, r + 1))
                    pe.wait_ge(*both("q_ready", c, r + 1))
                    pe.wait_ge(*both("kl_ready", c, r + 1))
                    pe.wait_ge(*both("qk_ready", c, r + 1))
                    for h in range(4):
                        if r < NT - 1:
                            pe.matmul(hb(4 * c + 1, h), ST[c][:, h, :], QG[c][:, h, :], start=True, stop=False)
                        pe.matmul(hb(4 * c + 1, h), VB[c][:, h, :], DQ[c][:, h, :], start=(r == NT - 1), stop=True)
                    for h in range(4):
                        last = pe.matmul(hb(4 * c + 2, h), KL[c][:, h, :], VB[c][:, h, :], start=True, stop=True)
                    last.then_inc(S("os_done"), 1)

            for c in range(2):
                pe.wait_ge(*both("o_done", c, NT))
            for h in range(4):
                if h >= 2:
                    pe.wait_ge(*of("ln", "on", h - 1))
                pe.wait_ge(*of("sq", "on", h + 1))
                stat(S("norm_stat"), SQ[h % 2], 4 + 2 * (h % 2))

            pe.wait_ge(*of("ln", "on", 4))
            for t in range(NT):
                if t >= 2:
                    pe.wait_ge(S("v_rows"), t - 1)
                turn(hb(6 + t % 2, 0), QA[:, 5, TILES[t]:TILES[t] + P]).then_inc(S("va_turned"), 1)
            pe.wait_ge(S("side_landed"), 16 * 7)
            turn(hb(5, 0), AKC[:, :])
            turn(hb(5, 1), QA[:, 4, P0:P0 + P]).then_inc(S("ka_turned"), 1)
            for c in range(5):
                if c == 4:
                    pe.wait_ge(S("a_roped"), 1)
                pe.matmul(bank(c % 4), const(C_SWAP), QA[:, c, S0:S0 + SAMPLE], start=True, stop=True).then_inc(S("a_swapped"), 1)
            pe.wait_ge(S("k_attn"), 1)
            pe.wait_ge(S("a_roped"), 5)
            pe.wait_ge(S("v_rows"), NT)

            def att_scores(u):
                t, h = ALLU[u]
                if u >= 2:
                    pe.wait_ge(S("a_rowmax"), u - 1)
                kt, q = AKT[h // 4], QA[:, h % 4, TILES[t]:TILES[t] + P]
                for c, kt_tile in att_tiles(t):
                    k0 = 0 if kt_tile == NT else PAST + TILES[kt_tile]
                    last = pe.matmul(PS[:, 512 * (u % 2) + c:512 * (u % 2) + c + P], q, kt[:, k0:k0 + P], start=True, stop=True)
                last.then_inc(S("a_scores"), 1)

            def att_turn(u):
                t, h = ALLU[u]
                pe.wait_ge(S("a_exp"), u + 1)
                if u >= 2:
                    pe.wait_ge(S("a_pt"), u - 1)
                for c, _ in att_tiles(t):
                    last = turn(PS[:, 1024 + 512 * (u % 2) + c:1024 + 512 * (u % 2) + c + P], PR[u % 2][:, c:c + P])
                last.then_inc(S("a_turned"), 1)

            def att_values(u):
                t, h = ALLU[u]
                i = ATT.index(t)
                pe.wait_ge(S("a_pt"), u + 1)
                if u >= 2:
                    pe.wait_ge(S("oa_scaled"), u - 1)
                out = PS[:, (4 + u % 2) * 512 + 64 * h:(4 + u % 2) * 512 + 64 * h + 64]
                tiles = att_tiles(t)
                for x, (c, kt_tile) in enumerate(tiles):
                    last = pe.matmul(out, PT[u % 2][:, c:c + P], AV[:, kt_tile, 64 * (h // 4):64 * (h // 4) + 64],
                                     start=(x == 0), stop=(x == len(tiles) - 1))
                last.then_inc(S("a_pv"), 1)

            def att_out(i):
                pe.wait_ge(S("oa_scaled"), 8 * (i + 1))
                if i:
                    pe.wait_ge(S("oa_lo"), i)
                for k in range(4):
                    last = turn(hb(6, k), OA[i % 2][:, P * k:P * k + P])
                last.then_inc(S("oa_turned"), 1)

            for u in range(len(ALLU) + 2):
                if u < len(ALLU):
                    att_scores(u)
                if 1 <= u <= len(ALLU):
                    att_turn(u - 1)
                if u >= 2:
                    att_values(u - 2)
                if u % 8 == 3 and u > 8:
                    att_out(u // 8 - 1)
                if 1 <= u <= 40:
                    mod_turn(4 + u - 1, MROW[(u - 1) % 2], 2, 7, 352 + 4 * (u - 1))
                if u < 40:
                    pe.wait_ge(S(f"mod_landed{u % 2}"), 16 * (u // 2 + 1))
                    mod_part(MW[u % 2], 0, 2 * P, 7)
            att_out(NT - 1)
            pe.wait_ge(S("oa_hi"), NT)
            pe.wait_ge(S("oa_lo"), NT)
            pe.wait_ge(S("on_lo"), 1)
            pe.wait_ge(S("o_attn_gaps"), 1)
            for m in range(8):
                proj(N0_EVEN_OUT + m, H)

            def ffn(l, tag):
                pe.wait_ge(S(f"gap_zeroed{l}"), 1)
                pe.wait_ge(S(f"g_edges{l}"), 1)
                pe.wait_ge(*of("hl", tag, 2 * KD))
                for half in range(2):
                    n0 = N0_FFN[l] + half * (2 * FH + KD)
                    with pe.Fori(0, FH) as j:
                        for b in range(2):
                            proj(n0 + b + 2 * j, H, slot=(n0 + b) % 2, k=KD,
                                 free=[(evac_v, before(n0, True) - 1 + b), (evac_a, before(n0, False) - 1 + b + 2 * j)])
                    pe.wait_ge(S("g_lo_written"), FH * (2 * l + half + 1))
                    n1 = n0 + 2 * FH
                    with pe.Fori(0, KD // 2) as i:
                        for b in range(2):
                            proj(n1 + b + 2 * i, (Gh, Gl), slot=(n1 + b) % 2, k=FH,
                                 free=[(evac_a, before(n1, False) - 1 + b), (evac_v, before(n1, True) - 1 + b + 2 * i)])

            norm_stat("post00")
            norm_stat("pre01")
            ffn(0, "pre01")
            norm_stat("post01")
            norm_stat("pre10")

            pe.wait_ge(S("side_landed"), 16 * 10)
            for k in range(2):
                turn(hb(6, k), CROW[:, k, :])
            turn(hb(6, 2), KROW[:, :]).then_inc(S("c_ctx_turned"), 1)
            pe.wait_ge(*of("hl", "pre10", 2 * KD))
            for m in range(6):
                proj(N0_ODD_IN + m, H)
                if m == 4:
                    norm_stat("cq")
            norm_stat("ckv")
            pe.wait_ge(*evacuated(N0_ODD_IN + 5))
            pe.matmul(bank(7), const(C_SWAP), KPT[:, PAST + S0:PAST + S0 + SAMPLE], start=True, stop=True).then_inc(S("k_swapped"), 1)
            pe.wait_ge(S("c_ctx"), 2)
            pe.wait_ge(S("ckv_scaled"), 2)
            for k in range(2):
                turn(hb(6, k), CKV[:, k, PAST + P0:PAST + P0 + P])
            turn(hb(6, 2), KPT[:, PAST + P0:PAST + P0 + P]).then_inc(S("c_out_turned"), 1)

            def head_proj(h):
                nr, nq, nk, nv = odd_blocks(h)
                if h == 0:
                    pe.wait_ge(S("cq_lo"), 3)
                if h % 2 == 0:
                    proj(nr, (CQh, CQl))
                proj(nq, (CQh, CQl))
                if h == 0:
                    pe.wait_ge(S("ckv_lo"), 2)
                proj(nk, (CKh, CKl), width=KW // 2)
                pe.wait_ge(w_lo, nv + 1)
                pe.wait_ge(*evacuated(nv - 2))
                slot = nv % 2
                c = (CKh, CKl)
                for kt_tile in range(NT + 1):
                    k0 = 0 if kt_tile == NT else PAST + TILES[kt_tile]
                    last = split_mm([PS[:, 1024 * slot + P * kt_tile:1024 * slot + P * kt_tile + P]],
                                    lambda kk, i: c[i][:, kk, k0:k0 + P], lambda kk, i, _: (WH, WL)[i][slot][:, kk, :], 2)
                last.then_inc(proj_done, 1)

            def rope_swap(i):
                nr = odd_blocks(2 * i)[0]
                pe.wait_ge(*evacuated(nr))
                if i == 0:
                    pe.wait_ge(S("c_out_rows"), 2)
                else:
                    pe.wait_ge(S("c_pt"), 10 * i - 1)
                pe.matmul(bank(6), const(C_SWAP), QPE[i % 2][:, S0:S0 + SAMPLE], start=True, stop=True).then_inc(S("q_swapped"), 1)

            def c_scores(u):
                h, t = ODDU[u]
                if u:
                    pe.wait_ge(S("c_exp"), u)
                if u % 5 == 0:
                    pe.wait_ge(*evacuated(odd_blocks(h)[3]))
                    if h % 2 == 0:
                        pe.wait_ge(S("q_roped"), h // 2 + 1)
                q, qr = QN[h % 2][:, TILES[t]:TILES[t] + P], QPE[h // 2 % 2][:, TILES[t]:TILES[t] + P]
                areas = [(CSC, PAST + P0, P)] if t == 0 else [(CSC, PAST + S0, SAMPLE), (CSC + 512, 0, PAST)]
                for c0, k0, w in areas:
                    pe.matmul(PS[:, c0:c0 + w], q, KN[h % 2][:, k0:k0 + w], start=True, stop=False)
                    last = pe.matmul(PS[:, c0:c0 + w], qr, KPE[h % 2][:, k0:k0 + w], start=False, stop=True)
                last.then_inc(S("c_scores"), 1)

            def c_turn(u):
                h, t = ODDU[u]
                pe.wait_ge(S("c_normed"), u + 1)
                if u >= 1:
                    pe.wait_ge(S("c_pt"), u)
                if u >= 2:
                    pe.wait_ge(S("c_out_lo"), u - 1)
                if u % 10 == 9 and u < len(ODDU) - 1:
                    pe.wait_ge(S("q_roped"), (u + 1) // 10 + 1)
                for x in range(1 if t == 0 else 5):
                    last = turn(PS[:, CTP + P * x:CTP + P * x + P], CP[u % 2][:, P * x:P * x + P])
                last.then_inc(S("c_turned"), 1)

            def c_values(u, ahead):
                h, t = ODDU[u]
                pe.wait_ge(S("c_pt"), u + 1)
                n7 = sum(1 for hh, tt in ODDU[0:ahead] if tt != 0)
                pe.wait_ge(S("c_pt7"), n7)
                if u >= 1:
                    pe.wait_ge(S("c_out_lo"), u)
                tiles = [(0, 0)] if t == 0 else [(x, 1 + x) for x in range(4)] + [(4, NT)]
                for x, (c, kt_tile) in enumerate(tiles):
                    last = pe.matmul(COUT, VO[h % 2][:, kt_tile, :], CPT[u % 2][:, P * c:P * c + P], start=(x == 0),
                                     stop=(x == len(tiles) - 1))
                last.then_inc(S("c_pv"), 1)

            head_proj(0)
            rope_swap(0)
            pe.wait_ge(S("kpe_ready"), 1)
            for u in range(len(ODDU) + 2):
                if u < len(ODDU):
                    c_scores(u)
                if 1 <= u <= len(ODDU):
                    c_turn(u - 1)
                if u >= 2:
                    c_values(u - 2, min(u, len(ODDU)))
                if u % 5 == 1 and u // 5 + 1 < C_HEADS:
                    head_proj(u // 5 + 1)
                if u % 10 == 9 and u < 39:
                    rope_swap((u + 1) // 10)
            pe.wait_ge(S("c_out_lo"), len(ODDU))
            for m in range(8):
                proj(N0_ODD_OUT + m, H)
            norm_stat("post10")
            norm_stat("pre11")
            ffn(1, "pre11")
            norm_stat("post11")
            pe.wait_ge(*of("x", "post11", 2 * KD))
            for t in range(NT):
                for part, sem in ((0, "y_rows_a"), (1, "y_rows_v")):
                    if t:
                        pe.wait_ge(S(sem), t)
                    for k in range(4):
                        last = turn(hb(6 + part, k), X[:, 4 * part + k, TILES[t]:TILES[t] + P])
                    last.then_inc(S("y_turned"), 1)


_INS = ["x_prompt", "x_sample", "cache_attn_k", "cache_attn_v", "state_delta_fwd", "state_delta_bwd",
        "cache_mla_ckv", "cache_mla_kpe", "c", "c_ctx", "w_mod", "b_mod", "norm_pre", "norm_post",
        "ffn_w_up", "ffn_conv", "ffn_w_down", "ev_w_in", "ev_conv", "ev_a_log", "ev_dt_bias", "ev_sink",
        "ev_out_norm", "ev_w_out", "od_w_in", "od_q_norm", "od_kv_norm", "od_w_q_up", "od_w_kv_up", "od_w_out"]
_OUTS = [(1, PROMPT, D), (1, SAMPLE, D), (1, 1, PROMPT, 2, A_HD), (1, 1, PROMPT, 2, A_HD),
         (1, 1, B_HEADS, P, P), (1, 1, B_HEADS, P, P), (1, 1, PROMPT, C_KV), (1, 1, PROMPT, C_ROPE)]


def kernel(**inputs):
    import concourse.bacc as bacc
    from concourse.bass_utils import run_bass_kernel_spmd

    nc = bacc.Bacc("TRN2", target_bir_lowering=False, num_devices=1)
    arrays = {name: np.ascontiguousarray(inputs[name]) for name in _INS}
    arrays["consts"] = shape_constants()
    ins = {name: nc.dram_tensor(f"in_{name}", v.shape, mybir.dt.from_np(v.dtype), kind="ExternalInput").ap()
           for name, v in arrays.items()}
    outs = [nc.dram_tensor(f"out_{i}", shape, F32, kind="ExternalOutput").ap() for i, shape in enumerate(_OUTS)]
    build(nc, ins, outs)
    r = run_bass_kernel_spmd(nc, [{f"in_{name}": v for name, v in arrays.items()}], core_ids=[0])
    return tuple(r.results[0][f"out_{i}"] for i in range(len(_OUTS)))
```

```python
from contextlib import ExitStack

import numpy as np
import concourse.bass as bass
from concourse import mybir

ALU = mybir.AluOpType
ACT = mybir.ActivationFunctionType
AX_X = mybir.AxisListType.X
F32 = mybir.dt.float32
F32R = mybir.dt.float32r

P = 128
D = 1024
KD = D // P
PROMPT, SAMPLE, PAST = 128, 512, 128
P0, S0 = 1, 130
TW = 644
HW = TW // 2
CONDS = ((0, P0, P0 + PROMPT), (1, S0, S0 + SAMPLE))
TILES = [P0] + [S0 + P * t for t in range(SAMPLE // P)]
NT = len(TILES)
GRID_W = 64
A_HEADS, A_HD = 8, 64
A_Q, A_KV = 512, 128
B_HEADS = 4
C_HEADS, C_Q, C_KV, C_NOPE, C_ROPE, C_V = 8, 384, 256, 128, 64, 128
D_FF = 2816
FCH = D_FF // P
FH = FCH // 2
EPS = 1e-6
BIG = 1e30
LEVELS = 7
KMAX = FH

V_C, V_PRE, V_POST, V_ECONV, V_QN, V_KVN, V_ON = 0, 16, 48, 80, 116, 119, 121
V_FCONV, V_BMOD = 128, 392
(C_ID, C_ONES, C_SWAP, C_TRIU, C_TRIL) = range(5)
C_AMASK, C_COS, C_SIN = 5, 9, 13
C_PAIR = 17
C_LEVEL = 18
N_CONST = C_LEVEL + 2 * LEVELS


def shape_constants():
    i = np.arange(P)
    row, col = i[:, None], i[None, :]
    out = np.zeros((P, N_CONST, P), np.float32)
    out[:, C_ID] = row == col
    out[:, C_ONES] = 1.0
    out[:, C_SWAP] = row == (col ^ 32)
    out[0:4, C_PAIR, 0:2] = row[0:4] % 2 == col[:, 0:2]
    out[:, C_TRIU] = row <= col
    out[:, C_TRIL] = row >= col
    out[:, C_AMASK] = np.where(col >= row, 0.0, -BIG)
    out[:, C_AMASK + 3] = np.where(col <= row, 0.0, -BIG)
    t = np.arange(SAMPLE)
    n_freq = A_HD // 4
    inv = (np.float32(10000.0) ** (-np.arange(n_freq, dtype=np.float32) / np.float32(n_freq))).astype(np.float32)
    ang = np.concatenate([(t // GRID_W).astype(np.float32)[:, None] * inv,
                          (t % GRID_W).astype(np.float32)[:, None] * inv], axis=-1)
    cos, sin = np.cos(ang), np.sin(ang)
    sign = np.where((i // 32) % 2 == 0, -1.0, 1.0).astype(np.float32)
    out[:, C_COS:C_COS + 4] = cos[:, i % 32].T.reshape(P, 4, P)
    out[:, C_SIN:C_SIN + 4] = (sin[:, i % 32].T * sign[:, None]).reshape(P, 4, P)
    for lv in range(LEVELS):
        s = 1 << lv
        low = ((row // s) % 2 == 1) & (col // s == row // s - 1)
        out[:, C_LEVEL + lv] = -low.astype(np.float32)
        out[:, C_LEVEL + LEVELS + lv] = -low.T.astype(np.float32)
    return out.reshape(P, N_CONST * P)


def block_table():
    blocks = [("even_in", KD)] * 23 + [("even_out", KD)] * 8
    blocks += ([("up", KD)] * (2 * FH) + [("down", FH)] * KD) * 2
    blocks += [("odd_in", KD)] * 6
    for h in range(C_HEADS):
        if h % 2 == 0:
            blocks.append(("q_rope", C_Q // P))
        blocks += [("q", C_Q // P), ("k", C_KV // P), ("v", C_KV // P)]
    blocks += [("odd_out", KD)] * 8
    blocks += ([("up", KD)] * (2 * FH) + [("down", FH)] * KD) * 2
    return blocks


def build(nc, a, outs):
    BL = block_table()
    N0_EVEN_IN, N0_EVEN_OUT, N0_FFN0 = 0, 23, 31
    N0_ODD_IN = N0_FFN0 + 2 * (2 * FH + KD)
    N0_ODD_H = N0_ODD_IN + 6
    N0_ODD_OUT = N0_ODD_H + 28
    N0_FFN = (N0_FFN0, N0_ODD_OUT + 8)
    assert len(BL) == N0_FFN[1] + 2 * (2 * FH + KD)

    y_prompt, y_sample, new_k, new_v, new_fwd, new_bwd, new_ckv, new_kpe = outs

    sems = {}
    stack = ExitStack()

    def S(name):
        if name not in sems:
            sems[name] = stack.enter_context(nc.semaphore(name))
        return sems[name]

    NORMS = (("pre00", KD, 1), ("l2", 8, 8), ("on", 4, 4), ("post00", KD, 1), ("pre01", KD, 1), ("post01", KD, 1),
             ("pre10", KD, 1), ("cq", C_Q // P, 1), ("ckv", C_KV // P, 1), ("post10", KD, 1), ("pre11", KD, 1),
             ("post11", KD, 1))
    CHUNKS = {name: k for name, k, _ in NORMS}

    def of(kind, tag, n):
        before = NORMS[:[name for name, _, _ in NORMS].index(tag)]
        if kind in ("stat", "ln", "rstd"):
            base = sum(s for name, _, s in before if kind != "stat" or not name.startswith("pre"))
        elif kind == "sq":
            base = sum(k for _, k, _ in before)
        elif kind == "sum":
            base = sum(k for name, k, s in before if s == 1 and not name.startswith("pre"))
        elif kind in EACH:
            base = EACH[kind][1] * sum(name.startswith(EACH[kind][0]) for name, _, _ in before)
        return S(f"norm_{kind}"), base + n

    POOL_X = (2, 5)
    EACH = {"scaled": ("pre", 2 * KD), "hh": ("pre", 2 * KD), "shifted": ("pre", KD), "part": ("pre", KD), "hl_v": ("pre", KD), "hl_p": ("pre", KD),
            "fs": ("post", KD), "delta_v": ("post", KD - 2), "x_v": ("post", KD - 2), "delta_p": ("post", 2), "x_p": ("post", 2)}

    def x_ready(tag, k):
        by_pool = k in POOL_X
        return of("x_p" if by_pool else "x_v", tag, sum((j in POOL_X) == by_pool for j in range(k + 1)))

    def h_ready(tag, k):
        return of("hl_p" if k % 2 else "hl_v", tag, 2 * (k // 2) + 2)

    FILLED = ("eps", "h_gaps_e", "qkv_edges", "od_gaps", "o_attn_gaps", "h_gaps0", "g_edges0", "h_gaps1", "g_edges1")

    def filled(name):
        return S("gpsimd_filled"), FILLED.index(name) + 1

    def both(kind, c, n):
        return S(kind), 2 * n - 1 + c

    BASE = 16512
    at = [0]

    def al(n):
        return -(-n // 8) * 8

    def region(n):
        o = at[0]
        at[0] += al(n)
        return o

    def place(name, shape, off, dt=F32):
        return nc.alloc_sbuf_tensor_at(name, [P] + shape, dt, offset=BASE + 4 * off)

    R_X = region(KD * TW)
    R_H = region(2 * KD * TW)
    R_G = region(2 * al(FH * TW))
    R_F = region(KD * TW)
    R_RAW = region(2 * KMAX * P)
    R_W = region(4 * KMAX * P)
    R_CONST = region(17 * P)
    R_DC = region((N_CONST - 17) * P)
    R_VC = region(512)
    R_MOD = region(2 * 96 + 4 * 16 + 4 * 16)
    R_EPS = region(8)
    R_SC = region(48)
    R_SCS = region(KD * 4 + P - 4)
    R_T = region(6 * al(TW))
    assert BASE + 4 * at[0] <= nc.sbuf_usable_end, (BASE + 4 * at[0], nc.sbuf_usable_end)

    X = place("x_t", [KD, TW], R_X)
    Hh = place("h_hi", [KD, TW], R_H, F32R)
    Hl = place("h_lo", [KD, TW], R_H + KD * TW, F32R)
    Gh = place("g_hi", [FH, TW], R_G, F32R)
    Gl = place("g_lo", [FH, TW], R_G + al(FH * TW), F32R)
    F = place("f_t", [KD, TW], R_F)
    RAW = [place(f"w_raw{s}", [KMAX, P], R_RAW + s * KMAX * P) for s in range(2)]
    WH = [place(f"w_hi{s}", [KMAX, P], R_W + s * KMAX * P, F32R) for s in range(2)]
    WL = [place(f"w_lo{s}", [KMAX, P], R_W + (2 + s) * KMAX * P, F32R) for s in range(2)]
    CT = place("consts", [N_CONST, P], R_CONST)
    VC = place("vec_cols", [512], R_VC)
    MOD = [place(f"mod{l}", [96], R_MOD + 96 * l) for l in range(2)]
    PA = [[place(f"pre_gain{l}{i}", [16], R_MOD + 192 + 16 * (2 * l + i)) for i in range(2)] for l in range(2)]
    PG = [[place(f"post_gain{l}{i}", [16], R_MOD + 256 + 16 * (2 * l + i)) for i in range(2)] for l in range(2)]

    EPSC = place("eps", [8], R_EPS)

    def tslot(name, i, shape=None):
        return place(name, shape or [TW], R_T + i * al(TW))

    SQ = [tslot("sq0", 0), tslot("sq1", 1)]
    ACC = tslot("sq_sum", 2)
    RST = tslot("rstd", 3)
    TN = [tslot("scaled0", 4), tslot("scaled1", 5), tslot("scaled2", 2)]
    U = [tslot("u0", 0), tslot("u1", 1)]
    Y = [tslot("conv0", 2), tslot("conv1", 3)]
    SILU_A = tslot("silu_a", 4)
    GP = tslot("gated", 5)
    MWS = [place("w_shift", [KD, D], R_H), place("w_scale", [KD, D], R_G + NT * D)]
    XR = [place(f"x_rows{t}", [D], R_G + D * t) for t in range(NT)]
    MROW0 = place("mod_first_rows", [2 * D], R_T + 1024)
    VR = [place(f"vec_rows{b}", [P], R_T + P * b) for b in range(4)]
    SCX = place("silu_c", [16], R_SC)
    SCS = place("silu_c_split", [KD * 4 + P - 4], R_SCS, F32R)
    SCE = place("silu_e", [16], R_SC + 16)
    SCR = place("silu_r", [16], R_SC + 32)
    QA = place("qa_ka_va", [6, TW], R_G)
    QKV = place("qkv_b", [12, TW], R_G + 6 * TW)
    SG = place("silu_gate", [4, TW], R_G + 18 * TW)
    AB = tslot("ab_rows", 4)
    KTOK = place("k_tok", [NT, 4, P], R_F)
    VTOK = place("v_tok", [NT, 4, P], R_F + NT * 4 * P)
    gate_at = [R_T + 5 * al(TW)]

    def gate(name, n):
        o = gate_at[0]
        gate_at[0] += al(n)
        assert gate_at[0] <= R_T + 6 * al(TW)
        return place(name, [n], o)

    ABC = gate("ab_cols", NT * 16)
    ZG = gate("gate_z", NT * 8)
    ZA = gate("gate_t", NT * 8)
    G = gate("log_decay", NT * 8)
    BETA = gate("beta", NT * 8)
    GC = gate("decay_sum", NT * 8)
    GT = gate("decay_total", NT * 8)
    EB = gate("beta_decay", NT * 8)
    EK = gate("key_decay", NT * 8)
    DTB = gate("dt_bias_b", 8)
    EAL = gate("neg_exp_a_log", 8)
    ELC = [gate(f"tile_decay{c}", 4) for c in range(2)]

    def hslot(name, i, dt=F32):
        return place(name, [4, P], R_H + 512 * i, dt)

    DA = [hslot(f"d_a{c}", 9 * c + 0) for c in range(2)]
    DQ = [hslot(f"d_qk{c}", 9 * c + 1) for c in range(2)]
    QG = [hslot(f"q_decay{c}", 9 * c + 2) for c in range(2)]
    BS = [[hslot(f"level_b{c}{x}", 9 * c + (3, 7)[x]) for x in range(2)] for c in range(2)]
    VB = [hslot(f"v_beta{c}", 9 * c + 3) for c in range(2)]
    KBE = [hslot(f"k_beta_decay{c}", 9 * c + 7) for c in range(2)]
    ZS = [hslot(f"level_z{c}", 9 * c + 4) for c in range(2)]
    TS = [hslot(f"t_inv{c}", 9 * c + 5) for c in range(2)]
    UU = [hslot(f"u_tok{c}", 9 * c + 5) for c in range(2)]
    RS = [hslot(f"r_inv{c}", 9 * c + 6) for c in range(2)]
    WT = [hslot(f"w_t{c}", 9 * c + 6) for c in range(2)]
    KL = [hslot(f"k_state{c}", 9 * c + 8) for c in range(2)]
    ST = [hslot(f"state{c}", 18 + c) for c in range(2)]
    OD = place("o_delta", [4, TW], R_G + 14 * TW)
    def mod_slot(name, s, dt=F32):
        return place(name, [KD, 2 * P], R_G + 6 * TW + s * 2 * KD * P, dt)

    MW = [mod_slot(f"w_mod_raw{s}", s) for s in range(3)]
    ML = [mod_slot(f"w_mod_lo{s}", s, F32R) for s in range(3)]
    MH = [mod_slot(f"w_mod_hi{s}", 3 + s, F32R) for s in range(2)]
    MPARTS, MK = 40, 5
    MROW = [place(f"mod_rows{s}", [2 * P], R_T + 3328 + 2 * P * s) for s in range(2)]
    SM = [place(f"scores{s}", [512], R_T + 512 * s) for s in range(2)]
    PR = [place(f"probs{s}", [512], R_T + 1024 + 512 * s) for s in range(2)]
    PT = [place(f"probs_t{s}", [512], R_T + 2048 + 512 * s) for s in range(2)]
    ASM = place("attn_small", [256], R_T + 3072)
    OA = [place(f"o_attn{s}", [512], R_F + 512 * s) for s in range(2)]
    KW = PAST + TW
    AKT = [place(f"k_attn{g}", [KW], R_F + 1024 + g * al(KW)) for g in range(2)]
    AV = place("v_attn_tok", [NT + 1, P], R_F + 1024 + 2 * al(KW))
    AKC = place("k_ctx_rows", [P], R_F + 1024 + 2 * al(KW) + (NT + 1) * P)
    AKO = place("k_out_rows", [P], R_F + 1024 + 2 * al(KW) + (NT + 2) * P)
    SNK = place("sink_b", [8], R_F + 1024 + 2 * al(KW) + (NT + 3) * P)
    SNK8 = place("sink_scaled", [8], R_F + 1024 + 2 * al(KW) + (NT + 3) * P + 8)
    g = [R_G]

    def gslot(name, shape, dt=F32):
        o = g[0]
        g[0] += al(int(np.prod(shape)))
        assert g[0] <= R_G + 2 * al(FH * TW) + KD * TW
        return place(name, shape, o, dt)

    CQ = gslot("cq", [3, TW])
    CKV = gslot("ckv", [2, KW])
    CQh = gslot("cq_hi", [3, TW], F32R)
    CQl = gslot("cq_lo", [3, TW], F32R)
    CKh = gslot("ckv_hi", [2, KW], F32R)
    CKl = gslot("ckv_lo", [2, KW], F32R)
    KPT = gslot("kpe_two", [KW])
    KPE = [gslot(f"kpe{r}", [KW]) for r in range(2)]
    QPE = [gslot(f"q_rope{s}", [TW]) for s in range(2)]
    QN = [gslot(f"q_nope{s}", [TW]) for s in range(2)]
    KN = [gslot(f"k_nope{s}", [KW]) for s in range(2)]
    VO = [gslot(f"v_head{s}", [NT + 1, P]) for s in range(2)]
    CROW = gslot("ckv_rows", [2, P])
    KROW = gslot("kpe_rows", [P])
    CP = [place(f"c_probs{s}", [640], R_T + 640 * s) for s in range(2)]
    CPT = [place(f"c_probs_t{s}", [640], R_T + 1280 + 640 * s) for s in range(2)]
    CSM = place("c_small", [256], R_T + 2560)
    ROT = place("rotated", [512], R_T + 2816)

    PS = stack.enter_context(nc.psum_tensor("ps", [P, 8 * 512], F32))

    def bank(b, n=512, p=P):
        return PS[0:p, b * 512:b * 512 + n]

    def pair(b, n=HW, p=P):
        return PS[0:p, b * 512:(b + 2) * 512].rearrange("p (h c) -> p h c", c=512)[:, :, 0:n]

    def halves(ap):
        return ap.rearrange("p (h c) -> p h c", h=2)

    def const(c, n=1):
        return CT[:, c, :] if n == 1 else CT[:, c:c + n, :]

    IDENT, ONES = const(C_ID), const(C_ONES)

    w_hi, w_lo, proj_done = S("w_hi_written"), S("w_lo_written"), S("proj_done")
    evac_a, evac_v = S("evacuated_a"), S("evacuated_v")

    def before(n, by_vector):
        return sum((name in ("even_out", "down", "odd_out")) == by_vector for name, _ in BL[:n])

    def evacuated(n):
        by_vector = before(n + 1, True) > before(n, True)
        return (evac_v if by_vector else evac_a), before(n + 1, by_vector)
    w_landed = [S("w_landed0"), S("w_landed1")]

    up_v = [a["ffn_w_up"][l].rearrange("(k p) f -> p k f", p=P) for l in range(2)]
    down_v = [a["ffn_w_down"][l].rearrange("(k p) n -> p k n", p=P) for l in range(2)]
    ein_v = a["ev_w_in"][0].rearrange("(k p) f -> p k f", p=P)
    eout_v = a["ev_w_out"][0].rearrange("(k p) n -> p k n", p=P)
    oin_v = a["od_w_in"][0].rearrange("(k p) f -> p k f", p=P)
    oout_v = a["od_w_out"][0].rearrange("(k p) n -> p k n", p=P)
    qup_v = a["od_w_q_up"][0].rearrange("(k p) f -> p k f", p=P)
    kvup_v = a["od_w_kv_up"][0].rearrange("(k p) f -> p k f", p=P)

    in_two = set(range(4)) | {N0_ODD_IN + 5} | {N0_ODD_H + 7 * h for h in range(C_HEADS // 2)}

    def landed_by(n):
        return 16 * sum(2 if m in in_two else 1 for m in range(n % 2, n + 1, 2))

    def odd_blocks(h):
        n = N0_ODD_H + 7 * (h // 2)
        return (n, n + 1, n + 2, n + 3) if h % 2 == 0 else (n, n + 4, n + 5, n + 6)

    def tile_of(r, c):
        return 0 if r == NT - 1 else (1 + r if c == 0 else NT - 1 - r)

    ATT = list(range(1, NT)) + [0]

    def att_local(t):
        return (128, 256) if t == 0 else (128 if t == 1 else 0, 384 if t == NT - 1 else 512)

    def att_tiles(t):
        if t == 0:
            return [(128, 0)]
        return ([(0, t - 1)] if t > 1 else []) + [(128, t), (256, NT)] + ([(384, t + 1)] if t < NT - 1 else [])

    def cols(m, s, odd):
        return m[:, :, :].rearrange("p h (b two s) -> p (h b) two s", two=2, s=s)[:, :, odd, :]

    def cols1(m, h, s, odd):
        return m[:, h, :].rearrange("p (b two s) -> p b two s", two=2, s=s)[:, :, odd, :]

    def compact(b, s, h=None):
        ap = bank(b, 256) if h is None else PS[:, b * 512 + 64 * h:b * 512 + 64 * h + 64]
        return ap.rearrange("p (b s) -> p b s", s=s)

    def per_head(m, g0):
        return m[:, g0:g0 + 4].unsqueeze(2).broadcast_to([P, 4, P])

    ALLU = [(t, h) for t in ATT for h in range(A_HEADS)]
    ODDU = [(h, t) for h in range(C_HEADS) for t in ATT]

    def row(m, j):
        return m[:, j, :] if isinstance(j, int) else m[:, bass.ds(j, 1), :].rearrange("p o c -> p (o c)")

    def vcol(base, j):
        return VC[:, base + j:base + j + 1] if isinstance(j, int) else VC[:, bass.ds(j + base, 1)]

    def q4(ap):
        return ap.rearrange("p (h c) -> p h c", c=P)

    def gates(t):
        return t[:, :].rearrange("p (t d h) -> p t d h", d=2, h=4)

    def abv(kind):
        return ABC[:, :].rearrange("p (t d k h) -> p t d k h", d=2, k=2, h=4)[:, :, :, kind, :]

    def att_copy_a(act, u):
        t, h = ALLU[u]
        c0, c1 = att_local(t)
        act.wait_ge(S("a_turned"), u + 1)
        if u >= 2:
            act.wait_ge(S("a_pv"), u - 1)
        act.activation(PT[u % 2][:, c0:c1], PS[:, 1024 + 512 * (u % 2) + c0:1024 + 512 * (u % 2) + c1], ACT.Copy
                       ).then_inc(S("a_pt"), 1)

    CSC, CTP, COUT = 4 * 512, 6 * 512, PS[:, 7 * 512 + 256:7 * 512 + 384]

    def odd_out_hi(act, u):
        h, t = ODDU[u]
        act.wait_ge(S("c_pv"), u + 1)
        act.activation(Hh[:, h, TILES[t]:TILES[t] + P], COUT, ACT.Copy).then_inc(S("c_out_hi"), 1)

    with stack:
        block = stack.enter_context(nc.Block())

        @block.sync
        def _(sp):
            def raw_free(n):
                if not isinstance(n, int) or n >= 2:
                    sp.wait_ge(w_lo, n - 1)

            def load(n, src, slot=None, k=None):
                slot = n % 2 if slot is None else slot
                k = BL[n][1] if k is None else k
                raw_free(n)
                sp.dma_start(RAW[slot][:, 0:k, 0:src.shape[-1]], src).then_inc(w_landed[slot], 16)

            def load_two(n, srcs):
                raw_free(n)
                for r in range(2):
                    sp.dma_start(RAW[n % 2][:, 0:BL[n][1], 64 * r:64 * r + 64], srcs[r]).then_inc(w_landed[n % 2], 16)

            def rows(dst, r0, src):
                sp.dma_start(dst[r0:r0 + src.shape[0], :], src).then_inc(S("vec_landed"), 16)

            consts = a["consts"].rearrange("p (c n) -> p c n", n=P)
            sp.dma_start(CT[:, 0:C_LEVEL, :], consts[:, 0:C_LEVEL, :]).then_inc(S("consts_landed"), 16)
            rows(VR[0], V_C, a["c_ctx"].rearrange("(k p) -> k p", p=P))
            rows(VR[0], V_C + 8, a["c"].rearrange("b (k p) -> (b k) p", p=P))
            rows(VR[0], V_PRE, a["norm_pre"].rearrange("l i (k p) -> (l i k) p", p=P))
            rows(VR[0], V_POST, a["norm_post"].rearrange("l i (k p) -> (l i k) p", p=P))
            rows(VR[0], V_ECONV, a["ev_conv"].rearrange("j t (k p) -> (j t k) p", p=P))
            rows(VR[0], V_QN, a["od_q_norm"].rearrange("j (k p) -> (j k) p", p=P))
            rows(VR[0], V_KVN, a["od_kv_norm"].rearrange("j (k p) -> (j k) p", p=P))
            rows(VR[0], V_ON, a["ev_out_norm"])
            fc = a["ffn_conv"].rearrange("l t (m p) -> (l t m) p", p=P)
            rows(VR[1], 0, fc[0:128, :])
            rows(VR[2], 0, fc[128:256, :])
            rows(VR[3], 0, fc[256:264, :])
            rows(VR[3], 8, a["b_mod"].rearrange("l (m p) -> (l m) p", p=P))
            for t in range(NT):
                src = a["x_prompt"][0] if t == 0 else a["x_sample"][0, (t - 1) * P:t * P, :]
                sp.dma_start(XR[t][:, :], src).then_inc(S("x_landed"), 16)
            wm = [a["w_mod"][l].rearrange("(k p) m -> p k m", p=P) for l in range(2)]
            for part in range(2):
                for q in range(2):
                    m0 = part * D + q * D // 2
                    sp.dma_start(MWS[part][:, :, q * D // 2:(q + 1) * D // 2], wm[0][:, :, m0:m0 + D // 2]
                                 ).then_inc(S(f"mod_first_landed{2 * part + q}"), 16)
            for c in range(4):
                load_two(c, [ein_v[:, :, 64 * h:64 * h + 64] for h in (c, c + 4)])
            for c in range(4, 22):
                load(c, ein_v[:, :, c * P:(c + 1) * P])
            load(22, ein_v[:, :, 22 * P:22 * P + 16])
            sp.dma_start(CT[:, C_LEVEL:, :], consts[:, C_LEVEL:, :]).then_inc(S("consts_landed"), 16)
            for m in range(2):
                load(N0_EVEN_OUT + m, eout_v[:, :, m * P:(m + 1) * P])
            sp.wait_ge(proj_done, N0_EVEN_IN + 23)
            for c, name in enumerate(("state_delta_fwd", "state_delta_bwd")):
                sp.dma_start(ST[c][:, :, :], a[name][0, 0].rearrange("h k v -> k h v")).then_inc(S("side_landed"), 16)
            sp.wait_ge(S("l2_done"), 8)
            for dst, name in ((DTB, "ev_dt_bias"), (EAL, "ev_a_log")):
                src = a[name][0].rearrange("(o d) h -> o (d h)", o=1).broadcast_to([P, 8])
                sp.dma_start(dst[:, :], src).then_inc(S("side_landed"), 16)
            for c, dst in enumerate((new_fwd, new_bwd)):
                sp.wait_ge(*both("state_done", c, NT))
                sp.dma_start(dst[0, 0].rearrange("h k v -> k h v"), ST[c][:, :, :]).then_inc(S("out_written"), 16)
            for c in range(2):
                sp.wait_ge(*both("o_done", c, NT))
            sp.dma_start(AKC[:, :], a["cache_attn_k"][0, 0].rearrange("t g d -> t (g d)")).then_inc(S("side_landed"), 16)
            sp.dma_start(AV[:, NT, :], a["cache_attn_v"][0, 0].rearrange("t g d -> t (g d)")).then_inc(S("side_landed"), 16)
            sp.dma_start(SNK[:, :], a["ev_sink"].broadcast_to([P, 8])).then_inc(S("side_landed"), 16)
            sp.wait_ge(S("k_out_rows"), 1)
            sp.dma_start(new_k[0, 0].rearrange("t g d -> t (g d)"), AKO[:, :]).then_inc(S("out_written"), 16)
            sp.wait_ge(S("v_rows"), 1)
            sp.dma_start(new_v[0, 0].rearrange("t g d -> t (g d)"), AV[:, 0, :]).then_inc(S("out_written"), 16)
            for u in range(MPARTS):
                if u == 2:
                    sp.wait_ge(S("on_lo"), 1)
                if u >= 3:
                    sp.wait_ge(S("mod_rows_done"), 4 + u - 2)
                l, m0 = (0, 2 * D + 2 * P * u) if u < 16 else (1, 2 * P * (u - 16))
                sp.dma_start(MW[u % 3][:, :, :], wm[l][:, :, m0:m0 + 2 * P]).then_inc(S(f"mod_landed{u % 3}"), 16)
            for m in range(2, 8):
                load(N0_EVEN_OUT + m, eout_v[:, :, m * P:(m + 1) * P])

            def ffn_loads(l):
                for half in range(2):
                    n0, j0 = N0_FFN[l] + half * (2 * FH + KD), half * FH
                    with sp.Fori(0, FH) as j:
                        for b in range(2):
                            load(n0 + b + 2 * j, up_v[l][:, :, bass.ds(j * P + (b * D_FF + j0 * P), P)],
                                 slot=(n0 + b) % 2, k=KD)
                    n1 = n0 + 2 * FH
                    with sp.Fori(0, KD // 2) as i:
                        for b in range(2):
                            load(n1 + b + 2 * i, down_v[l][:, j0:j0 + FH, bass.ds(i * 2 * P + b * P, P)],
                                 slot=(n1 + b) % 2, k=FH)

            ffn_loads(0)
            for c in range(2):
                load(N0_ODD_IN + c, oin_v[:, :, c * P:(c + 1) * P])
            for k in (KD - 1, POOL_X[-1]):
                sp.wait_ge(*x_ready("post01", k))
            sp.dma_start(CROW[:, :, :], a["cache_mla_ckv"][0, 0].rearrange("t (k c) -> t k c", c=P)).then_inc(S("side_landed"), 16)
            for r in range(2):
                sp.dma_start(KROW[:, 64 * r:64 * r + 64], a["cache_mla_kpe"][0, 0]).then_inc(S("side_landed"), 16)
            for c in range(2, 5):
                load(N0_ODD_IN + c, oin_v[:, :, c * P:(c + 1) * P])
            load_two(N0_ODD_IN + 5, [oin_v[:, :, 640:704]] * 2)
            for h in range(C_HEADS):
                nr, nq, nk, nv = odd_blocks(h)
                c0 = h * (C_NOPE + C_ROPE)
                if h % 2 == 0:
                    c1 = c0 + C_NOPE
                    load_two(nr, [qup_v[:, :, c:c + 64] for c in (c1, c1 + C_NOPE + C_ROPE)])
                load(nq, qup_v[:, :, c0:c0 + P])
                load(nk, kvup_v[:, :, 2 * P * h:2 * P * h + P])
                load(nv, kvup_v[:, :, 2 * P * h + P:2 * P * h + 2 * P])
                if h == 0:
                    sp.wait_ge(S("c_out_rows"), 2)
                    sp.dma_start(new_ckv[0, 0].rearrange("t (k c) -> t k c", c=P), CROW[:, :, :]).then_inc(S("out_written"), 16)
                    sp.dma_start(new_kpe[0, 0], KROW[:, 0:64]).then_inc(S("out_written"), 16)
            for m in range(8):
                load(N0_ODD_OUT + m, oout_v[:, :, m * P:(m + 1) * P])
            ffn_loads(1)
            for t in range(NT):
                sp.wait_ge(S("y_rows_a"), t + 1)
                sp.wait_ge(S("y_rows_v"), t + 1)
                dst = y_prompt[0] if t == 0 else y_sample[0, (t - 1) * P:t * P, :]
                sp.dma_start(dst, XR[t][:, :]).then_inc(S("out_written"), 16)
            sp.wait_ge(S("out_written"), 16 * (2 + 2 + 2 + NT))

        @block.gpsimd
        def _(pool):
            def lo(n, slot=None, k=None):
                slot = n % 2 if slot is None else slot
                k = BL[n][1] if k is None else k
                pool.wait_ge(w_hi, n + 1)
                pool.tensor_tensor(WL[slot][:, 0:k, :], RAW[slot][:, 0:k, :], WH[slot][:, 0:k, :].bitcast(F32),
                                   ALU.subtract).then_inc(w_lo, 1)

            def zero_gaps(sem, *matrices):
                for x in matrices:
                    pool.memset(x[:, :, 0:1], 0.0)
                    pool.memset(x[:, :, P0 + PROMPT:S0], 0.0)
                    last = pool.memset(x[:, :, S0 + SAMPLE:TW], 0.0)
                last.then_inc(sem, 1)

            H2 = (Hh[:, :, :].bitcast(F32), Hl[:, :, :].bitcast(F32))

            def post_norm(tag):
                pool.wait_ge(*of("rstd", tag, 1))
                for n, k in enumerate(POOL_X):
                    if n:
                        pool.wait_ge(*of("x_p", tag, n))
                    pool.wait_ge(*of("fs", tag, k + 1))
                    pool.tensor_tensor(TN[2][:, :], F[:, k, :], RST[:, :], ALU.mult).then_inc(S("norm_delta_p"), 1)
                    pool.wait_ge(*of("delta_p", tag, n + 1))
                    pool.tensor_tensor(X[:, k, :], X[:, k, :], TN[2][:, :], ALU.add).then_inc(S("norm_x_p"), 1)

            def pre_norm(tag):
                for k in range(1, KD, 2):
                    for q, c0, c1 in CONDS:
                        pool.wait_ge(*of("hh", tag, 2 * k + q + 1))
                        pool.tensor_tensor(Hl[:, k, c0:c1], TN[k % 3][:, c0:c1], Hh[:, k, c0:c1].bitcast(F32),
                                           ALU.subtract).then_inc(S("norm_hl_p"), 1)

            pool.memset(EPSC[:, :], EPS).then_inc(S("gpsimd_filled"), 1)
            pool.wait_ge(S("mod_rows_done"), 4)
            zero_gaps(S("gpsimd_filled"), *H2)
            lo(0)
            lo(1)
            pre_norm("pre00")
            for n in range(N0_EVEN_IN, N0_EVEN_IN + 23):
                lo(n + 2)
                if n == 2:
                    pool.wait_ge(S("x_turned"), 2 * NT)
                    pool.memset(QKV[:, :, 0:1], 0.0)
                    pool.memset(QKV[:, :, TW - 1:TW], 0.0).then_inc(S("gpsimd_filled"), 1)
            pool.wait_ge(S("kv_turned"), 2 * NT)
            zero_gaps(S("gpsimd_filled"), OD[:, :, :])
            pool.wait_ge(S("consts_landed"), 32)
            for r in range(NT):
                def level(lv):
                    for c in range(2):
                        if lv == 0:
                            pool.wait_ge(*both("a_ready", c, r + 1))
                            if r > 0:
                                pool.wait_ge(*both("os_done", c, r))
                        elif lv == 1:
                            if r > 0:
                                pool.wait_ge(*both("uw_done", c, r))
                        else:
                            pool.wait_ge(*both("z_done", c, LEVELS * r + lv - 1))
                            if lv == 2:
                                pool.wait_ge(*both("t_written", c, (LEVELS - 1) * r + 1))
                        mask = CT[:, C_LEVEL + LEVELS * c + lv:C_LEVEL + LEVELS * c + lv + 1, :].broadcast_to([P, 4, P])
                        pool.tensor_tensor(BS[c][lv % 2][:, :, :], DA[c][:, :, :], mask, ALU.mult).then_inc(S("level_ready"), 1)
                level(0)
                level(1)
                for c in range(2):
                    mask = CT[:, (C_TRIU, C_TRIL)[c]:(C_TRIU, C_TRIL)[c] + 1, :].broadcast_to([P, 4, P])
                    pool.tensor_tensor(DQ[c][:, :, :], DQ[c][:, :, :], mask, ALU.mult).then_inc(S("decay_masked"), 1)
                level(2)
                if r == 0:
                    pool.wait_ge(S("k_tok"), NT)
                    pool.wait_ge(S("gates_ready"), 1)
                for c in range(2):
                    t = tile_of(r, c)
                    pool.tensor_tensor(KL[c][:, :, :], KTOK[:, t, :, :], per_head(EK, 8 * t + 4 * c), ALU.mult
                                       ).then_inc(S("kl_ready"), 1)
                for lv in range(3, LEVELS):
                    level(lv)
                for c in range(2):
                    t = tile_of(r, c)
                    pool.wait_ge(*both("z_done", c, LEVELS * r + LEVELS - 1))
                    pool.tensor_tensor(KBE[c][:, :, :], KTOK[:, t, :, :], per_head(EB, 8 * t + 4 * c), ALU.mult
                                       ).then_inc(S("kb_ready"), 1)
            for c in range(2):
                pool.wait_ge(*both("o_done", c, NT))
            zero_gaps(S("gpsimd_filled"), *(x[:, 0:4, :] for x in H2))
            for u in range(MPARTS):
                pool.wait_ge(S("mod_hi"), u + 1)
                pool.tensor_tensor(ML[u % 3][:, 0:MK, :], MW[u % 3][:, 0:MK, :], MH[u % 2][:, 0:MK, :].bitcast(F32),
                                   ALU.subtract).then_inc(S("mod_lo_p"), 1)
            for n in range(N0_EVEN_OUT, N0_EVEN_OUT + 8):
                lo(n + 2)

            def ffn(l):
                pool.wait_ge(proj_done, N0_FFN[l])
                zero_gaps(S("gpsimd_filled"), *H2)
                for x in (Gh, Gl):
                    x = x[:, :, :].bitcast(F32)
                    pool.memset(x[:, :, 0:1], 0.0)
                    last = pool.memset(x[:, :, TW - 1:TW], 0.0)
                last.then_inc(S("gpsimd_filled"), 1)
                post_norm(f"post{l}0")
                pre_norm(f"pre{l}1")
                for half in range(2):
                    n0 = N0_FFN[l] + half * (2 * FH + KD)
                    c0 = FH * (2 * l + half)

                    def body(j, ks):
                        for b in range(2):
                            lo(n0 + 2 + b + 2 * j, slot=(n0 + b) % 2, k=ks)
                        pool.wait_ge(S("g_hi_written"), c0 + 1 + j)
                        pool.tensor_tensor(row(Gl, j)[:, 1:643], GP[:, 1:643], row(Gh, j)[:, 1:643].bitcast(F32),
                                           ALU.subtract).then_inc(S("g_lo_written"), 1)
                    with pool.Fori(0, FH - 1) as j:
                        body(j, KD)
                    body(FH - 1, FH)
                    n1 = n0 + 2 * FH
                    with pool.Fori(0, KD // 2 - 1) as i:
                        for b in range(2):
                            lo(n1 + 2 + b + 2 * i, slot=(n1 + b) % 2, k=FH)
                    for n in (n1 + KD, n1 + KD + 1):
                        if n < len(BL):
                            lo(n)
            ffn(0)
            post_norm("post01")
            pre_norm("pre10")
            for n in range(N0_ODD_IN + 2, N0_FFN[1] + 2):
                lo(n)
            ffn(1)
            post_norm("post11")

        @block.scalar
        def _(act):
            def hi(n, slot=None, k=None, landed=None):
                slot = n % 2 if slot is None else slot
                k = BL[n][1] if k is None else k
                act.wait_ge(w_landed[slot], landed_by(n) if landed is None else landed)
                if not isinstance(n, int) or n >= 2:
                    act.wait_ge(proj_done, n - 1)
                act.activation(WH[slot][:, 0:k, :], RAW[slot][:, 0:k, :], ACT.Copy).then_inc(w_hi, 1)

            def squares(tag, src, ready, count):
                for k in range(count):
                    ready(k)
                    if k >= 2:
                        act.wait_ge(*of("sum", tag, k - 1))
                    act.activation(SQ[k % 2][:, 0:TW], src(k), ACT.Square).then_inc(S("norm_sq"), 1)

            def rstd(tag, features):
                act.wait_ge(*of("stat", tag, 1))
                inverse_root(tag, features)

            def inverse_root(tag, features):
                act.activation(halves(RST[:, :]), pair(4), ACT.Ln, scale=1.0 / features, bias=EPSC[:, 0:1]
                               ).then_inc(S("norm_ln"), 1)
                act.wait_ge(*of("ln", tag, 1))
                act.activation(RST[:, :], RST[:, :], ACT.Exp, scale=-0.5).then_inc(S("norm_rstd"), 1)

            def pre_norm(tag, l, i, ready, between=None):
                for k in range(KD):
                    ready(k)
                    if k >= 2:
                        act.wait_ge(*of("part", tag, k - 1))
                    act.activation(SQ[k % 2][:, :], X[:, k, :], ACT.Square).then_inc(S("norm_sq"), 1)
                if between:
                    between()
                act.wait_ge(*of("part", tag, KD))
                inverse_root(tag, D)
                for k in range(KD):
                    for q, c0, c1 in CONDS:
                        act.wait_ge(*of("scaled", tag, 2 * k + q + 1))
                        col = 2 * (3 * i * 8 + k) + q
                        if k % 2:
                            act.activation(TN[k % 3][:, c0:c1], TN[k % 3][:, c0:c1], ACT.Identity,
                                           bias=MOD[l][:, col:col + 1]).then_inc(S("norm_shifted"), 1)
                        else:
                            act.activation(Hh[:, k, c0:c1], TN[k % 3][:, c0:c1], ACT.Identity,
                                           bias=MOD[l][:, col:col + 1]).then_inc(S("norm_hh"), 1)
                    if k % 2:
                        for q, c0, c1 in CONDS:
                            act.wait_ge(*of("shifted", tag, k + q))
                            act.activation(Hh[:, k, c0:c1], TN[k % 3][:, c0:c1], ACT.Copy).then_inc(S("norm_hh"), 1)

            def f_chunk(tag, l, i, m, b, evac):
                act.wait_ge(*evac)
                if not (isinstance(m, int) and m < 2):
                    sem, value = of("sum", tag, b - 1)
                    act.wait_ge(sem, value + m - b)
                act.activation(SQ[b][:, :], row(F, m), ACT.Square).then_inc(S("norm_sq"), 1)
                sem, value = of("sq", tag, b + 1)
                act.wait_ge(sem, value + m - b)
                for q, c0, c1 in CONDS:
                    gain = PG[l][i][:, 2 * m + q:2 * m + q + 1] if isinstance(m, int) else PG[l][i][:, bass.ds(2 * m + q, 1)]
                    last = act.activation(row(F, m)[:, c0:c1], row(F, m)[:, c0:c1], ACT.Copy, scale=gain)
                last.then_inc(S("norm_fs"), 1)

            act.preload_act_table_set("natural_log_exp_and_others")
            act.wait_ge(S("vec_cols"), 2)
            act.activation(SCE[:, :], VC[:, 0:16], ACT.Exp, scale=-1.0).then_inc(S("exp_c"), 1)
            act.wait_ge(S("silu_c"), 2)
            sc4 = SCS[:, 0:KD * 4].rearrange("p (k f) -> p k f", f=4)
            act.activation(sc4[:, :, 0:2], SCX[:, :].rearrange("p (q k) -> p k q", q=2), ACT.Copy).then_inc(S("silu_hi"), 1)
            for t in range(NT):
                act.wait_ge(S("x_turned"), 2 * t + 1)
                act.activation(X[:, 0:4, TILES[t]:TILES[t] + P], bank(6).rearrange("p (k c) -> p k c", c=P),
                               ACT.Copy).then_inc(S("x_evac_a"), 1)
            act.wait_ge(S("mod_ready"), 1)
            act.wait_ge(S("x_evac_a"), NT)
            act.wait_ge(S("x_evac_v"), NT)
            act.wait_ge(*filled("eps"))
            def first_blocks():
                hi(0)
                hi(1)
            pre_norm("pre00", 0, 0, lambda k: None, first_blocks)

            for n in range(23):
                act.wait_ge(proj_done, n + 1)
                hi(n + 2)
                b = 2 * (n % 2)
                c = n - 6
                if n < 6:
                    act.activation(halves(QA[:, n, :]), pair(b), ACT.Copy).then_inc(evac_a, 1)
                elif n < 18:
                    if c >= 2:
                        act.wait_ge(S("e_conv"), 2 * (c - 1))
                        act.wait_ge(S("e_silu"), c - 1)
                    act.activation(halves(U[c % 2][:, :]), pair(b), ACT.Copy).then_inc(S("e_u"), 1)
                    act.activation(halves(Y[c % 2][:, :]), pair(b), ACT.Copy,
                                   scale=VC[:, V_ECONV + 12 + c:V_ECONV + 13 + c]).then_inc(evac_a, 1)
                if 1 <= c <= 12:
                    act.wait_ge(S("e_conv"), 2 * c)
                    act.activation(QKV[:, c - 1, 1:643], Y[(c - 1) % 2][:, 1:643], ACT.Silu).then_inc(S("e_silu"), 1)
                if 18 <= n < 22:
                    act.activation(halves(SG[:, n - 18, :]), pair(b), ACT.Silu).then_inc(evac_a, 1)
                elif n == 22:
                    act.activation(halves(AB[0:16, :]), pair(b, p=16), ACT.Copy).then_inc(evac_a, 1)

            act.preload_act_table_set("natural_log_exp_and_others")
            RL = [ACC, RST]

            def l2_square(c):
                act.wait_ge(S("e_silu"), 12)
                act.wait_ge(*filled("qkv_edges"))
                if c >= 2:
                    act.wait_ge(*of("stat", "l2", c - 1))
                act.activation(SQ[c % 2][:, :], QKV[:, c, :], ACT.Square).then_inc(S("norm_sq"), 1)
            l2_square(0)
            l2_square(1)
            for c in range(8):
                act.wait_ge(*of("stat", "l2", c + 1))
                if c >= 2:
                    act.wait_ge(S("l2_done"), c - 1)
                act.activation(halves(RL[c % 2][:, :]), pair(4 + 2 * (c % 2)), ACT.Ln, bias=EPSC[:, 0:1]).then_inc(S("norm_ln"), 1)
                act.wait_ge(*of("ln", "l2", c + 1))
                act.activation(RL[c % 2][:, :], RL[c % 2][:, :], ACT.Exp, scale=-0.5).then_inc(S("norm_rstd"), 1)
                if c + 2 < 8:
                    l2_square(c + 2)

            act.wait_ge(S("gate_z"), 1)
            act.activation(ZA[:, :], ZG[:, :], ACT.Abs).then_inc(S("gate_act"), 1)
            act.wait_ge(S("gate_act"), 1)
            act.activation(ZA[:, :], ZA[:, :], ACT.Exp, scale=-1.0).then_inc(S("gate_act"), 1)
            act.wait_ge(S("gate_act"), 2)
            act.activation(ZA[:, :], ZA[:, :], ACT.Ln, bias=1.0).then_inc(S("gate_act"), 1)
            act.activation(gates(BETA), abv(1), ACT.Exp, scale=-1.0).then_inc(S("gate_act"), 1)
            act.activation(EAL[:, :], EAL[:, :], ACT.Exp).then_inc(S("gate_act"), 1)
            for t in range(NT):
                act.wait_ge(S("kv_turned"), 2 * t + 1)
                act.activation(KTOK[:, t, :, :], bank(4 + 2 * (t % 2)).rearrange("p (h c) -> p h c", c=P), ACT.Copy
                               ).then_inc(S("k_tok"), 1)
            act.wait_ge(S("decay_sums"), 1)
            act.activation(EB[:, :], GC[:, :], ACT.Exp).then_inc(S("gate_exp"), 1)
            act.activation(EK[:, :], GT[:, :], ACT.Exp).then_inc(S("gate_exp"), 1)

            act.wait_ge(S("v_tok"), NT)
            act.wait_ge(S("gates_ready"), 1)
            for r in range(NT):
                for c in range(2):
                    act.wait_ge(*both("d_args", c, r + 1))
                    act.activation(DQ[c][:, :, :], DQ[c][:, :, :], ACT.Abs).then_inc(S("d_abs"), 1)
                    if r > 0:
                        act.wait_ge(*both("os_done", c, r))
                    act.activation(QG[c][:, :, :], q4(bank(4 * c + 2)), ACT.Exp).then_inc(S("eg"), 1)
                    act.wait_ge(*both("d_abs", c, r + 1))
                    act.activation(DQ[c][:, :, :], DQ[c][:, :, :], ACT.Exp, scale=-1.0).then_inc(S("d_exp"), 1)
                for lv in range(1, LEVELS):
                    for c in range(2):
                        act.wait_ge(*both("z_done", c, LEVELS * r + lv + 1))
                        act.activation(ZS[c][:, :, :], q4(bank(4 * c)), ACT.Copy).then_inc(S("z_written"), 1)
                for c in range(2):
                    t = tile_of(r, c)
                    g0 = 8 * t + 4 * c
                    for h in range(4):
                        last = act.activation(VB[c][:, h, :], VTOK[:, t, h, :], ACT.Copy, scale=BETA[:, g0 + h:g0 + h + 1])
                    last.then_inc(S("vb_ready"), 1)
                if r < NT - 1:
                    for c in range(2):
                        act.wait_ge(*both("uw_done", c, r + 1))
                        act.activation(UU[c][:, :, :], q4(bank(4 * c + 2)), ACT.Copy).then_inc(S("u_written"), 1)

            def on_square(h):
                for c in range(2):
                    act.wait_ge(*both("o_done", c, NT))
                act.wait_ge(*filled("od_gaps"))
                if h >= 2:
                    act.wait_ge(*of("stat", "on", h - 1))
                act.activation(SQ[h % 2][:, :], OD[:, h, :], ACT.Square).then_inc(S("norm_sq"), 1)
            on_square(0)
            on_square(1)
            for h in range(4):
                act.wait_ge(*of("stat", "on", h + 1))
                if h >= 2:
                    act.wait_ge(S("on_gated"), 2 * (h - 1))
                act.activation(halves(RL[h % 2][:, :]), pair(4 + 2 * (h % 2)), ACT.Ln, scale=1.0 / P, bias=EPSC[:, 0:1]
                               ).then_inc(S("norm_ln"), 1)
                act.wait_ge(*of("ln", "on", h + 1))
                act.activation(RL[h % 2][:, :], RL[h % 2][:, :], ACT.Exp, scale=-0.5).then_inc(S("norm_rstd"), 1)
                if h + 2 < 4:
                    on_square(h + 2)
                act.wait_ge(S("on_gated"), 2 * h + 2)
                act.activation(Hh[:, 4 + h, :], OD[:, h, :], ACT.Copy).then_inc(S("on_hi"), 1)

            for t in range(NT):
                act.wait_ge(S("va_turned"), t + 1)
                act.activation(AV[:, t, :], bank(6 + t % 2, P), ACT.Copy).then_inc(S("v_rows"), 1)

            def att_out(i, sem):
                t = ATT[i]
                act.wait_ge(S("oa_turned"), i + 1)
                act.activation(Hh[:, 0:4, TILES[t]:TILES[t] + P], q4(bank(6)), ACT.Copy).then_inc(S(sem), 1)

            def mod_hi(u):
                act.wait_ge(S(f"mod_landed{u % 3}"), 16 * (u // 3 + 1))
                if u >= 2:
                    act.wait_ge(S("mod_rows_done"), 4 + u - 1)
                act.activation(MH[u % 2][:, :, :], MW[u % 3][:, :, :], ACT.Copy).then_inc(S("mod_hi"), 1)

            act.wait_ge(S("on_lo"), 1)
            mod_hi(0)
            for u, (t, h) in enumerate(ALLU):
                s = u % 2
                c0, c1 = att_local(t)
                if u + 1 < MPARTS:
                    mod_hi(u + 1)
                act.wait_ge(S("a_max"), u + 1)
                if u >= 2:
                    act.wait_ge(S("a_turned"), u - 1)
                act.activation(PR[s][:, c0:c1], SM[s][:, c0:c1], ACT.Exp, bias=ASM[:, 64 + u:65 + u],
                               scale=A_HD ** -0.5, accum_out=ASM[:, 128 + u:129 + u]).then_inc(S("a_exp"), 1)
                act.activation(ASM[:, 192 + u:193 + u], SNK[:, h:h + 1], ACT.Exp, bias=ASM[:, 64 + u:65 + u]
                               ).then_inc(S("a_sink"), 1)
                if u >= 1:
                    att_copy_a(act, u - 1)
                if h == 3 and t != ATT[0]:
                    att_out(ATT.index(t) - 1, "oa_hi")
            att_copy_a(act, len(ALLU) - 1)
            att_out(NT - 1, "oa_hi")

            def out_proj(n0, tag, l):
                act.preload_act_table_set("natural_log_exp_and_others")
                for m in range(8):
                    act.wait_ge(proj_done, n0 + m + 1)
                    hi(n0 + m + 2)
                    f_chunk(tag, l, 0, m, m % 2, evacuated(n0 + m))
                rstd(tag, D)
            out_proj(N0_EVEN_OUT, "post00", 0)

            def ffn(l):
                for half in range(2):
                    n0 = N0_FFN[l] + half * (2 * FH + KD)
                    c0 = FH * (2 * l + half)
                    v0 = V_FCONV + (3 * l + 1) * 2 * FCH + half * FH

                    def body(j, ks):
                        c = c0 + j
                        for b in range(2):
                            n = n0 + b + 2 * j
                            slot = (n0 + b) % 2
                            act.wait_ge(proj_done, n + 1)
                            hi(n + 2, slot=slot, k=ks, landed=landed_by(n0 + b + 2) + 16 * j)
                            if not (isinstance(j, int) and c == 0):
                                act.wait_ge(S(f"f_conv{b}"), 2 * c)
                                act.wait_ge(S("f_silu"), c)
                                act.wait_ge(S("f_gated"), c)
                            act.activation(halves(U[b][:, :]), pair(2 * slot), ACT.Copy).then_inc(S("f_u"), 1)
                            act.activation(halves(Y[b][:, :]), pair(2 * slot), ACT.Copy, scale=vcol(v0 + b * FCH, j)
                                           ).then_inc(evac_a, 1)
                        act.wait_ge(S("f_conv0"), 2 * c + 2)
                        act.activation(SILU_A[:, 1:643], Y[0][:, 1:643], ACT.Silu).then_inc(S("f_silu"), 1)
                        act.wait_ge(S("f_gated"), c + 1)
                        act.activation(row(Gh, j)[:, 1:643], GP[:, 1:643], ACT.Copy).then_inc(S("g_hi_written"), 1)
                    body(0, KD)
                    with act.Fori(1, FH - 1) as j:
                        body(j, KD)
                    body(FH - 1, FH)
                    n1 = n0 + 2 * FH
                    tag = f"post{l}1"
                    if half:
                        act.preload_act_table_set("natural_log_exp_and_others")
                    with act.Fori(0, KD // 2 - 1) as i:
                        for b in range(2):
                            act.wait_ge(proj_done, n1 + b + 1 + 2 * i)
                            hi(n1 + b + 2 + 2 * i, slot=(n1 + b) % 2, k=FH, landed=landed_by(n1 + b + 2) + 16 * i)
                            if half:
                                f_chunk(tag, l, 1, 2 * i + b, b, (evac_v, before(n1, True) + b + 1 + 2 * i))
                    for b in range(2):
                        n = n1 + KD - 2 + b
                        act.wait_ge(proj_done, n + 1)
                        if n + 2 < len(BL):
                            hi(n + 2)
                        if half:
                            f_chunk(tag, l, 1, KD - 2 + b, b, evacuated(n))
                    if half:
                        rstd(tag, D)

            pre_norm("pre01", 0, 1, lambda k: act.wait_ge(*x_ready("post00", k)))
            ffn(0)
            pre_norm("pre10", 1, 0, lambda k: act.wait_ge(*x_ready("post01", k)))

            act.wait_ge(S("c_ctx_turned"), 1)
            act.activation(CKV[:, :, 0:PAST], bank(6, 256).rearrange("p (k c) -> p k c", c=P), ACT.Copy).then_inc(S("c_ctx"), 1)
            act.activation(KPT[:, 0:PAST], PS[:, 6 * 512 + 256:6 * 512 + 384], ACT.Copy).then_inc(S("c_ctx"), 1)
            for m in range(6):
                n = N0_ODD_IN + m
                act.wait_ge(proj_done, n + 1)
                hi(n + 2)
                dst = CQ[:, m, :] if m < 3 else CKV[:, m - 3, PAST:KW] if m < 5 else KPT[:, PAST:KW]
                act.activation(halves(dst), pair(2 * (n % 2)), ACT.Copy).then_inc(evac_a, 1)
                if m == 2:
                    squares("cq", lambda k: CQ[:, k, :], lambda k: act.wait_ge(*evacuated(N0_ODD_IN + k)), 3)
                    rstd("cq", C_Q)
                    for k in range(3):
                        act.wait_ge(S("cq_scaled"), k + 1)
                        act.activation(CQh[:, k, :], CQ[:, k, :], ACT.Copy).then_inc(S("cq_hi"), 1)
            act.wait_ge(*evacuated(N0_ODD_IN + 4))
            act.wait_ge(*of("stat", "cq", 1))
            squares("ckv", lambda k: CKV[:, k, PAST:KW], lambda k: act.wait_ge(S("cq_scaled"), 3), 2)
            rstd("ckv", C_KV)
            for k in range(2):
                act.wait_ge(S("ckv_scaled"), k + 1)
                act.activation(CKh[:, k, :], CKV[:, k, :], ACT.Copy).then_inc(S("ckv_hi"), 1)

            def head_evac(h):
                nr, nq, nk, nv = odd_blocks(h)
                if h >= 2:
                    act.wait_ge(S("c_pv"), NT * (h - 1))
                todo = [(nq, halves(QN[h % 2][:, :]), pair(2 * (nq % 2))),
                        (nk, halves(KN[h % 2][:, :]), pair(2 * (nk % 2), KW // 2)),
                        (nv, VO[h % 2][:, :, :].rearrange("p t c -> p (t c)"), PS[:, 1024 * (nv % 2):1024 * (nv % 2) + 768])]
                if h % 2 == 0:
                    todo.insert(0, (nr, halves(QPE[h // 2 % 2][:, :]), pair(2 * (nr % 2))))
                for n, dst, src in todo:
                    act.wait_ge(proj_done, n + 1)
                    hi(n + 2)
                    act.activation(dst, src, ACT.Copy).then_inc(evac_a, 1)

            def odd_turned_copy(u):
                h, t = ODDU[u]
                s = u % 2
                act.wait_ge(S("c_turned"), u + 1)
                if u >= 2:
                    act.wait_ge(S("c_pv"), u - 1)
                if t != 0:
                    act.activation(CPT[s][:, 512:640], PS[:, CTP + 512:CTP + 640], ACT.Copy).then_inc(S("c_pt7"), 1)
                w = P if t == 0 else 512
                act.activation(CPT[s][:, 0:w], PS[:, CTP:CTP + w], ACT.Copy).then_inc(S("c_pt"), 1)
            head_evac(0)
            for u, (h, t) in enumerate(ODDU):
                s = u % 2
                w = P if t == 0 else 640
                if u >= 1:
                    odd_turned_copy(u - 1)
                act.wait_ge(S("c_max"), u + 1)
                if u >= 2:
                    act.wait_ge(S("c_turned"), u - 1)
                act.activation(CP[s][:, 0:w], PS[:, CSC:CSC + w], ACT.Exp, bias=CSM[:, 64 + u:65 + u],
                               scale=(C_NOPE + C_ROPE) ** -0.5, accum_out=CSM[:, 128 + u:129 + u]).then_inc(S("c_exp"), 1)
                if u >= 2:
                    odd_out_hi(act, u - 2)
                if t == ATT[1] and h + 1 < C_HEADS:
                    head_evac(h + 1)
            odd_turned_copy(len(ODDU) - 1)
            odd_out_hi(act, len(ODDU) - 2)
            odd_out_hi(act, len(ODDU) - 1)

            out_proj(N0_ODD_OUT, "post10", 1)
            pre_norm("pre11", 1, 1, lambda k: act.wait_ge(*x_ready("post10", k)))
            ffn(1)
            for t in range(NT):
                act.wait_ge(S("y_turned"), 2 * t + 1)
                act.activation(XR[t][:, 0:512], bank(6), ACT.Copy).then_inc(S("y_rows_a"), 1)

        @block.vector
        def _(dve):
            steps = {}

            def step(ins, signal="dve_step"):
                steps[signal] = steps.get(signal, 0) + 1
                ins.then_inc(S(signal), 1)
                dve.wait_ge(S(signal), steps[signal])

            def sums(tag, count):
                for k in range(count):
                    dve.wait_ge(*of("sq", tag, k + 1))
                    if k == 0:
                        dve.tensor_copy(ACC[:, :], SQ[0][:, :]).then_inc(S("norm_sum"), 1)
                    else:
                        dve.wait_ge(*of("sum", tag, k))
                        dve.tensor_tensor(ACC[:, :], ACC[:, :], SQ[k % 2][:, :], ALU.add).then_inc(S("norm_sum"), 1)

            def pre_norm(tag, l, i):
                dve.wait_ge(*of("rstd", tag, 1))

                def lo(k):
                    for q, c0, c1 in CONDS:
                        col = 2 * (3 * i * 8 + k) + q
                        dve.wait_ge(*of("hh", tag, 2 * k + q + 1))
                        dve.scalar_tensor_tensor(Hl[:, k, c0:c1], TN[k % 3][:, c0:c1], MOD[l][:, col:col + 1],
                                                 Hh[:, k, c0:c1].bitcast(F32), ALU.add, ALU.subtract
                                                 ).then_inc(S("norm_hl_v"), 1)
                for k in range(KD):
                    if k >= 3:
                        dve.wait_ge(*h_ready(tag, k - 3))
                    for q, c0, c1 in CONDS:
                        dve.scalar_tensor_tensor(TN[k % 3][:, c0:c1], X[:, k, c0:c1], PA[l][i][:, 2 * k + q:2 * k + q + 1],
                                                 RST[:, c0:c1], ALU.mult, ALU.mult).then_inc(S("norm_scaled"), 1)
                    if k % 2 == 1:
                        lo(k - 1)

            def post_norm(tag):
                dve.wait_ge(*of("rstd", tag, 1))
                mine = [k for k in range(KD) if k not in POOL_X]
                for n in range(len(mine) + 1):
                    if n < len(mine):
                        if n >= 2:
                            dve.wait_ge(*of("x_v", tag, n - 1))
                        dve.wait_ge(*of("fs", tag, mine[n] + 1))
                        dve.tensor_tensor(TN[n % 2][:, :], F[:, mine[n], :], RST[:, :], ALU.mult).then_inc(S("norm_delta_v"), 1)
                    if n >= 1:
                        k = mine[n - 1]
                        dve.wait_ge(*of("delta_v", tag, n))
                        dve.tensor_tensor(X[:, k, :], X[:, k, :], TN[(n - 1) % 2][:, :], ALU.add).then_inc(S("norm_x_v"), 1)

            def mod_columns(l, m0, m1, b, c0):
                step(dve.tensor_tensor(MOD[l][:, 2 * m0:2 * m1].rearrange("p (m q) -> p m q", q=2),
                                       PS[:, b * 512 + c0:b * 512 + c0 + 2 * (m1 - m0)].rearrange("p (m q) -> p m q", q=2),
                                       VC[:, V_BMOD + 48 * l + m0:V_BMOD + 48 * l + m1].unsqueeze(2).broadcast_to([P, m1 - m0, 2]),
                                       ALU.add))

            def gains(l, i, part, signal="dve_step"):
                dst, vec, op = ((PA, V_PRE, ALU.add), (PG, V_POST, ALU.mult))[part - 1]
                m0 = 2 * 8 * (3 * i + part)
                v0 = vec + (2 * l + i) * 8
                step(dve.scalar_tensor_tensor(
                    dst[l][i][:, :].rearrange("p (k q) -> p k q", q=2),
                    MOD[l][:, m0:m0 + 16].rearrange("p (k q) -> p k q", q=2), 1.0,
                    VC[:, v0:v0 + 8].unsqueeze(2).broadcast_to([P, 8, 2]), op, ALU.mult), signal)

            dve.memset(X[:, :, 0:1], 0.0)
            dve.memset(X[:, :, P0 + PROMPT:S0], 0.0)
            dve.memset(X[:, :, S0 + SAMPLE:TW], 0.0)
            dve.wait_ge(S("vec_turned"), 4)
            dve.tensor_copy(VC[:, 0:122], bank(4, 122)).then_inc(S("vec_cols"), 1)
            dve.tensor_copy(VC[:, 128:488], PS[:, 4 * 512 + 128:4 * 512 + 488]).then_inc(S("vec_cols"), 1)
            dve.wait_ge(S("exp_c"), 1)
            step(dve.tensor_scalar(SCR[:, :], SCE[:, :], 1.0, None, ALU.add))
            step(dve.reciprocal(SCR[:, :], SCR[:, :]))
            step(dve.tensor_tensor(SCX[:, :], SCR[:, :], VC[:, 0:16], ALU.mult), "silu_c")
            dve.memset(SCS[:, :].bitcast(F32), 0.0).then_inc(S("silu_c"), 1)
            for t in range(NT):
                dve.wait_ge(S("x_turned"), 2 * t + 2)
                dve.tensor_copy(X[:, 4:8, TILES[t]:TILES[t] + P], q4(bank(7))).then_inc(S("x_evac_v"), 1)
            dve.wait_ge(*filled("eps"))
            dve.wait_ge(S("silu_hi"), 1)
            sc4 = SCS[:, 0:KD * 4].rearrange("p (k f) -> p k f", f=4)
            dve.tensor_tensor(sc4[:, :, 2:4], SCX[:, :].rearrange("p (q k) -> p k q", q=2), sc4[:, :, 0:2].bitcast(F32),
                              ALU.subtract).then_inc(S("silu_lo"), 1)
            for q in range(4):
                dve.wait_ge(S("mod_rows_done"), q + 1)
                dve.tensor_copy(MROW0[0:2, 512 * q:512 * q + 512], bank(q, p=2)).then_inc(S("mod_rows"), 1)
            dve.wait_ge(S("mod_turned"), 4)
            mod_columns(0, 0, 16, 5, 0)
            gains(0, 0, 1, "mod_ready")
            pre_norm("pre00", 0, 0)

            for c in range(12):
                y, u = Y[c % 2], U[c % 2]
                dve.wait_ge(S("e_u"), c + 1)
                dve.wait_ge(*evacuated(6 + c))
                dve.scalar_tensor_tensor(y[:, 1:643], u[:, 0:642], VC[:, V_ECONV + c:V_ECONV + c + 1], y[:, 1:643],
                                         ALU.mult, ALU.add).then_inc(S("e_conv"), 1)
                dve.wait_ge(S("e_conv"), 2 * c + 1)
                dve.scalar_tensor_tensor(y[:, 1:643], u[:, 2:644], VC[:, V_ECONV + 24 + c:V_ECONV + 25 + c], y[:, 1:643],
                                         ALU.mult, ALU.add).then_inc(S("e_conv"), 1)

            for c in range(8):
                dve.wait_ge(*of("rstd", "l2", c + 1))
                dve.scalar_tensor_tensor(QKV[:, c, 1:643], QKV[:, c, 1:643], P ** -0.5 if c < 4 else 1.0,
                                         [ACC, RST][c % 2][:, 1:643], ALU.mult, ALU.mult).then_inc(S("l2_done"), 1)

            dve.wait_ge(S("ab_turned"), NT)
            step(dve.tensor_copy(ABC[:, :], bank(6, NT * 16)))
            dve.wait_ge(S("side_landed"), 64)
            for t in range(NT):
                last = dve.tensor_tensor(gates(ZG)[:, t], abv(0)[:, t], DTB[:, :].rearrange("p (d h) -> p d h", d=2), ALU.add)
            last.then_inc(S("gate_z"), 1)
            dve.wait_ge(S("gate_z"), 1)
            dve.wait_ge(S("gate_act"), 5)
            step(dve.tensor_scalar(BETA[:, :], BETA[:, :], 1.0, None, ALU.add))
            step(dve.reciprocal(BETA[:, :], BETA[:, :]))
            step(dve.tensor_scalar(EAL[:, :], EAL[:, :], -1.0, None, ALU.mult))
            step(dve.scalar_tensor_tensor(G[:, :], ZG[:, :], 0.0, ZA[:, :], ALU.max, ALU.add))
            for t in range(NT):
                last = dve.tensor_tensor(G[:, 8 * t:8 * t + 8], G[:, 8 * t:8 * t + 8], EAL[:, :], ALU.mult)
            last.then_inc(S("log_decay"), 1)
            for t in range(NT):
                dve.wait_ge(S("kv_turned"), 2 * t + 2)
                dve.tensor_copy(VTOK[:, t, :, :], q4(bank(5 + 2 * (t % 2)))).then_inc(S("v_tok"), 1)
            dve.wait_ge(S("decay_cols"), 1)
            for d in range(2):
                dve.tensor_copy(gates(GC)[:, :, d, :], PS[:, 20 * d:20 * d + 20].rearrange("p (t h) -> p t h", h=4))
            step(dve.tensor_copy(GT[:, :], PS[:, 40:80]))
            step(dve.tensor_tensor(GT[:, :], GT[:, :], GC[:, :], ALU.subtract), "decay_sums")
            dve.wait_ge(S("gate_exp"), 2)
            step(dve.tensor_tensor(EB[:, :], EB[:, :], BETA[:, :], ALU.mult), "gates_ready")

            ident4 = CT[:, C_ID:C_ID + 1, :].broadcast_to([P, 4, P])
            for r in range(NT):
                n0, t0 = LEVELS * r, (LEVELS - 1) * r
                for c in range(2):
                    g0 = 8 * tile_of(r, c) + 4 * c
                    dve.wait_ge(*both("gc_row", c, r + 1))
                    if r > 0:
                        dve.wait_ge(*both("os_done", c, r))
                    dve.tensor_tensor(DQ[c][:, :, :], q4(bank(4 * c + 2)), per_head(GC, g0), ALU.subtract).then_inc(S("d_args"), 1)
                for c in range(2):
                    g0 = 8 * tile_of(r, c) + 4 * c
                    dve.wait_ge(*both("d_exp", c, r + 1))
                    dve.wait_ge(*both("kk_done", c, r + 1))
                    if r > 0:
                        dve.wait_ge(*both("level_ready", c, n0))
                    for h in range(4):
                        last = dve.scalar_tensor_tensor(DA[c][:, h, :], PS[:, 4 * c * 512 + P * h:4 * c * 512 + P * h + P],
                                                        BETA[:, g0 + h:g0 + h + 1], DQ[c][:, h, :], ALU.mult, ALU.mult)
                    last.then_inc(S("a_ready"), 1)
                for c in range(2):
                    dve.wait_ge(*both("level_ready", c, n0 + 1))
                    dve.tensor_tensor(TS[c][:, :, :], BS[c][0][:, :, :], ident4, ALU.add).then_inc(S("t_written"), 1)
                    dve.wait_ge(*both("z_done", c, n0 + 1))
                    dve.tensor_tensor(RS[c][:, :, :], q4(bank(4 * c)), ident4, ALU.add).then_inc(S("r_written"), 1)
                for lv in range(1, LEVELS):
                    s = 1 << lv
                    for c in range(2):
                        dve.wait_ge(*both("tr_done", c, t0 + lv))
                        dve.wait_ge(*both("r_written", c, n0 + lv))
                        dve.tensor_tensor(cols(RS[c], s, 1 - c), cols(RS[c], s, 1 - c), compact(4 * c + 3, s), ALU.add
                                          ).then_inc(S("r_written"), 1)
                        if lv < LEVELS - 1:
                            dve.wait_ge(*both("t_written", c, t0 + lv))
                            dve.tensor_tensor(cols(TS[c], s, c), cols(TS[c], s, c), compact(4 * c + 2, s), ALU.add
                                              ).then_inc(S("t_written"), 1)
                    if lv == 1:
                        for c in range(2):
                            T0 = TILES[tile_of(r, c)]
                            dve.wait_ge(*both("decay_masked", c, r + 1))
                            dve.wait_ge(*both("kq_done", c, r + 1))
                            dve.tensor_tensor(DQ[c][:, :, :], q4(bank(4 * c + 1)), DQ[c][:, :, :], ALU.mult
                                              ).then_inc(S("qk_ready"), 1)
                            dve.wait_ge(*both("eg", c, r + 1))
                            col = P - 1 if c == 0 else 0
                            if r > 0:
                                dve.wait_ge(*both("state_done", c, r))
                            step(dve.tensor_copy(ELC[c][:, :].unsqueeze(2), QG[c][:, :, col:col + 1]))
                            dve.tensor_tensor(QG[c][:, :, :], QG[c][:, :, :], QKV[:, 0:4, T0:T0 + P], ALU.mult
                                              ).then_inc(S("q_ready"), 1)
                for c in range(2):
                    dve.wait_ge(*both("uw_done", c, r + 1))
                    if r < NT - 1:
                        dve.tensor_copy(WT[c][:, :, :], q4(bank(4 * c + 3))).then_inc(S("w_written"), 1)
                for c in range(2):
                    if r < NT - 1:
                        dve.wait_ge(*both("ws_done", c, r + 1))
                        dve.wait_ge(*both("u_written", c, r + 1))
                        dve.tensor_tensor(VB[c][:, :, :], UU[c][:, :, :], q4(bank(4 * c)), ALU.subtract).then_inc(S("v_new"), 1)
                    else:
                        dve.tensor_copy(VB[c][:, :, :], q4(bank(4 * c + 2))).then_inc(S("v_new"), 1)
                for c in range(2):
                    t = tile_of(r, c)
                    T0 = TILES[t]
                    dve.wait_ge(*both("os_done", c, r + 1))
                    if r < NT - 1:
                        for h in range(4):
                            q0 = (4 * c + 2) * 512 + P * h
                            last = dve.scalar_tensor_tensor(ST[c][:, h, :], ST[c][:, h, :], ELC[c][:, h:h + 1],
                                                            PS[:, q0:q0 + P], ALU.mult, ALU.add)
                        last.then_inc(S("state_done"), 1)
                    else:
                        dve.tensor_copy(ST[c][:, :, :], q4(bank(4 * c + 2))).then_inc(S("state_done"), 1)
                    dst = OD[:, :, T0:T0 + P]
                    first = r < 2 or (r == NT - 1 and c == 0)
                    if first:
                        dve.tensor_copy(dst, q4(bank(4 * c + 1))).then_inc(S("o_done"), 1)
                    else:
                        for cc in range(2):
                            if r == NT - 1 and cc == 1:
                                continue
                            dve.wait_ge(*both("o_done", cc, 2 if r < NT - 1 else NT))
                        dve.tensor_tensor(dst, dst, q4(bank(4 * c + 1)), ALU.add).then_inc(S("o_done"), 1)

            dve.wait_ge(S("out_written"), 32)
            for h in range(4):
                RL = [ACC, RST][h % 2]
                dve.wait_ge(*of("rstd", "on", h + 1))
                dve.scalar_tensor_tensor(OD[:, h, :], OD[:, h, :], VC[:, V_ON:V_ON + 1], RL[:, :],
                                         ALU.mult, ALU.mult).then_inc(S("on_gated"), 1)
                dve.wait_ge(S("on_gated"), 2 * h + 1)
                dve.tensor_tensor(OD[:, h, :], OD[:, h, :], SG[:, h, :], ALU.mult).then_inc(S("on_gated"), 1)
                if h > 0:
                    dve.wait_ge(S("on_hi"), h)
                    dve.tensor_tensor(Hl[:, 3 + h, :], OD[:, h - 1, :], Hh[:, 3 + h, :].bitcast(F32), ALU.subtract)
            dve.wait_ge(S("on_hi"), 4)
            dve.tensor_tensor(Hl[:, 7, :], OD[:, 3, :], Hh[:, 7, :].bitcast(F32), ALU.subtract).then_inc(S("on_lo"), 1)

            def rope(dst, b, turned, n):
                dve.wait_ge(turned, n)
                step(dve.tensor_tensor(ROT[:, :], bank(b), CT[:, C_SIN:C_SIN + 4, :].rearrange("p a b -> p (a b)"), ALU.mult))
                step(dve.tensor_tensor(dst, dst, CT[:, C_COS:C_COS + 4, :].rearrange("p a b -> p (a b)"), ALU.mult))
                return dve.tensor_tensor(dst, dst, ROT[:, :], ALU.add)

            dve.wait_ge(S("ka_turned"), 1)
            dve.tensor_copy(AKO[:, :], PS[:, 5 * 512 + P:5 * 512 + 2 * P]).then_inc(S("k_out_rows"), 1)
            for c in range(5):
                step(rope(QA[:, c, S0:S0 + SAMPLE], c % 4, S("a_swapped"), c + 1), "a_roped")
            dve.wait_ge(S("side_landed"), 16 * 7)
            for g2 in range(2):
                z = slice(64 * (1 - g2), 64 * (1 - g2) + 64)
                o = slice(64 * g2, 64 * g2 + 64)
                dve.memset(AKT[g2][z, :], 0.0)
                dve.tensor_copy(AKT[g2][o, 0:PAST], PS[o, 5 * 512:5 * 512 + P])
                for q, c0, c1 in CONDS:
                    dve.tensor_copy(AKT[g2][o, PAST + c0:PAST + c1], QA[o, 4, c0:c1])
            step(dve.tensor_scalar(SNK8[:, :], SNK[:, :], A_HD ** 0.5, None, ALU.mult), "k_attn")

            def att_scale(u):
                t, h = ALLU[u]
                i = ATT.index(t)
                dve.wait_ge(S("a_sink"), u + 1)
                step(dve.tensor_tensor(ASM[:, u:u + 1], ASM[:, 128 + u:129 + u], ASM[:, 192 + u:193 + u], ALU.add))
                step(dve.reciprocal(ASM[:, u:u + 1], ASM[:, u:u + 1]))
                dve.wait_ge(S("a_pv"), u + 1)
                if h == 0 and i >= 2:
                    dve.wait_ge(S("oa_turned"), i - 1)
                q0 = (4 + u % 2) * 512 + 64 * h
                dve.tensor_scalar(OA[i % 2][:, 64 * h:64 * h + 64], PS[:, q0:q0 + 64], ASM[:, u:u + 1], None, ALU.mult
                                  ).then_inc(S("oa_scaled"), 1)

            def att_lo(i):
                t = ATT[i]
                dve.wait_ge(S("oa_hi"), i + 1)
                dve.tensor_tensor(Hl[:, 0:4, TILES[t]:TILES[t] + P], q4(bank(6)),
                                  Hh[:, 0:4, TILES[t]:TILES[t] + P].bitcast(F32), ALU.subtract).then_inc(S("oa_lo"), 1)

            def mod_rows(u):
                dve.wait_ge(S("mod_rows_done"), 4 + u + 1)
                if u >= 2:
                    dve.wait_ge(S("mod_turned"), 4 + u - 1)
                dve.tensor_copy(MROW[u % 2][0:4, :], bank(7, 256, 4)).then_inc(S("mod_rows"), 1)

            def mod_lo(u):
                dve.wait_ge(S("mod_hi"), u + 1)
                dve.tensor_tensor(ML[u % 3][:, MK:, :], MW[u % 3][:, MK:, :], MH[u % 2][:, MK:, :].bitcast(F32),
                                  ALU.subtract).then_inc(S("mod_lo_v"), 1)
            mod_lo(0)

            for u, (t, h) in enumerate(ALLU):
                s = u % 2
                c0, c1 = att_local(t)
                dve.wait_ge(S("a_scores"), u + 1)
                if u >= 2:
                    dve.wait_ge(S("a_exp"), u - 1)
                dve.tensor_tensor_reduce(SM[s][:, c0:c1], PS[:, 512 * s + c0:512 * s + c1],
                                         CT[:, C_AMASK:C_AMASK + 4, :].rearrange("p a b -> p (a b)")[:, c0:c1],
                                         1.0, SNK8[:, h:h + 1], ALU.add, ALU.max, ASM[:, u:u + 1]).then_inc(S("a_rowmax"), 1)
                dve.wait_ge(S("a_rowmax"), u + 1)
                dve.tensor_scalar(ASM[:, 64 + u:65 + u], ASM[:, u:u + 1], -A_HD ** -0.5, None, ALU.mult).then_inc(S("a_max"), 1)
                if u >= 2:
                    att_scale(u - 2)
                if u >= 1:
                    mod_rows(u - 1)
                if h == 4 and t != ATT[0]:
                    att_lo(ATT.index(t) - 1)
                if u + 1 < MPARTS:
                    mod_lo(u + 1)
            mod_rows(39)
            att_scale(len(ALLU) - 2)
            att_scale(len(ALLU) - 1)
            att_lo(NT - 1)
            dve.wait_ge(S("mod_turned"), 4 + 40)
            mod_columns(0, 16, 48, 7, 352)
            mod_columns(1, 0, 48, 7, 352 + 64)
            for l in range(2):
                for i in range(2):
                    if (l, i) != (0, 0):
                        gains(l, i, 1)
                    gains(l, i, 2)

            def add_square(tag, m, b):
                sem, value = of("sq", tag, b + 1)
                dve.wait_ge(sem, value + m - b)
                sem, value = of("sum", tag, b)
                dve.wait_ge(sem, value + m - b)
                dve.tensor_tensor(ACC[:, :], ACC[:, :], SQ[b][:, :], ALU.add).then_inc(S("norm_sum"), 1)

            def out_evac(n0, tag):
                step(dve.memset(ACC[:, :], 0.0))
                for m in range(8):
                    dve.wait_ge(proj_done, n0 + m + 1)
                    dve.tensor_copy(halves(F[:, m, :]), pair(2 * ((n0 + m) % 2))).then_inc(evac_v, 1)
                    add_square(tag, m, m % 2)

            def ffn(l):
                for half in range(2):
                    n0 = N0_FFN[l] + half * (2 * FH + KD)
                    c0 = FH * (2 * l + half)
                    v0 = V_FCONV + 3 * l * 2 * FCH + half * FH

                    def body(j):
                        c = c0 + j
                        for b in range(2):
                            dve.wait_ge(evac_a, before(n0, False) + b + 1 + 2 * j)
                            y, u = Y[b], U[b]
                            dve.scalar_tensor_tensor(y[:, 1:643], u[:, 0:642], vcol(v0 + b * FCH, j), y[:, 1:643],
                                                     ALU.mult, ALU.add).then_inc(S(f"f_conv{b}"), 1)
                            dve.wait_ge(S(f"f_conv{b}"), 2 * c + 1)
                            last = dve.scalar_tensor_tensor(y[:, 1:643], u[:, 2:644], vcol(v0 + b * FCH + 4 * FCH, j), y[:, 1:643],
                                                            ALU.mult, ALU.add)
                            last.then_inc(S(f"f_conv{b}"), 1)
                        dve.wait_ge(S("f_silu"), c + 1)
                        dve.wait_ge(S("f_conv1"), 2 * c + 2)
                        if not (isinstance(j, int) and c == 0):
                            dve.wait_ge(S("g_lo_written"), c)
                        dve.tensor_tensor(GP[:, 1:643], SILU_A[:, 1:643], Y[1][:, 1:643], ALU.mult).then_inc(S("f_gated"), 1)
                    body(0)
                    with dve.Fori(1, FH) as j:
                        body(j)
                    n1 = n0 + 2 * FH
                    if half == 1:
                        dve.wait_ge(evac_v, before(n1, True))
                        dve.wait_ge(S("g_lo_written"), FH * (2 * l + half + 1))
                        step(dve.memset(ACC[:, :], 0.0))

                    def down(i):
                        for b in range(2):
                            slot = (n1 + b) % 2
                            m = 2 * i + b
                            dve.wait_ge(proj_done, n1 + b + 1 + 2 * i)
                            if half == 0:
                                dve.tensor_copy(halves(row(F, m)), pair(2 * slot)).then_inc(evac_v, 1)
                            else:
                                dve.tensor_tensor(halves(row(F, m)), pair(2 * slot), halves(row(F, m)), ALU.add
                                                  ).then_inc(evac_v, 1)
                                add_square(f"post{l}1", m, b)
                    with dve.Fori(0, KD // 2) as i:
                        down(i)

            out_evac(N0_EVEN_OUT, "post00")
            post_norm("post00")
            pre_norm("pre01", 0, 1)
            ffn(0)
            post_norm("post01")
            pre_norm("pre10", 1, 0)

            sums("cq", 3)
            dve.wait_ge(*of("rstd", "cq", 1))
            for k in range(3):
                dve.scalar_tensor_tensor(CQ[:, k, :], CQ[:, k, :], VC[:, V_QN + k:V_QN + k + 1], RST[:, :], ALU.mult, ALU.mult
                                         ).then_inc(S("cq_scaled"), 1)
            for k in range(3):
                dve.wait_ge(S("cq_hi"), k + 1)
                dve.tensor_tensor(CQl[:, k, :], CQ[:, k, :], CQh[:, k, :].bitcast(F32), ALU.subtract).then_inc(S("cq_lo"), 1)
            sums("ckv", 2)
            dve.wait_ge(*of("rstd", "ckv", 1))
            for k in range(2):
                dve.scalar_tensor_tensor(CKV[:, k, PAST:KW], CKV[:, k, PAST:KW], VC[:, V_KVN + k:V_KVN + k + 1], RST[:, :],
                                         ALU.mult, ALU.mult).then_inc(S("ckv_scaled"), 1)
            for k in range(2):
                dve.wait_ge(S("ckv_hi"), k + 1)
                dve.tensor_tensor(CKl[:, k, :], CKV[:, k, :], CKh[:, k, :].bitcast(F32), ALU.subtract).then_inc(S("ckv_lo"), 1)
            dve.wait_ge(S("c_out_turned"), 1)
            dve.tensor_copy(CROW[:, :, :], bank(6, 256).rearrange("p (k c) -> p k c", c=P)).then_inc(S("c_out_rows"), 1)
            dve.tensor_copy(KROW[:, :], PS[:, 6 * 512 + 256:6 * 512 + 384]).then_inc(S("c_out_rows"), 1)
            step(rope(KPT[:, PAST + S0:PAST + S0 + SAMPLE], 7, S("k_swapped"), 1))
            for r in range(2):
                dve.memset(KPE[r][64 * (1 - r):64 * (1 - r) + 64, :], 0.0)
                last = dve.tensor_copy(KPE[r][64 * r:64 * r + 64, :], KPT[64 * r:64 * r + 64, :])
            last.then_inc(S("kpe_ready"), 1)

            def rope_q(i):
                step(rope(QPE[i % 2][:, S0:S0 + SAMPLE], 6, S("q_swapped"), i + 1), "q_roped")
            rope_q(0)

            def odd_lo(u):
                h, t = ODDU[u]
                dve.wait_ge(S("c_out_hi"), u + 1)
                dve.tensor_tensor(Hl[:, h, TILES[t]:TILES[t] + P], COUT, Hh[:, h, TILES[t]:TILES[t] + P].bitcast(F32),
                                  ALU.subtract).then_inc(S("c_out_lo"), 1)

            for u, (h, t) in enumerate(ODDU):
                s = u % 2
                w = P if t == 0 else 640
                dve.wait_ge(S("c_scores"), u + 1)
                dve.tensor_reduce(CSM[:, u:u + 1], PS[:, CSC:CSC + w], AX_X, ALU.max).then_inc(S("c_rowmax"), 1)
                dve.wait_ge(S("c_rowmax"), u + 1)
                dve.tensor_scalar(CSM[:, 64 + u:65 + u], CSM[:, u:u + 1], -(C_NOPE + C_ROPE) ** -0.5, None, ALU.mult
                                  ).then_inc(S("c_max"), 1)
                dve.wait_ge(S("c_exp"), u + 1)
                step(dve.reciprocal(CSM[:, 192 + u:193 + u], CSM[:, 128 + u:129 + u]))
                dve.tensor_scalar(CP[s][:, 0:w], CP[s][:, 0:w], CSM[:, 192 + u:193 + u], None, ALU.mult).then_inc(S("c_normed"), 1)
                if u >= 2:
                    odd_lo(u - 2)
                if h % 2 == 1 and t == 0 and h + 1 < C_HEADS:
                    rope_q((h + 1) // 2)
            odd_lo(len(ODDU) - 2)
            odd_lo(len(ODDU) - 1)

            out_evac(N0_ODD_OUT, "post10")
            post_norm("post10")
            pre_norm("pre11", 1, 1)
            ffn(1)
            post_norm("post11")
            for t in range(NT):
                dve.wait_ge(S("y_turned"), 2 * t + 2)
                dve.tensor_copy(XR[t][:, 512:1024], bank(7)).then_inc(S("y_rows_v"), 1)

        @block.tensor
        def _(pe):
            def split_mm(outs, w_of, x_of, ks):
                last = None
                for k in range(ks):
                    for p, (wi, xi) in enumerate(((0, 0), (0, 1), (1, 0))):
                        for i, out in enumerate(outs):
                            last = pe.matmul(out, w_of(k, wi), x_of(k, xi, i), start=(k == 0 and p == 0),
                                             stop=(k == ks - 1 and p == 2))
                return last

            def proj(n, x, slot=None, k=None, width=HW, free=None):
                slot = n % 2 if slot is None else slot
                k = BL[n][1] if k is None else k
                pe.wait_ge(w_lo, n + 1)
                if free is None:
                    free = [evacuated(n - 2)] if n >= 2 else []
                for sem, value in free:
                    pe.wait_ge(sem, value)
                w = (WH[slot], WL[slot])
                b = 2 * slot
                split_mm([bank(b, width), bank(b + 1, width)], lambda kk, i: w[i][:, kk, :],
                         lambda kk, i, hf: x[i][:, kk, hf * width:(hf + 1) * width], k).then_inc(proj_done, 1)

            def stat(sem, src, b=4):
                for hf in range(2):
                    last = pe.matmul(bank(b + hf, HW), ONES, src[:, hf * HW:(hf + 1) * HW], start=True, stop=True)
                last.then_inc(sem, 1)

            def norm_stat(tag):
                pe.wait_ge(*of("sum", tag, CHUNKS[tag]))
                stat(S("norm_stat"), ACC)

            def pre_stat(tag):
                for k in range(KD):
                    pe.wait_ge(*of("sq", tag, k + 1))
                    for hf in range(2):
                        last = pe.matmul(bank(4 + hf, HW), ONES, SQ[k % 2][:, hf * HW:(hf + 1) * HW], start=(k == 0),
                                         stop=(k == KD - 1))
                    last.then_inc(S("norm_part"), 1)

            def pair_chunk(n, b, k, x, ks):
                slot = (n + b) % 2
                for p, (wi, xi) in enumerate(((0, 0), (0, 1), (1, 0))):
                    for hf in range(2):
                        last = pe.matmul(bank(2 * slot + hf, HW), (WH, WL)[wi][slot][:, k, :],
                                         x[xi][:, k, hf * HW:(hf + 1) * HW], start=(k == 0 and p == 0),
                                         stop=(k == ks - 1 and p == 2))
                if k == ks - 1:
                    last.then_inc(proj_done, 1)

            def first_pair(n, tag):
                pe.wait_ge(w_lo, n + 2)
                if n >= 2:
                    pe.wait_ge(*evacuated(n - 2))
                    pe.wait_ge(*evacuated(n - 1))
                for k in range(KD):
                    pe.wait_ge(*h_ready(tag, k))
                    for b in range(2):
                        pair_chunk(n, b, k, (Hh, Hl), KD)

            def down_pair(n, g0):
                for b in range(2):
                    pe.wait_ge(w_lo, n + b + 1)
                    pe.wait_ge(*evacuated(n + b - 2))
                    for k in range(FH - 1):
                        if b == 0:
                            pe.wait_ge(S("g_lo_written"), g0 + k + 1)
                        pair_chunk(n, b, k, (Gh, Gl), FH)
                pe.wait_ge(S("g_lo_written"), g0 + FH)
                for b in range(2):
                    pair_chunk(n, b, FH - 1, (Gh, Gl), FH)

            def turn(out, src, rows=P):
                return pe.transpose(out, src, IDENT[0:rows, 0:rows])

            def mod_part(w, c0, n, b):
                for k in range(KD):
                    last = pe.matmul(bank(b, n, 2), SCX[:, k:16:8], w[:, k, c0:c0 + n], start=(k == 0), stop=(k == KD - 1))
                last.then_inc(S("mod_rows_done"), 1)

            def mod_turn(q, rows, n, b, c0):
                pe.wait_ge(S("mod_rows"), q + 1)
                for j in range(n):
                    last = turn(PS[:, b * 512 + c0 + 2 * j:b * 512 + c0 + 2 * j + 2], rows[0:2, P * j:P * j + P], 2)
                last.then_inc(S("mod_turned"), 1)

            pe.wait_ge(S("consts_landed"), 16)
            pe.wait_ge(S("vec_landed"), 16 * 12)
            for b, n in enumerate((122, 128, 128, 104)):
                turn(PS[:, 4 * 512 + 128 * b:4 * 512 + 128 * b + n], VR[b][0:n, :], n).then_inc(S("vec_turned"), 1)
            pe.wait_ge(S("x_landed"), 16 * NT)
            for t in range(NT):
                for part, sem in ((0, "x_evac_a"), (1, "x_evac_v")):
                    if t:
                        pe.wait_ge(S(sem), t)
                    for k in range(4):
                        last = turn(PS[:, (6 + part) * 512 + P * k:(6 + part) * 512 + P * k + P],
                                    XR[t][:, (4 * part + k) * P:(4 * part + k + 1) * P])
                    last.then_inc(S("x_turned"), 1)
            pe.wait_ge(S("silu_c"), 1)
            for q in range(4):
                pe.wait_ge(S(f"mod_first_landed{q}"), 16)
                mod_part(MWS[q // 2], 512 * (q % 2), 512, q)
            for q in range(4):
                mod_turn(q, MROW0[:, 512 * q:512 * q + 512], 4, 5, 8 * q)
            H = (Hh, Hl)
            pe.wait_ge(S("mod_ready"), 1)
            pre_stat("pre00")
            pe.wait_ge(*filled("h_gaps_e"))
            first_pair(0, "pre00")
            for n in range(2, 23):
                proj(n, H)

            for c in range(8):
                if c >= 2:
                    pe.wait_ge(*of("ln", "l2", c - 1))
                pe.wait_ge(*of("sq", "l2", c + 1))
                stat(S("norm_stat"), SQ[c % 2], 4 + 2 * (c % 2))
            pe.wait_ge(*evacuated(22))
            pe.wait_ge(*of("ln", "l2", 8))
            for t in range(NT):
                turn(PS[:, 6 * 512 + 16 * t:6 * 512 + 16 * t + 16], AB[0:16, TILES[t]:TILES[t] + P], 16).then_inc(S("ab_turned"), 1)
            pe.wait_ge(S("l2_done"), 8)
            pe.wait_ge(S("gate_z"), 1)
            for t in range(NT):
                for kind, sem in ((1, "k_tok"), (2, "v_tok")):
                    if t >= 2:
                        pe.wait_ge(S(sem), t - 1)
                    b = 3 + kind + 2 * (t % 2)
                    for h in range(4):
                        last = turn(PS[:, b * 512 + P * h:b * 512 + P * h + P], QKV[:, 4 * kind + h, TILES[t]:TILES[t] + P])
                    last.then_inc(S("kv_turned"), 1)
            pe.wait_ge(S("log_decay"), 1)
            pe.matmul(PS[:, 0:20], const(C_TRIU), gates(G)[:, :, 0, :], start=True, stop=True)
            pe.matmul(PS[:, 20:40], const(C_TRIL), gates(G)[:, :, 1, :], start=True, stop=True)
            pe.matmul(PS[:, 40:80], ONES, G[:, :], start=True, stop=True).then_inc(S("decay_cols"), 1)
            pe.wait_ge(S("gates_ready"), 1)
            pe.wait_ge(S("k_tok"), NT)
            pe.wait_ge(S("v_tok"), NT)
            pe.wait_ge(S("side_landed"), 64)

            def hb(b, h):
                return PS[:, b * 512 + P * h:b * 512 + P * h + P]

            for r in range(NT):
                n0 = LEVELS * r
                for c in range(2):
                    t = tile_of(r, c)
                    T0 = TILES[t]
                    if r > 0:
                        pe.wait_ge(*both("state_done", c, r))
                        pe.wait_ge(*both("o_done", c, r))
                    for h in range(4):
                        g0 = 8 * t + 4 * c + h
                        last = pe.matmul(hb(4 * c + 2, h), G[:, g0:g0 + 1].broadcast_to([P, P]),
                                         const((C_TRIU, C_TRIL)[c]), start=True, stop=True)
                    last.then_inc(S("gc_row"), 1)
                for c in range(2):
                    T0 = TILES[tile_of(r, c)]
                    for h in range(4):
                        kt = QKV[:, 4 + h, T0:T0 + P]
                        last = pe.matmul(hb(4 * c, h), kt, kt, start=True, stop=True)
                    last.then_inc(S("kk_done"), 1)
                for c in range(2):
                    T0 = TILES[tile_of(r, c)]
                    for h in range(4):
                        last = pe.matmul(hb(4 * c + 1, h), QKV[:, 4 + h, T0:T0 + P], QKV[:, h, T0:T0 + P], start=True, stop=True)
                    last.then_inc(S("kq_done"), 1)
                t0 = (LEVELS - 1) * r
                for lv in range(LEVELS):
                    n, s = n0 + lv, 1 << lv
                    for c in range(2):
                        pe.wait_ge(*both("level_ready", c, n + 1))
                        if lv > 0:
                            pe.wait_ge(*both("r_written", c, n))
                        if lv > 1:
                            pe.wait_ge(*both("z_written", c, t0 + lv - 1))
                        for h in range(4):
                            last = pe.matmul(hb(4 * c, h), BS[c][lv % 2][:, h, :], IDENT if lv == 0 else RS[c][:, h, :],
                                             start=True, stop=True)
                        last.then_inc(S("z_done"), 1)
                    if lv == 0:
                        continue
                    for c in range(2):
                        pe.wait_ge(*both("z_written", c, t0 + lv))
                        pe.wait_ge(*both("t_written", c, t0 + lv))
                        if lv == 1:
                            pe.wait_ge(*both("eg", c, r + 1))
                        for h in range(4):
                            last = pe.matmul(compact(4 * c + 3, s, h), TS[c][:, h, :], cols1(ZS[c], h, s, 1 - c), start=True, stop=True)
                        if lv < LEVELS - 1:
                            for h in range(4):
                                last = pe.matmul(compact(4 * c + 2, s, h), ZS[c][:, h, :], cols1(TS[c], h, s, c), start=True, stop=True)
                        last.then_inc(S("tr_done"), 1)
                for c in range(2):
                    pe.wait_ge(*both("r_written", c, n0 + LEVELS))
                    pe.wait_ge(*both("kb_ready", c, r + 1))
                    if r < NT - 1:
                        for h in range(4):
                            pe.matmul(hb(4 * c + 3, h), KBE[c][:, h, :], RS[c][:, h, :], start=True, stop=True)
                    pe.wait_ge(*both("vb_ready", c, r + 1))
                    for h in range(4):
                        last = pe.matmul(hb(4 * c + 2, h), RS[c][:, h, :], VB[c][:, h, :], start=True, stop=True)
                    last.then_inc(S("uw_done"), 1)
                if r < NT - 1:
                    for c in range(2):
                        pe.wait_ge(*both("w_written", c, r + 1))
                        for h in range(4):
                            last = pe.matmul(hb(4 * c, h), WT[c][:, h, :], ST[c][:, h, :], start=True, stop=True)
                        last.then_inc(S("ws_done"), 1)
                for c in range(2):
                    pe.wait_ge(*both("v_new", c, r + 1))
                    pe.wait_ge(*both("q_ready", c, r + 1))
                    pe.wait_ge(*both("kl_ready", c, r + 1))
                    pe.wait_ge(*both("qk_ready", c, r + 1))
                    for h in range(4):
                        if r < NT - 1:
                            pe.matmul(hb(4 * c + 1, h), ST[c][:, h, :], QG[c][:, h, :], start=True, stop=False)
                        pe.matmul(hb(4 * c + 1, h), VB[c][:, h, :], DQ[c][:, h, :], start=(r == NT - 1), stop=True)
                    for h in range(4):
                        last = pe.matmul(hb(4 * c + 2, h), KL[c][:, h, :], VB[c][:, h, :], start=True, stop=True)
                    last.then_inc(S("os_done"), 1)

            for c in range(2):
                pe.wait_ge(*both("o_done", c, NT))
            for h in range(4):
                if h >= 2:
                    pe.wait_ge(*of("ln", "on", h - 1))
                pe.wait_ge(*of("sq", "on", h + 1))
                stat(S("norm_stat"), SQ[h % 2], 4 + 2 * (h % 2))

            pe.wait_ge(*of("ln", "on", 4))
            for t in range(NT):
                if t >= 2:
                    pe.wait_ge(S("v_rows"), t - 1)
                turn(hb(6 + t % 2, 0), QA[:, 5, TILES[t]:TILES[t] + P]).then_inc(S("va_turned"), 1)
            pe.wait_ge(S("side_landed"), 16 * 7)
            turn(hb(5, 0), AKC[:, :])
            turn(hb(5, 1), QA[:, 4, P0:P0 + P]).then_inc(S("ka_turned"), 1)
            for c in range(5):
                if c == 4:
                    pe.wait_ge(S("a_roped"), 1)
                pe.matmul(bank(c % 4), const(C_SWAP), QA[:, c, S0:S0 + SAMPLE], start=True, stop=True).then_inc(S("a_swapped"), 1)
            pe.wait_ge(S("k_attn"), 1)
            pe.wait_ge(S("a_roped"), 5)
            pe.wait_ge(S("v_rows"), NT)

            def att_scores(u):
                t, h = ALLU[u]
                if u >= 2:
                    pe.wait_ge(S("a_rowmax"), u - 1)
                kt, q = AKT[h // 4], QA[:, h % 4, TILES[t]:TILES[t] + P]
                for c, kt_tile in att_tiles(t):
                    k0 = 0 if kt_tile == NT else PAST + TILES[kt_tile]
                    last = pe.matmul(PS[:, 512 * (u % 2) + c:512 * (u % 2) + c + P], q, kt[:, k0:k0 + P], start=True, stop=True)
                last.then_inc(S("a_scores"), 1)

            def att_turn(u):
                t, h = ALLU[u]
                pe.wait_ge(S("a_exp"), u + 1)
                if u >= 2:
                    pe.wait_ge(S("a_pt"), u - 1)
                for c, _ in att_tiles(t):
                    last = turn(PS[:, 1024 + 512 * (u % 2) + c:1024 + 512 * (u % 2) + c + P], PR[u % 2][:, c:c + P])
                last.then_inc(S("a_turned"), 1)

            def att_values(u):
                t, h = ALLU[u]
                i = ATT.index(t)
                pe.wait_ge(S("a_pt"), u + 1)
                if u >= 2:
                    pe.wait_ge(S("oa_scaled"), u - 1)
                out = PS[:, (4 + u % 2) * 512 + 64 * h:(4 + u % 2) * 512 + 64 * h + 64]
                tiles = att_tiles(t)
                for x, (c, kt_tile) in enumerate(tiles):
                    last = pe.matmul(out, PT[u % 2][:, c:c + P], AV[:, kt_tile, 64 * (h // 4):64 * (h // 4) + 64],
                                     start=(x == 0), stop=(x == len(tiles) - 1))
                last.then_inc(S("a_pv"), 1)

            def att_out(i):
                pe.wait_ge(S("oa_scaled"), 8 * (i + 1))
                if i:
                    pe.wait_ge(S("oa_lo"), i)
                for k in range(4):
                    last = turn(hb(6, k), OA[i % 2][:, P * k:P * k + P])
                last.then_inc(S("oa_turned"), 1)

            for u in range(len(ALLU) + 2):
                if u < len(ALLU):
                    att_scores(u)
                if 1 <= u <= len(ALLU):
                    att_turn(u - 1)
                if u >= 2:
                    att_values(u - 2)
                if u % 8 == 3 and u > 8:
                    att_out(u // 8 - 1)
                if 1 <= u <= MPARTS:
                    pe.wait_ge(S("mod_rows"), 4 + u)
                    for j in range(2):
                        c = 7 * 512 + 352 + 4 * (u - 1) + 2 * j
                        last = pe.matmul(PS[:, c:c + 2], MROW[(u - 1) % 2][0:4, P * j:P * j + P], CT[0:4, C_PAIR, 0:2],
                                         start=True, stop=True)
                    last.then_inc(S("mod_turned"), 1)
                if u < MPARTS:
                    pe.wait_ge(S("mod_lo_p"), u + 1)
                    pe.wait_ge(S("mod_lo_v"), u + 1)
                    pe.wait_ge(S("silu_lo"), 1)
                    for k in range(KD):
                        for x, w in enumerate((MH[u % 2], ML[u % 3])):
                            last = pe.matmul(bank(7, 2 * P), SCS[:, 4 * k:4 * k + P], w[:, k, :], start=(k == 0 and x == 0),
                                             stop=(k == KD - 1 and x == 1))
                    last.then_inc(S("mod_rows_done"), 1)
            att_out(NT - 1)
            pe.wait_ge(S("oa_hi"), NT)
            pe.wait_ge(S("oa_lo"), NT)
            pe.wait_ge(S("on_lo"), 1)
            pe.wait_ge(*filled("o_attn_gaps"))
            for m in range(8):
                proj(N0_EVEN_OUT + m, H)

            def ffn(l, tag):
                pe.wait_ge(*filled(f"h_gaps{l}"))
                pe.wait_ge(*filled(f"g_edges{l}"))
                for half in range(2):
                    n0 = N0_FFN[l] + half * (2 * FH + KD)
                    if half == 0:
                        first_pair(n0, tag)
                    with pe.Fori(1 - half, FH) as j:
                        for b in range(2):
                            proj(n0 + b + 2 * j, H, slot=(n0 + b) % 2, k=KD,
                                 free=[(evac_v, before(n0, True) - 1 + b), (evac_a, before(n0, False) - 1 + b + 2 * j)])
                    n1 = n0 + 2 * FH
                    down_pair(n1, FH * (2 * l + half))
                    with pe.Fori(1, KD // 2) as i:
                        for b in range(2):
                            proj(n1 + b + 2 * i, (Gh, Gl), slot=(n1 + b) % 2, k=FH,
                                 free=[(evac_v, before(n1, True) - 1 + b + 2 * i)])

            norm_stat("post00")
            pre_stat("pre01")
            ffn(0, "pre01")
            norm_stat("post01")
            pre_stat("pre10")

            pe.wait_ge(S("side_landed"), 16 * 10)
            for k in range(2):
                turn(hb(6, k), CROW[:, k, :])
            turn(hb(6, 2), KROW[:, :]).then_inc(S("c_ctx_turned"), 1)
            first_pair(N0_ODD_IN, "pre10")
            for m in range(2, 6):
                proj(N0_ODD_IN + m, H)
                if m == 4:
                    norm_stat("cq")
            norm_stat("ckv")
            pe.wait_ge(*evacuated(N0_ODD_IN + 5))
            pe.matmul(bank(7), const(C_SWAP), KPT[:, PAST + S0:PAST + S0 + SAMPLE], start=True, stop=True).then_inc(S("k_swapped"), 1)
            pe.wait_ge(S("c_ctx"), 2)
            pe.wait_ge(S("ckv_scaled"), 2)
            for k in range(2):
                turn(hb(6, k), CKV[:, k, PAST + P0:PAST + P0 + P])
            turn(hb(6, 2), KPT[:, PAST + P0:PAST + P0 + P]).then_inc(S("c_out_turned"), 1)

            def head_proj(h):
                nr, nq, nk, nv = odd_blocks(h)
                if h == 0:
                    pe.wait_ge(S("cq_lo"), 3)
                if h % 2 == 0:
                    proj(nr, (CQh, CQl))
                proj(nq, (CQh, CQl))
                if h == 0:
                    pe.wait_ge(S("ckv_lo"), 2)
                proj(nk, (CKh, CKl), width=KW // 2)
                pe.wait_ge(w_lo, nv + 1)
                pe.wait_ge(*evacuated(nv - 2))
                slot = nv % 2
                c = (CKh, CKl)
                for kt_tile in range(NT + 1):
                    k0 = 0 if kt_tile == NT else PAST + TILES[kt_tile]
                    last = split_mm([PS[:, 1024 * slot + P * kt_tile:1024 * slot + P * kt_tile + P]],
                                    lambda kk, i: c[i][:, kk, k0:k0 + P], lambda kk, i, _: (WH, WL)[i][slot][:, kk, :], 2)
                last.then_inc(proj_done, 1)

            def rope_swap(i):
                nr = odd_blocks(2 * i)[0]
                pe.wait_ge(*evacuated(nr))
                if i == 0:
                    pe.wait_ge(S("c_out_rows"), 2)
                else:
                    pe.wait_ge(S("c_pt"), 10 * i - 1)
                pe.matmul(bank(6), const(C_SWAP), QPE[i % 2][:, S0:S0 + SAMPLE], start=True, stop=True).then_inc(S("q_swapped"), 1)

            def c_scores(u):
                h, t = ODDU[u]
                if u:
                    pe.wait_ge(S("c_exp"), u)
                if u % 5 == 0:
                    pe.wait_ge(*evacuated(odd_blocks(h)[3]))
                    if h % 2 == 0:
                        pe.wait_ge(S("q_roped"), h // 2 + 1)
                q, qr = QN[h % 2][:, TILES[t]:TILES[t] + P], QPE[h // 2 % 2][:, TILES[t]:TILES[t] + P]
                areas = [(CSC, PAST + P0, P)] if t == 0 else [(CSC, PAST + S0, SAMPLE), (CSC + 512, 0, PAST)]
                for c0, k0, w in areas:
                    pe.matmul(PS[:, c0:c0 + w], q, KN[h % 2][:, k0:k0 + w], start=True, stop=False)
                    last = pe.matmul(PS[:, c0:c0 + w], qr, KPE[h % 2][:, k0:k0 + w], start=False, stop=True)
                last.then_inc(S("c_scores"), 1)

            def c_turn(u):
                h, t = ODDU[u]
                pe.wait_ge(S("c_normed"), u + 1)
                if u >= 1:
                    pe.wait_ge(S("c_pt"), u)
                if u >= 2:
                    pe.wait_ge(S("c_out_lo"), u - 1)
                if u % 10 == 9 and u < len(ODDU) - 1:
                    pe.wait_ge(S("q_roped"), (u + 1) // 10 + 1)
                for x in range(1 if t == 0 else 5):
                    last = turn(PS[:, CTP + P * x:CTP + P * x + P], CP[u % 2][:, P * x:P * x + P])
                last.then_inc(S("c_turned"), 1)

            def c_values(u, ahead):
                h, t = ODDU[u]
                pe.wait_ge(S("c_pt"), u + 1)
                n7 = sum(1 for hh, tt in ODDU[0:ahead] if tt != 0)
                pe.wait_ge(S("c_pt7"), n7)
                if u >= 1:
                    pe.wait_ge(S("c_out_lo"), u)
                tiles = [(0, 0)] if t == 0 else [(x, 1 + x) for x in range(4)] + [(4, NT)]
                for x, (c, kt_tile) in enumerate(tiles):
                    last = pe.matmul(COUT, VO[h % 2][:, kt_tile, :], CPT[u % 2][:, P * c:P * c + P], start=(x == 0),
                                     stop=(x == len(tiles) - 1))
                last.then_inc(S("c_pv"), 1)

            head_proj(0)
            rope_swap(0)
            pe.wait_ge(S("kpe_ready"), 1)
            for u in range(len(ODDU) + 2):
                if u < len(ODDU):
                    c_scores(u)
                if 1 <= u <= len(ODDU):
                    c_turn(u - 1)
                if u >= 2:
                    c_values(u - 2, min(u, len(ODDU)))
                if u % 5 == 1 and u // 5 + 1 < C_HEADS:
                    head_proj(u // 5 + 1)
                if u % 10 == 9 and u < 39:
                    rope_swap((u + 1) // 10)
            pe.wait_ge(S("c_out_lo"), len(ODDU))
            for m in range(8):
                proj(N0_ODD_OUT + m, H)
            norm_stat("post10")
            pre_stat("pre11")
            ffn(1, "pre11")
            norm_stat("post11")
            for k in (KD - 1, POOL_X[-1]):
                pe.wait_ge(*x_ready("post11", k))
            for t in range(NT):
                for part, sem in ((0, "y_rows_a"), (1, "y_rows_v")):
                    if t:
                        pe.wait_ge(S(sem), t)
                    for k in range(4):
                        last = turn(hb(6 + part, k), X[:, 4 * part + k, TILES[t]:TILES[t] + P])
                    last.then_inc(S("y_turned"), 1)


_INS = ["x_prompt", "x_sample", "cache_attn_k", "cache_attn_v", "state_delta_fwd", "state_delta_bwd",
        "cache_mla_ckv", "cache_mla_kpe", "c", "c_ctx", "w_mod", "b_mod", "norm_pre", "norm_post",
        "ffn_w_up", "ffn_conv", "ffn_w_down", "ev_w_in", "ev_conv", "ev_a_log", "ev_dt_bias", "ev_sink",
        "ev_out_norm", "ev_w_out", "od_w_in", "od_q_norm", "od_kv_norm", "od_w_q_up", "od_w_kv_up", "od_w_out"]
_OUTS = [(1, PROMPT, D), (1, SAMPLE, D), (1, 1, PROMPT, 2, A_HD), (1, 1, PROMPT, 2, A_HD),
         (1, 1, B_HEADS, P, P), (1, 1, B_HEADS, P, P), (1, 1, PROMPT, C_KV), (1, 1, PROMPT, C_ROPE)]


def kernel(**inputs):
    import concourse.bacc as bacc
    from concourse.bass_utils import run_bass_kernel_spmd

    nc = bacc.Bacc("TRN2", target_bir_lowering=False, num_devices=1)
    arrays = {name: np.ascontiguousarray(inputs[name]) for name in _INS}
    arrays["consts"] = shape_constants()
    ins = {name: nc.dram_tensor(f"in_{name}", v.shape, mybir.dt.from_np(v.dtype), kind="ExternalInput").ap()
           for name, v in arrays.items()}
    outs = [nc.dram_tensor(f"out_{i}", shape, F32, kind="ExternalOutput").ap() for i, shape in enumerate(_OUTS)]
    build(nc, ins, outs)
    r = run_bass_kernel_spmd(nc, [{f"in_{name}": v for name, v in arrays.items()}], core_ids=[0])
    return tuple(r.results[0][f"out_{i}"] for i in range(len(_OUTS)))
```
